# Optimizing a Trainium2 kernel written in Bass

```python
import jax, jax.numpy as jnp
from jax import lax
import numpy as np

D_MODEL = 1024
BATCH = 1
SEQ = 1024
DEPTH = 1

CHUNK = 64
Q_BLOCK = 2 * CHUNK
N_META = 16
HEAD_DIM = 64
MIX_WIDTH = D_MODEL
ATTN_WIDTH = MIX_WIDTH // 2
CONV_WIDTH = MIX_WIDTH - ATTN_WIDTH
N_ATTN_HEADS = ATTN_WIDTH // HEAD_DIM
N_MIX_GROUPS = MIX_WIDTH // HEAD_DIM
CONV_K = 3
SPLIT_SIZES = (ATTN_WIDTH, ATTN_WIDTH, ATTN_WIDTH, N_ATTN_HEADS, CONV_WIDTH, CONV_WIDTH, CONV_WIDTH)
IN_WIDTH = sum(SPLIT_SIZES)
N_GROUPS = 4
EXPERTS_PER_GROUP = 8
N_EXPERTS = N_GROUPS * EXPERTS_PER_GROUP
TOP_K = 2
D_EXPERT = D_MODEL // 2
MOE_BLOCK = 128
EPS = 1e-6

kernel_name = "hymba_fox_shortconv_hmoe_block"

def rmsnorm(x, g):
    xf = x.astype(jnp.float32)
    y = xf * lax.rsqrt(jnp.mean(xf * xf, axis=-1, keepdims=True) + EPS)
    return (y * g.astype(jnp.float32)).astype(x.dtype)

def forgetting_attention(q, k, v, f_logit):
    bsz, L, H, hd = q.shape
    Lp = -(-L // Q_BLOCK) * Q_BLOCK
    pad = Lp - L
    q = jnp.pad(q, ((0, 0), (0, pad), (0, 0), (0, 0)))
    k = jnp.pad(k, ((0, 0), (0, pad), (0, 0), (0, 0)))
    v = jnp.pad(v, ((0, 0), (0, pad), (0, 0), (0, 0)))
    log_f = jnp.pad(jax.nn.log_sigmoid(f_logit.astype(jnp.float32)), ((0, 0), (0, pad), (0, 0)))
    cum = jnp.cumsum(log_f, axis=1).transpose(0, 2, 1)
    pos = jnp.arange(Lp)
    nb = Lp // Q_BLOCK
    qb = q.reshape(bsz, nb, Q_BLOCK, H, hd).transpose(1, 0, 3, 2, 4)
    cqb = cum.reshape(bsz, H, nb, Q_BLOCK).transpose(2, 0, 1, 3)
    pb = pos.reshape(nb, Q_BLOCK)
    scale = HEAD_DIM ** -0.5

    def block(args):
        qi, ci, pi = args
        s = jnp.einsum('bhqd,bkhd->bhqk', qi, k, preferred_element_type=jnp.float32) * scale
        s = s + ci[..., None] - cum[:, :, None, :]
        s = jnp.where(pos[None, :] <= pi[:, None], s, -jnp.inf)
        p = jax.nn.softmax(s, axis=-1)
        return jnp.einsum('bhqk,bkhd->bqhd', p.astype(v.dtype), v)

    o = lax.map(block, (qb, cqb, pb))
    return o.transpose(1, 0, 2, 3, 4).reshape(bsz, Lp, H, hd)[:, :L]

def short_gated_conv(xc, b_gate, c_gate, w):
    u = c_gate * xc
    L = u.shape[1]
    up = jnp.pad(u, ((0, 0), (CONV_K - 1, 0), (0, 0)))
    z = sum(up[:, i:i + L] * w[i].astype(u.dtype) for i in range(CONV_K))
    return b_gate * z

def hierarchical_moe(h, w_rg, b_rg, w_re, b_re, w_gate, w_up, w_down):
    n_tok, d = h.shape
    g_prob = jax.nn.softmax((h @ w_rg).astype(jnp.float32) + b_rg.astype(jnp.float32), axis=-1)
    g_idx = jnp.argmax(g_prob, axis=-1)
    g_w = jnp.max(g_prob, axis=-1)
    e_logits = ((h @ w_re).astype(jnp.float32) + b_re.astype(jnp.float32)).reshape(n_tok, N_GROUPS, EXPERTS_PER_GROUP)
    e_logits = jnp.take_along_axis(e_logits, g_idx[:, None, None], axis=1)[:, 0]
    top_p, top_i = lax.top_k(jax.nn.softmax(e_logits, axis=-1), TOP_K)
    top_p = top_p / jnp.sum(top_p, axis=-1, keepdims=True)
    weights = g_w[:, None] * top_p
    expert = g_idx[:, None] * EXPERTS_PER_GROUP + top_i

    n_asg = n_tok * TOP_K
    flat_e = expert.reshape(-1)
    flat_tok = jnp.repeat(jnp.arange(n_tok), TOP_K)
    flat_w = weights.reshape(-1)
    order = jnp.argsort(flat_e)
    se, stok, sw = flat_e[order], flat_tok[order], flat_w[order]
    counts = jnp.bincount(flat_e, length=N_EXPERTS)
    starts = jnp.cumsum(counts) - counts
    padded = (counts + MOE_BLOCK - 1) // MOE_BLOCK * MOE_BLOCK
    pad_end = jnp.cumsum(padded)
    pad_start = pad_end - padded
    dest = pad_start[se] + (jnp.arange(n_asg) - starts[se])
    n_blocks = -(-n_asg // MOE_BLOCK) + N_EXPERTS
    rows = n_blocks * MOE_BLOCK
    xbuf = jnp.zeros((rows, d), h.dtype).at[dest].set(h[stok])
    blk_e = jnp.minimum(jnp.searchsorted(pad_end, jnp.arange(n_blocks) * MOE_BLOCK, side='right'), N_EXPERTS - 1)

    def expert_block(args):
        xb, e = args
        return (jax.nn.silu(xb @ w_gate[e]) * (xb @ w_up[e])) @ w_down[e]

    ybuf = lax.map(expert_block, (xbuf.reshape(n_blocks, MOE_BLOCK, d), blk_e)).reshape(rows, d)
    y = ybuf[dest] * sw[:, None].astype(h.dtype)
    return jax.ops.segment_sum(y, stok, num_segments=n_tok)

def setup_inputs(seed: int = 0) -> dict:
    key = jax.random.key(seed)
    ks = jax.random.split(key, 20)
    f32 = jnp.float32
    nrm = lambda k, shape, scale: jax.random.normal(k, shape, f32) * scale
    return {
        'x': nrm(ks[0], (BATCH, SEQ, D_MODEL), 1.0),
        'meta_tokens': nrm(ks[1], (N_META, D_MODEL), 1.0),
        'attn_norm': 1.0 + nrm(ks[2], (DEPTH, D_MODEL), 0.02),
        'w_in': nrm(ks[3], (DEPTH, D_MODEL, IN_WIDTH), D_MODEL ** -0.5),
        'b_forget': jax.random.uniform(ks[4], (DEPTH, N_ATTN_HEADS), f32, 1.0, 4.0),
        'conv_w': nrm(ks[5], (DEPTH, CONV_K, CONV_WIDTH), CONV_K ** -0.5),
        'mix_norm': 1.0 + nrm(ks[6], (DEPTH, MIX_WIDTH), 0.02),
        'w_out': nrm(ks[7], (DEPTH, MIX_WIDTH, D_MODEL), MIX_WIDTH ** -0.5),
        'ffn_norm': 1.0 + nrm(ks[8], (DEPTH, D_MODEL), 0.02),
        'w_router_group': nrm(ks[9], (DEPTH, D_MODEL, N_GROUPS), D_MODEL ** -0.5),
        'b_router_group': nrm(ks[10], (DEPTH, N_GROUPS), 0.01),
        'w_router_expert': nrm(ks[11], (DEPTH, D_MODEL, N_EXPERTS), D_MODEL ** -0.5),
        'b_router_expert': nrm(ks[12], (DEPTH, N_EXPERTS), 0.01),
        'w_gate': nrm(ks[13], (DEPTH, N_EXPERTS, D_MODEL, D_EXPERT), D_MODEL ** -0.5),
        'w_up': nrm(ks[14], (DEPTH, N_EXPERTS, D_MODEL, D_EXPERT), D_MODEL ** -0.5),
        'w_down': nrm(ks[15], (DEPTH, N_EXPERTS, D_EXPERT, D_MODEL), D_EXPERT ** -0.5),
        'final_norm': 1.0 + nrm(ks[16], (D_MODEL,), 0.02),
    }

def reference(x, meta_tokens, attn_norm, w_in, b_forget, conv_w, mix_norm, w_out, ffn_norm,
              w_router_group, b_router_group, w_router_expert, b_router_expert,
              w_gate, w_up, w_down, final_norm):
    bsz = x.shape[0]
    meta = jnp.broadcast_to(meta_tokens[None].astype(x.dtype), (bsz, N_META, D_MODEL))
    h = jnp.concatenate([meta, x], axis=1)
    L = h.shape[1]
    split_at = [int(s) for s in np.cumsum(SPLIT_SIZES)[:-1]]
    for l in range(DEPTH):
        z = rmsnorm(h, attn_norm[l])
        q, k, v, f_logit, xc, b_gate, c_gate = jnp.split(z @ w_in[l], split_at, axis=-1)
        f_logit = f_logit.astype(jnp.float32) + b_forget[l].astype(jnp.float32)
        heads = (bsz, L, N_ATTN_HEADS, HEAD_DIM)
        attn = forgetting_attention(q.reshape(heads), k.reshape(heads), v.reshape(heads), f_logit)
        attn = attn.reshape(bsz, L, ATTN_WIDTH)
        conv = short_gated_conv(xc, b_gate, c_gate, conv_w[l])
        mixed = jnp.concatenate([attn, conv.astype(attn.dtype)], axis=-1)
        mixed = rmsnorm(mixed.reshape(bsz, L, N_MIX_GROUPS, HEAD_DIM),
                        mix_norm[l].reshape(N_MIX_GROUPS, HEAD_DIM)).reshape(bsz, L, MIX_WIDTH)
        h = h + mixed @ w_out[l]
        z = rmsnorm(h, ffn_norm[l]).reshape(bsz * L, D_MODEL)
        ffn = hierarchical_moe(z, w_router_group[l], b_router_group[l], w_router_expert[l],
                               b_router_expert[l], w_gate[l], w_up[l], w_down[l])
        h = h + ffn.reshape(bsz, L, D_MODEL)
    out = rmsnorm(h, final_norm)
    return out[:, N_META:]


_drawn_inputs = setup_inputs


def setup_inputs(seed=0):
    import zlib

    import numpy as np

    out = dict(_drawn_inputs(seed))
    spreads = {}
    factors = {'ffn_norm': 3.03, 'b_router_group': 6.559, 'b_router_expert': 6.368, 'final_norm': 2.858}
    for name, (base, spread) in spreads.items():
        noise = np.random.default_rng([zlib.crc32(name.encode()), seed]).standard_normal(out[name].shape)
        drawn = base * np.exp(spread * noise) if base else spread * noise
        out[name] = __import__('jax').numpy.asarray(drawn.astype(out[name].dtype))
    for name, factor in factors.items():
        out[name] = (out[name] * factor).astype(out[name].dtype)
    return out
```

```python
import concourse.bass as bass
from concourse import mybir
from contextlib import ExitStack, contextmanager

F32 = mybir.dt.float32
F32R = mybir.dt.float32r
BF16 = mybir.dt.bfloat16
I32 = mybir.dt.int32
U32 = mybir.dt.uint32
ACT = mybir.ActivationFunctionType
ALU = mybir.AluOpType
AX = mybir.AxisListType

P = 128
SEQ, META, D = 1024, 16, 1024
L = SEQ + META
NT = SEQ // P
KD = D // P
HEADS, HD = 8, 64
PAIRS = HEADS // 2
AW, CW = 512, 512
Q0, K0, V0, F0, X0, B0, C0 = 0, 512, 1024, 1536, 1544, 2056, 2568
NG, EPG, NE, DE = 4, 8, 32, 512
EPS = 1e-6
NEG = -1e30
BLK = P
CAP = BLK
OVB = 2 * SEQ // CAP
NBLK = NE + OVB
NB_LESS = SEQ // CAP
CHUNKS = [(0, 348), (348, 346), (694, 346)]
BANK = 512


class Chain:

    def __init__(self, eng, sem):
        self.eng, self.sem, self.base, self.n, self.off = eng, sem, 0, 0, None

    def link(self, ins):
        ins.then_inc(self.sem, 1)
        self.n += 1
        self.eng.wait_ge(self.sem, self.base + self.n if self.off is None else self.off + (self.base + self.n))

    def enter(self, i, per):
        self.base, self.n, self.off, self.per = self.base + self.n, 0, i * per, per

    def leave(self, trips):
        assert self.n == self.per, (self.n, self.per)
        self.base, self.n, self.off = self.base + trips * self.per, 0, None


def wait_apart(eng, sem, value, passed):
    eng.wait_ge(sem, value)
    eng.sem_inc(passed, 1)


class Core:

    def __init__(self, nc):
        self.nc = nc

    def sem(self, name):
        return self.sems.enter_context(self.nc.semaphore(name))

    @contextmanager
    def stage(self):
        used = []
        with ExitStack() as self.sems:
            named = self.sem
            self.sem = lambda name: used.append(named(name)) or used[-1]
            yield
            self.sem = named
            with self.nc.Block() as block:
                @block.gpsimd
                def _(pool):
                    for sem in used:
                        pool.sem_clear(sem)

    def sb(self, ctx, name, shape, dt):
        return ctx.enter_context(self.nc.sbuf_tensor(name, shape, dt))

    def ps(self, ctx, name, shape, dt=F32):
        return ctx.enter_context(self.nc.psum_tensor(name, shape, dt))


def constants(c, nc, mix_norm):
    made = c.sem("const_made")
    load = c.sem("const_load")
    steps = [
        (c.ident, 0.0), (c.maskneg, 0.0), (c.blkavg, 0.0), (c.tri, 1.0), (c.ones_bf, 1.0), (c.ident_bf, 0.0)]
    with nc.Block() as block:
        @block.sync
        def _(sp):
            for j in range(KD):
                sp.dma_start(c.mixg[:, j:j + 1], mix_norm[0, j * P:(j + 1) * P].rearrange("(p o) -> p o", o=1)).then_inc(load, 16)
            sp.wait_ge(load, 16 * KD)

        @block.gpsimd
        def _(pool):
            for buf, value in steps:
                nc.gpsimd.memset(buf[:], value).then_inc(made, 1)
            pool.wait_ge(made, len(steps))
            nc.gpsimd.affine_select(out=c.ident[:], in_=c.ident[:], compare_op=ALU.not_equal, fill=1.0, base=0,
                                    pattern=[[-1, P]], channel_multiplier=1)
            nc.gpsimd.affine_select(out=c.ident_bf[:], in_=c.ident_bf[:], compare_op=ALU.not_equal, fill=1.0, base=0,
                                    pattern=[[-1, P]], channel_multiplier=1)
            nc.gpsimd.affine_select(out=c.maskneg[:], in_=c.maskneg[:], compare_op=ALU.is_ge, fill=NEG, base=0,
                                    pattern=[[-1, P]], channel_multiplier=1)
            nc.gpsimd.affine_select(out=c.tri[:], in_=c.tri[:], compare_op=ALU.is_gt, fill=0.0, base=0,
                                    pattern=[[1, P]], channel_multiplier=-1).then_inc(made, 1)

        @block.vector
        def _(dve):
            dve.wait_ge(made, len(steps))
            nc.vector.memset(c.blkavg[0:HD, 0:HD], 1.0 / HD)
            nc.vector.memset(c.blkavg[HD:P, HD:P], 1.0 / HD)
            nc.vector.memset(c.eps[:], EPS)


def norm_and_transpose(c, nc, x, meta_tokens, attn_norm):
    with ExitStack() as ctx:
        xt = [c.sb(ctx, f"n_x{s}", [P, D], F32) for s in range(2)]
        zt = [c.sb(ctx, f"n_z{s}", [P, D], F32) for s in range(2)]
        gain = c.sb(ctx, "n_gain", [P, D], F32)
        ss = c.sb(ctx, "n_ss", [P, 2], F32)
        ms = c.sb(ctx, "n_ms", [P, 2], F32)
        rs = c.sb(ctx, "n_rs", [P, 2], F32)
        pz = [c.ps(ctx, f"n_pz{s}", [P, D]) for s in range(2)]
        gain_in = c.sem("n_gain_in")
        x_in = [c.sem(f"n_x_in{s}") for s in range(2)]
        squared, scaled, turned, hi_done, lo_done = (c.sem("n_" + n) for n in
                                                     ("squared", "scaled", "turned", "hi_done", "lo_done"))
        own, own_a, passed = c.sem("n_own"), c.sem("n_own_a"), c.sem("n_passed")
        with nc.Block() as block:
            @block.sync
            def _(sp):
                sp.dma_start(gain[:], attn_norm[0, :].partition_broadcast(P)).then_inc(gain_in, 16)
                sp.dma_start(xt[1][0:META, :], meta_tokens[:, :]).then_inc(x_in[1], 16)
                with sp.Fori(0, NT // 2) as i:
                    for u in range(2):
                        sp.wait_ge(scaled, i * 2 + (1 + u))
                        sp.dma_start(xt[u][:], x[0, bass.ds(i * (2 * P) + u * P, P), :]).then_inc(x_in[u], 16)

            @block.scalar
            def _(act):
                chain_a = Chain(act, own_a)
                link_a = chain_a.link

                def square(slot, n, m, arrived):
                    act.wait_ge(x_in[slot], arrived)
                    if n is not None:
                        act.wait_ge(turned, n)
                    link_a(nc.scalar.activation(zt[slot][0:m, :], xt[slot][0:m, :], ACT.Square,
                                                accum_out=ss[0:m, slot:slot + 1]))
                    nc.scalar.activation(ms[0:m, slot:slot + 1], ss[0:m, slot:slot + 1], ACT.Sqrt, scale=1.0 / D,
                                         bias=c.eps[0:m, 0:1]).then_inc(squared, 1)

                def high(slot, n, m, col):
                    wait_apart(act, turned, n, passed)
                    nc.scalar.activation(c.zh[:, :, bass.ds(col, m)],
                                         pz[slot][:].rearrange("p (k t) -> p k t", t=P)[:, :, 0:m],
                                         ACT.Copy).then_inc(hi_done, 1)
                square(1, None, META, 16)
                high(1, 2, META, 0)
                with act.Fori(0, NT // 2) as i:
                    chain_a.enter(i, 2)
                    for u in range(2):
                        square(u, i * 2 + (1 + u), P, i * 16 + 16 * (u + 1))
                    for u in range(2):
                        high(u, i * 2 + (3 + u), P, i * (2 * P) + META + u * P)
                chain_a.leave(NT // 2)

            @block.vector
            def _(dve):
                own_chain = Chain(dve, own)
                link = own_chain.link

                def scale(slot, n, m):
                    dve.wait_ge(squared, n)
                    link(nc.vector.reciprocal(rs[0:m, slot:slot + 1], ms[0:m, slot:slot + 1]))
                    nc.vector.scalar_tensor_tensor(out=zt[slot][0:m, :], in0=xt[slot][0:m, :],
                                                   scalar=rs[0:m, slot:slot + 1], in1=gain[0:m, :],
                                                   op0=ALU.mult, op1=ALU.mult).then_inc(scaled, 1)

                def low(slot, n, m, col):
                    dve.wait_ge(hi_done, n)
                    nc.vector.tensor_tensor(c.zl[:, :, bass.ds(col, m)],
                                            pz[slot][:].rearrange("p (k t) -> p k t", t=P)[:, :, 0:m],
                                            c.zh[:, :, bass.ds(col, m)].bitcast(F32), ALU.subtract).then_inc(lo_done, 1)
                dve.sem_inc(scaled, 1)
                dve.sem_inc(lo_done, 1)
                dve.wait_ge(gain_in, 16)
                scale(1, 1, META)
                low(1, 1, META, 0)
                with dve.Fori(0, NT // 2) as i:
                    own_chain.enter(i, 2)
                    for u in range(2):
                        scale(u, i * 2 + (2 + u), P)
                    for u in range(2):
                        low(u, i * 2 + (2 + u), P, i * (2 * P) + META + u * P)
                own_chain.leave(NT // 2)

            @block.tensor
            def _(pe):
                def turn(slot, n, m):
                    pe.wait_ge(scaled, n)
                    for k in range(KD):
                        last = nc.tensor.transpose(pz[slot][:, k * P:k * P + m], zt[slot][0:m, k * P:(k + 1) * P],
                                                   c.ident[0:m, 0:m])
                    last.then_inc(turned, 1)
                pe.sem_inc(turned, 1)
                turn(1, 2, META)
                with pe.Fori(0, NT // 2) as i:
                    for u in range(2):
                        pe.wait_ge(lo_done, i * 2 + (1 + u))
                        turn(u, i * 2 + (3 + u), P)


def three_passes(nc, out, xh, xl, wh, wl, first, last):
    nc.tensor.matmul(out, xh, wh, start=first, stop=False)
    nc.tensor.matmul(out, xh, wl, start=False, stop=False)
    return nc.tensor.matmul(out, xl, wh, start=False, stop=last)


def project(nc, c, outs, wh, wl, cols, m=P):
    for k in range(KD):
        for w, z, first, last in ((wh, c.zh, k == 0, False), (wh, c.zl, False, False), (wl, c.zh, False, k == KD - 1)):
            for out, (at, n) in zip(outs, cols):
                mm = nc.tensor.matmul(out, w[:, k, 0:m], z[:, k, at:at + n], start=first, stop=last)
    return mm


def forget_gates(c, nc, w_in, b_forget):
    with ExitStack() as ctx:
        w = c.sb(ctx, "f_w", [P, KD, HEADS], F32)
        wh = c.sb(ctx, "f_wh", [P, KD, HEADS], F32R)
        wl = c.sb(ctx, "f_wl", [P, KD, HEADS], F32R)
        bias = c.sb(ctx, "f_bias", [HEADS, 1], F32)
        y, mag, e, sp1, logf, cum, one = (c.sb(ctx, "f_" + n, [HEADS, L], F32) for n in
                                          ("y", "mag", "e", "sp1", "logf", "cum", "one"))
        pf = c.ps(ctx, "f_p", [P, 3 * BANK])
        w_ld, hi_done, lo_done, mm_done, y_done, soft_done, cum_done, stored, own, own_a = (
            c.sem("f_" + n) for n in ("w_in", "hi_done", "lo_done", "mm_done", "y_done", "soft_done", "cum_done",
                                      "stored", "own", "own_a"))
        with nc.Block() as block:
            @block.sync
            def _(sp):
                sp.dma_start(w[:], w_in[0, :, F0:F0 + HEADS].rearrange("(k p) n -> p k n", p=P)).then_inc(w_ld, 16)
                sp.dma_start(bias[:], b_forget[0, :].rearrange("(p o) -> p o", o=1)).then_inc(w_ld, 16)
                sp.wait_ge(cum_done, 1)
                sp.dma_start(c.negcum[:, :], cum[:]).then_inc(stored, 16)
                sp.wait_ge(stored, 16)

            @block.scalar
            def _(act):
                act.wait_ge(w_ld, 32)
                nc.scalar.activation(wh[:], w[:], ACT.Copy).then_inc(hi_done, 1)
                act.wait_ge(y_done, 1)
                nc.scalar.activation(mag[:], y[:], ACT.Abs).then_inc(own_a, 1)
                act.wait_ge(own_a, 1)
                nc.scalar.activation(e[:], mag[:], ACT.Exp, scale=-1.0).then_inc(own_a, 1)
                act.wait_ge(own_a, 2)
                nc.scalar.activation(sp1[:], e[:], ACT.Ln, bias=1.0).then_inc(soft_done, 1)

            @block.vector
            def _(dve):
                link = Chain(dve, own).link
                link(nc.vector.memset(one[:], 1.0))
                dve.wait_ge(w_ld, 32)
                dve.wait_ge(hi_done, 1)
                nc.vector.tensor_tensor(wl[:], w[:], wh[:].bitcast(F32), ALU.subtract).then_inc(lo_done, 1)
                dve.wait_ge(mm_done, 1)
                for b, (at, n) in enumerate(CHUNKS):
                    last = nc.vector.tensor_scalar(y[:, at:at + n], pf[0:HEADS, b * BANK:b * BANK + n], bias[:, 0:1],
                                                   None, ALU.add)
                last.then_inc(y_done, 1)
                dve.wait_ge(soft_done, 1)
                link(nc.vector.scalar_tensor_tensor(out=logf[:], in0=y[:], scalar=0.0, in1=sp1[:], op0=ALU.min,
                                                    op1=ALU.subtract))
                nc.vector.tensor_tensor_scan(cum[:], one[:], logf[:], 0.0, ALU.mult, ALU.subtract).then_inc(cum_done, 1)

            @block.tensor
            def _(pe):
                pe.wait_ge(hi_done, 1)
                pe.wait_ge(lo_done, 1)
                project(nc, c, [pf[0:HEADS, b * BANK:b * BANK + n] for b, (_, n) in enumerate(CHUNKS)], wh, wl, CHUNKS,
                        HEADS).then_inc(mm_done, 1)


def tile_groups(i):
    full = list(range(i + 1))
    return [full[a:a + 4] for a in range(0, i + 1, 4)] + [["meta"]]


def attention(c, nc, w_in):
    GR = [tile_groups(i) for i in range(NT)] * 2
    STEPS = 2 * NT
    before = [sum(len(g) for g in GR[:s]) for s in range(STEPS + 1)]
    NGR = before[-1]
    assert NGR % 2 == 0
    NPV = STEPS // 2
    with ExitStack() as ctx:
        raw = [c.sb(ctx, f"a_raw{s}", [P, KD, P], F32) for s in range(2)]
        wh = [c.sb(ctx, f"a_wh{t}", [P, KD, P], F32R) for t in range(3)]
        wl = [c.sb(ctx, f"a_wl{t}", [P, KD, P], F32R) for t in range(3)]
        qs = c.sb(ctx, "a_qs", [P, 2, SEQ], F32R)
        kh = c.sb(ctx, "a_kh", [P, 2, L], F32R)
        kl = c.sb(ctx, "a_kl", [P, L], F32R)
        v2 = c.sb(ctx, "a_v2", [P, NT + 1, 2, P], F32R)
        o = c.sb(ctx, "a_o", [P, L], F32)
        pth = c.sb(ctx, "a_pth", [P, NT + 1, 2 * P], F32R)
        ptl = c.sb(ctx, "a_ptl", [P, NT + 1, 2 * P], F32R)
        tp = [c.sb(ctx, f"a_tp{s}", [P, L], F32) for s in range(2)]
        cb = [c.sb(ctx, f"a_cb{h}", [P, L], F32) for h in range(2)]
        half = [c.sb(ctx, f"a_half{s}", [P, 2 * P], F32) for s in range(2)]
        top = c.sb(ctx, "a_top", [P, STEPS], F32)
        ntop = c.sb(ctx, "a_ntop", [P, STEPS], F32)
        den = c.sb(ctx, "a_den", [P, STEPS], F32)
        rden = c.sb(ctx, "a_rden", [P, STEPS], F32)
        s3 = c.ps(ctx, "a_s3", [P, 3 * BANK])
        s2 = c.ps(ctx, "a_s2", [P, 2 * BANK])
        pt = c.ps(ctx, "a_pt", [P, 2 * BANK])
        po = c.ps(ctx, "a_po", [P, BANK])
        sc_ps = [s2, s3]
        names = ("split_hi", "split_lo", "projected", "q_hi", "q_lo", "k_hi", "k_lo", "v_copied", "v_turned", "v_hi",
                 "v_lo", "scored", "topped", "probs", "turned", "pt_hi", "pt_lo", "pv_done", "half_copied", "o_added",
                 "rden_done", "spread", "o_scaled", "squared", "averaged", "rooted", "mixed", "own", "passed")
        S = {n: c.sem("a_" + n) for n in names}
        raw_in = [c.sem(f"a_raw_in{s}") for s in range(2)]
        cb_in = [c.sem(f"a_cb_in{h}") for h in range(2)]
        three = [s3[:, b * BANK:b * BANK + n] for b, (_, n) in enumerate(CHUNKS)]
        vbanks = [pt[:, 0:CHUNKS[0][1]], pt[:, BANK:BANK + CHUNKS[1][1]], po[:, 0:CHUNKS[2][1]]]
        RAW = [0, 1, 0]
        lower, upper = slice(0, HD), slice(HD, P)
        own_half = [lower, upper]
        other_half = [upper, lower]

        def width(i):
            return META + P * (i + 1)

        with nc.Block() as block:
            @block.sync
            def _(sp):
                with sp.Fori(0, PAIRS) as i:
                    for t, off in enumerate((Q0, K0, V0)):
                        sp.wait_ge(S["split_lo"], i * 3 + (3, 2, 4)[t])
                        sp.dma_start(raw[RAW[t]][:], w_in[0, :, bass.ds(i * P + off, P)].rearrange(
                            "(k p) n -> p k n", p=P)).then_inc(raw_in[RAW[t]], 16)
                    for h in range(2):
                        sp.wait_ge(S["topped"], i * STEPS + (NT * h + NT))
                        sp.dma_start(cb[h][:], c.negcum[bass.ds(i * 2 + h, 1), :].partition_broadcast(P).rearrange(
                            "p o l -> p (o l)")).then_inc(cb_in[h], 16)

            @block.scalar
            def _(act):
                with act.Fori(0, PAIRS) as i:
                    for t in range(3):
                        act.wait_ge(raw_in[RAW[t]], i * (32, 16, 32)[t] + (16, 16, 32)[t])
                        act.wait_ge(S["projected"], i * 3 + (t + 1))
                        nc.scalar.activation(wh[t][:], raw[RAW[t]][:], ACT.Copy).then_inc(S["split_hi"], 1)
                    act.wait_ge(S["projected"], i * 3 + 4)
                    nc.scalar.activation(qs[lower, 0, :], s2[lower, :], ACT.Copy, scale=HD ** -0.5)
                    nc.scalar.activation(qs[upper, 1, :], s2[upper, :], ACT.Copy, scale=HD ** -0.5).then_inc(S["q_hi"], 1)
                    act.wait_ge(S["projected"], i * 3 + 5)
                    for b, (at, n) in enumerate(CHUNKS):
                        ps = three[b]
                        nc.scalar.activation(kh[lower, 0, at:at + n], ps[lower, :], ACT.Copy)
                        nc.scalar.activation(kh[upper, 0, at:at + n], ps[lower, :], ACT.Copy)
                        nc.scalar.activation(kh[lower, 1, at:at + n], ps[upper, :], ACT.Copy)
                        last = nc.scalar.activation(kh[upper, 1, at:at + n], ps[upper, :], ACT.Copy)
                    last.then_inc(S["k_hi"], 1)
                    act.wait_ge(S["projected"], i * 3 + 6)
                    act.wait_ge(S["mixed"], i + 1)
                    for b, (at, n) in enumerate(CHUNKS):
                        last = nc.scalar.activation(o[:, at:at + n], vbanks[b], ACT.Copy)
                    last.then_inc(S["v_copied"], 1)
                    act.wait_ge(S["v_turned"], i + 1)
                    vt = s2[:].rearrange("p (t f) -> p t f", f=P)
                    for h in range(2):
                        f = own_half[h]
                        nc.scalar.activation(v2[:, 0:NT, h, f], vt[:, :, f], ACT.Copy)
                        last = nc.scalar.activation(v2[0:META, NT, h, f], s3[0:META, 2 * BANK + f.start:2 * BANK + f.stop],
                                                    ACT.Copy)
                    last.then_inc(S["v_hi"], 1)
                    for s in range(STEPS + 2):
                        if s >= 3 and s % 2 == 1:
                            g = (s - 3) // 2
                            h = g // (NPV // 2)
                            act.wait_ge(S["pv_done"], i * NPV + (g + 1))
                            act.wait_ge(S["o_added"], i * NPV + (g + 1))
                            nc.scalar.activation(half[g % 2][own_half[h], :],
                                                 po[other_half[h], (g % 2) * 2 * P:(g % 2 + 1) * 2 * P],
                                                 ACT.Copy).then_inc(S["half_copied"], 1)
                        if s < STEPS:
                            w = width(s % NT)
                            act.wait_ge(S["topped"], i * STEPS + (STEPS + s + 1))
                            nc.scalar.activation(tp[s % 2][:, 0:w], tp[s % 2][:, 0:w], ACT.Exp, bias=ntop[:, s:s + 1],
                                                 accum_out=den[:, s:s + 1]).then_inc(S["probs"], 1)
                        if 1 <= s <= STEPS:
                            r = s - 1
                            if r % 2 == 0 and r >= 2:
                                act.wait_ge(S["pv_done"], i * NPV + r // 2)
                            for a, group in enumerate(GR[r]):
                                n = before[r] + a
                                act.wait_ge(S["turned"], i * NGR + (n + 1))
                                slot = pt[:, (n % 2) * BANK:(n % 2) * BANK + BANK]
                                cols = slice((r % 2) * P, (r % 2) * P + P)
                                if group == ["meta"]:
                                    ins = nc.scalar.activation(pth[0:META, NT, cols], slot[0:META, 0:P], ACT.Copy)
                                else:
                                    ins = nc.scalar.activation(
                                        pth[:, group[0]:group[-1] + 1, cols],
                                        slot[:, 0:len(group) * P].rearrange("p (t q) -> p t q", q=P), ACT.Copy)
                                ins.then_inc(S["pt_hi"], 1)
                    act.wait_ge(S["o_scaled"], i + 1)
                    nc.scalar.activation(tp[0][:, 0:SEQ], o[:, 0:SEQ], ACT.Square).then_inc(S["squared"], 1)
                    act.wait_ge(S["averaged"], i + 1)
                    nc.scalar.activation(tp[1][:, 0:SEQ], s3[:, 0:SEQ], ACT.Sqrt, bias=c.eps[:, 0:1]).then_inc(S["rooted"], 1)

            @block.vector
            def _(dve):
                chain = Chain(dve, S["own"])
                link = chain.link
                dve.sem_inc(S["split_lo"], 3)
                dve.sem_inc(S["topped"], STEPS)
                dve.sem_inc(S["o_added"], 2)
                dve.sem_inc(S["mixed"], 1)
                with dve.Fori(0, PAIRS) as i:
                    chain.enter(i, STEPS + 2)
                    for t in range(3):
                        dve.wait_ge(S["split_hi"], i * 3 + (t + 1))
                        nc.vector.tensor_tensor(wl[t][:], raw[RAW[t]][:], wh[t][:].bitcast(F32),
                                                ALU.subtract).then_inc(S["split_lo"], 1)
                    dve.wait_ge(S["q_hi"], i + 1)
                    nc.vector.scalar_tensor_tensor(out=qs[upper, 0, :], in0=s2[lower, :], scalar=HD ** -0.5,
                                                   in1=qs[lower, 0, :].bitcast(F32), op0=ALU.mult, op1=ALU.subtract)
                    nc.vector.scalar_tensor_tensor(out=qs[lower, 1, :], in0=s2[upper, :], scalar=HD ** -0.5,
                                                   in1=qs[upper, 1, :].bitcast(F32), op0=ALU.mult,
                                                   op1=ALU.subtract).then_inc(S["q_lo"], 1)
                    dve.wait_ge(S["k_hi"], i + 1)
                    for b, (at, n) in enumerate(CHUNKS):
                        for h in range(2):
                            f = own_half[h]
                            last = nc.vector.tensor_tensor(kl[f, at:at + n], three[b][f, :],
                                                           kh[f, h, at:at + n].bitcast(F32), ALU.subtract)
                    last.then_inc(S["k_lo"], 1)
                    dve.wait_ge(S["v_hi"], i + 1)
                    vt = s2[:].rearrange("p (t f) -> p t f", f=P)
                    for h in range(2):
                        f, g = own_half[h], other_half[h]
                        nc.vector.tensor_tensor(v2[:, 0:NT, h, g], vt[:, :, f], v2[:, 0:NT, h, f].bitcast(F32),
                                                ALU.subtract)
                        last = nc.vector.tensor_tensor(v2[0:META, NT, h, g],
                                                       s3[0:META, 2 * BANK + f.start:2 * BANK + f.stop],
                                                       v2[0:META, NT, h, f].bitcast(F32), ALU.subtract)
                    last.then_inc(S["v_lo"], 1)
                    for s in range(STEPS + 2):
                        if s < STEPS:
                            h, w = s // NT, width(s % NT)
                            dve.wait_ge(S["scored"], i * STEPS + (s + 1))
                            if s % NT == 0:
                                dve.wait_ge(cb_in[h], i * 16 + 16)
                            if s >= 2:
                                dve.wait_ge(S["turned"], i * NGR + before[s - 1])
                            dve.sem_inc(S["passed"], 1)
                            link(nc.vector.tensor_tensor_reduce(tp[s % 2][:, 0:w], sc_ps[s % 2][:, 0:w],
                                                                cb[h][:, 0:w], 1.0, NEG, ALU.add, ALU.max,
                                                                top[:, s:s + 1]))
                            nc.vector.tensor_scalar(ntop[:, s:s + 1], top[:, s:s + 1], -1.0, None,
                                                    ALU.mult).then_inc(S["topped"], 1)
                        if s >= 3 and s % 2 == 1:
                            g = (s - 3) // 2
                            f = own_half[g // (NPV // 2)]
                            at = (g % (NPV // 2)) * 2 * P
                            dve.wait_ge(S["half_copied"], i * NPV + (g + 1))
                            nc.vector.tensor_tensor(o[f, at:at + 2 * P], po[f, (g % 2) * 2 * P:(g % 2 + 1) * 2 * P],
                                                    half[g % 2][f, :], ALU.add).then_inc(S["o_added"], 1)
                        if 1 <= s <= STEPS:
                            r = s - 1
                            for a, group in enumerate(GR[r]):
                                n = before[r] + a
                                dve.wait_ge(S["pt_hi"], i * NGR + (n + 1))
                                slot = pt[:, (n % 2) * BANK:(n % 2) * BANK + BANK]
                                cols = slice((r % 2) * P, (r % 2) * P + P)
                                if group == ["meta"]:
                                    ins = nc.vector.tensor_tensor(ptl[0:META, NT, cols], slot[0:META, 0:P],
                                                                  pth[0:META, NT, cols].bitcast(F32), ALU.subtract)
                                else:
                                    kt = slice(group[0], group[-1] + 1)
                                    ins = nc.vector.tensor_tensor(
                                        ptl[:, kt, cols], slot[:, 0:len(group) * P].rearrange("p (t q) -> p t q", q=P),
                                        pth[:, kt, cols].bitcast(F32), ALU.subtract)
                                ins.then_inc(S["pt_lo"], 1)
                    dve.wait_ge(S["probs"], i * STEPS + STEPS)
                    link(nc.vector.reciprocal(rden[:], den[:]))
                    dve.wait_ge(S["turned"], i * NGR + NGR)
                    nc.vector.tensor_copy(tp[0][:, 0:SEQ].rearrange("p (t h f) -> p t h f", t=NT, h=2),
                                          rden[:].rearrange("p (h t o) -> p t h o", h=2, o=1).to_broadcast(
                                              [P, NT, 2, HD])).then_inc(S["rden_done"], 1)
                    dve.wait_ge(S["spread"], i + 1)
                    dve.wait_ge(S["o_added"], i * NPV + (NPV + 2))
                    nc.vector.tensor_tensor(o[:, 0:SEQ], o[:, 0:SEQ], s2[:], ALU.mult).then_inc(S["o_scaled"], 1)
                    dve.wait_ge(S["rooted"], i + 1)
                    link(nc.vector.reciprocal(tp[1][:, 0:SEQ], tp[1][:, 0:SEQ]))
                    nc.vector.scalar_tensor_tensor(out=c.mx[:, bass.ds(i, 1), :].rearrange("p o t -> p (o t)"),
                                                   in0=o[:, 0:SEQ], scalar=c.mixg[:, bass.ds(i, 1)],
                                                   in1=tp[1][:, 0:SEQ], op0=ALU.mult,
                                                   op1=ALU.mult).then_inc(S["mixed"], 1)
                chain.leave(PAIRS)

            @block.tensor
            def _(pe):
                pe.sem_inc(S["projected"], 3)

                def scores(s):
                    h, q = s // NT, s % NT
                    ps, w, f = sc_ps[s % 2], width(q), own_half[h]
                    pieces = [(a, min(BANK, w - a)) for a in range(0, w, BANK)]
                    for at, n in pieces:
                        last_bank = at + n == w
                        nc.tensor.matmul(ps[:, at:at + n], qs[:, h, q * P:(q + 1) * P], kh[:, h, at:at + n],
                                         start=True, stop=False)
                        mm = nc.tensor.matmul(ps[:, at:at + n], qs[f, h, q * P:(q + 1) * P], kl[f, at:at + n],
                                              start=False, stop=True)
                        a = max(at, w - P)
                        if a < at + n:
                            mm = nc.tensor.matmul(ps[:, a:at + n], c.ident_bf[:], c.maskneg[:, a - (w - P):at + n - (w - P)],
                                                  start=False, stop=True, skip_group_check=True)
                    mm.then_inc(S["scored"], 1)

                with pe.Fori(0, PAIRS) as i:
                    pe.wait_ge(S["mixed"], i + 1)
                    for t, (outs, cols) in enumerate(((
                            [s2[:, 0:BANK], s2[:, BANK:2 * BANK]], [(META, BANK), (META + BANK, BANK)]),
                            (three, CHUNKS), (vbanks, CHUNKS))):
                        pe.wait_ge(S["split_lo"], i * 3 + (t + 4))
                        project(nc, c, outs, wh[t], wl[t], cols).then_inc(S["projected"], 1)
                    for name in ("v_copied", "q_lo", "k_lo"):
                        pe.wait_ge(S[name], i + 1)
                    for t in range(NT):
                        nc.tensor.transpose(s2[:, t * P:(t + 1) * P], o[:, META + t * P:META + (t + 1) * P], c.ident[:])
                    nc.tensor.transpose(s3[0:META, 2 * BANK:2 * BANK + P], o[:, 0:META], c.ident[:]).then_inc(S["v_turned"], 1)
                    pe.wait_ge(S["v_lo"], i + 1)
                    for s in range(STEPS + 2):
                        if s < STEPS:
                            if s >= 2:
                                pe.wait_ge(S["topped"], i * STEPS + (STEPS + s - 1))
                            scores(s)
                        if s >= 3 and s % 2 == 1:
                            g = (s - 3) // 2
                            h, ga = g // (NPV // 2), g % (NPV // 2)
                            pe.wait_ge(S["pt_lo"], i * NGR + before[2 * g + 2])
                            pe.wait_ge(S["o_added"], i * NPV + (g + 1))
                            out = po[:, (g % 2) * 2 * P:(g % 2 + 1) * 2 * P]
                            for kt in range(2 * ga + 2):
                                a = P if kt == 2 * ga + 1 else 0
                                for probs in (pth, ptl):
                                    nc.tensor.matmul(out[:, a:2 * P], v2[:, kt, h, :], probs[:, kt, a:2 * P],
                                                     start=kt == 0 and probs is pth, stop=False, skip_group_check=True)
                            nc.tensor.matmul(out, v2[0:META, NT, h, :], pth[0:META, NT, :], start=False, stop=False,
                                             skip_group_check=True)
                            nc.tensor.matmul(out, v2[0:META, NT, h, :], ptl[0:META, NT, :], start=False, stop=True,
                                             skip_group_check=True).then_inc(S["pv_done"], 1)
                        if 1 <= s <= STEPS:
                            r = s - 1
                            pe.wait_ge(S["probs"], i * STEPS + (r + 1))
                            for a, group in enumerate(GR[r]):
                                n = before[r] + a
                                if n >= 2:
                                    pe.wait_ge(S["pt_lo"], i * NGR + (n - 1))
                                slot = pt[:, (n % 2) * BANK:(n % 2) * BANK + BANK]
                                if group == ["meta"]:
                                    mm = nc.tensor.transpose(slot[0:META, 0:P], tp[r % 2][:, 0:META], c.ident[:])
                                else:
                                    for b, kt in enumerate(group):
                                        mm = nc.tensor.transpose(slot[:, b * P:(b + 1) * P],
                                                                 tp[r % 2][:, META + kt * P:META + (kt + 1) * P],
                                                                 c.ident[:])
                                mm.then_inc(S["turned"], 1)
                    pe.wait_ge(S["rden_done"], i + 1)
                    for t in range(NT):
                        mm = nc.tensor.transpose(s2[:, t * P:(t + 1) * P], tp[0][:, t * P:(t + 1) * P], c.ident[:])
                    mm.then_inc(S["spread"], 1)
                    pe.wait_ge(S["squared"], i + 1)
                    for b in range(2):
                        mm = nc.tensor.matmul(s3[:, b * BANK:(b + 1) * BANK], c.blkavg[:], tp[0][:, b * BANK:(b + 1) * BANK],
                                              start=True, stop=True)
                    mm.then_inc(S["averaged"], 1)


def convolution(c, nc, w_in, conv_w):
    FT = CW // P
    TAPS = 3
    with ExitStack() as ctx:
        raw = [c.sb(ctx, f"v_raw{t}", [P, KD, P], F32) for t in range(3)]
        wh = [c.sb(ctx, f"v_wh{t}", [P, KD, P], F32R) for t in range(3)]
        wl = [c.sb(ctx, f"v_wl{t}", [P, KD, P], F32R) for t in range(3)]
        taps = c.sb(ctx, "v_taps", [P, TAPS * FT], F32)
        xs = c.sb(ctx, "v_xs", [P, L], F32)
        u = c.sb(ctx, "v_u", [P, L], F32)
        acc = [c.sb(ctx, f"v_acc{s}", [P, SEQ], F32) for s in range(2)]
        sq = c.sb(ctx, "v_sq", [P, SEQ], F32)
        root = c.sb(ctx, "v_root", [P, SEQ], F32)
        px = c.ps(ctx, "v_px", [P, 3 * BANK])
        pc = c.ps(ctx, "v_pc", [P, 3 * BANK])
        pb = c.ps(ctx, "v_pb", [P, 2 * BANK])
        S = {n: c.sem("v_" + n) for n in ("taps_in", "split_hi", "split_lo", "projected", "x_copied", "u_done", "gated",
                                          "squared", "averaged", "rooted", "mixed", "own")}
        raw_in = [c.sem(f"v_raw_in{t}") for t in range(3)]
        xb = [px[:, b * BANK:b * BANK + n] for b, (_, n) in enumerate(CHUNKS)]
        cbk = [pc[:, b * BANK:b * BANK + n] for b, (_, n) in enumerate(CHUNKS)]
        halves = [pb[:, 0:BANK], pb[:, BANK:2 * BANK]]
        with nc.Block() as block:
            @block.sync
            def _(sp):
                for t in range(TAPS):
                    for f in range(FT):
                        sp.dma_start(taps[:, t * FT + f:t * FT + f + 1],
                                     conv_w[0, t, f * P:(f + 1) * P].rearrange("(p o) -> p o", o=1)).then_inc(S["taps_in"], 16)
                with sp.Fori(0, FT) as i:
                    for t, off in enumerate((X0, C0, B0)):
                        sp.wait_ge(S["split_lo"], i * 3 + (t + 1))
                        sp.dma_start(raw[t][:], w_in[0, :, bass.ds(i * P + off, P)].rearrange(
                            "(k p) n -> p k n", p=P)).then_inc(raw_in[t], 16)

            @block.scalar
            def _(act):
                with act.Fori(0, FT) as i:
                    for t in range(3):
                        act.wait_ge(raw_in[t], i * 16 + 16)
                        act.wait_ge(S["projected"], i * 3 + (t + 1))
                        nc.scalar.activation(wh[t][:], raw[t][:], ACT.Copy).then_inc(S["split_hi"], 1)
                    act.wait_ge(S["projected"], i * 3 + 4)
                    act.wait_ge(S["u_done"], i + 1)
                    for b, (at, n) in enumerate(CHUNKS):
                        last = nc.scalar.activation(xs[:, at:at + n], xb[b], ACT.Copy)
                    last.then_inc(S["x_copied"], 1)
                    act.wait_ge(S["gated"], i + 1)
                    nc.scalar.activation(sq[:], acc[1][:], ACT.Square).then_inc(S["squared"], 1)
                    act.wait_ge(S["averaged"], i + 1)
                    nc.scalar.activation(root[:], pb[:], ACT.Sqrt, bias=c.eps[:, 0:1]).then_inc(S["rooted"], 1)

            @block.vector
            def _(dve):
                chain = Chain(dve, S["own"])
                link = chain.link
                dve.sem_inc(S["split_lo"], 3)
                dve.sem_inc(S["u_done"], 1)
                dve.wait_ge(S["taps_in"], 16 * TAPS * FT)
                with dve.Fori(0, FT) as i:
                    chain.enter(i, 4)
                    for t in range(3):
                        dve.wait_ge(S["split_hi"], i * 3 + (t + 1))
                        nc.vector.tensor_tensor(wl[t][:], raw[t][:], wh[t][:].bitcast(F32),
                                                ALU.subtract).then_inc(S["split_lo"], 1)
                    dve.wait_ge(S["x_copied"], i + 1)
                    dve.wait_ge(S["projected"], i * 3 + 5)
                    for b, (at, n) in enumerate(CHUNKS):
                        last = nc.vector.tensor_tensor(u[:, at:at + n], xs[:, at:at + n], cbk[b], ALU.mult)
                    last.then_inc(S["u_done"], 1)
                    dve.wait_ge(S["u_done"], i + 2)
                    for t in range(TAPS):
                        src = u[:, META - (TAPS - 1) + t:META - (TAPS - 1) + t + SEQ]
                        w = taps[:, bass.ds(i + t * FT, 1)]
                        if t == 0:
                            link(nc.vector.tensor_scalar(acc[0][:], src, w, None, ALU.mult))
                        else:
                            link(nc.vector.scalar_tensor_tensor(out=acc[t % 2][:], in0=src, scalar=w,
                                                                in1=acc[1 - t % 2][:], op0=ALU.mult, op1=ALU.add))
                    dve.wait_ge(S["projected"], i * 3 + 6)
                    nc.vector.tensor_tensor(acc[1][:], acc[0][:], pb[:], ALU.mult).then_inc(S["gated"], 1)
                    dve.wait_ge(S["rooted"], i + 1)
                    link(nc.vector.reciprocal(root[:], root[:]))
                    nc.vector.scalar_tensor_tensor(
                        out=c.mx[:, bass.ds(i + PAIRS, 1), :].rearrange("p o t -> p (o t)"), in0=acc[1][:],
                        scalar=c.mixg[:, bass.ds(i + PAIRS, 1)], in1=root[:], op0=ALU.mult,
                        op1=ALU.mult).then_inc(S["mixed"], 1)
                    dve.wait_ge(S["mixed"], i + 1)
                chain.leave(FT)

            @block.tensor
            def _(pe):
                pe.sem_inc(S["projected"], 3)
                with pe.Fori(0, FT) as i:
                    for t, (outs, cols) in enumerate(((xb, CHUNKS), (cbk, CHUNKS),
                                                      (halves, [(META, BANK), (META + BANK, BANK)]))):
                        pe.wait_ge(S["split_lo"], i * 3 + (t + 4))
                        if t == 0:
                            pe.wait_ge(S["u_done"], i + 1)
                        project(nc, c, outs, wh[t], wl[t], cols).then_inc(S["projected"], 1)
                    pe.wait_ge(S["squared"], i + 1)
                    for b in range(2):
                        mm = nc.tensor.matmul(halves[b], c.blkavg[:], sq[:, b * BANK:(b + 1) * BANK], start=True, stop=True)
                    mm.then_inc(S["averaged"], 1)
                    pe.wait_ge(S["rooted"], i + 1)


def output_projection(c, nc, x, w_out, ffn_norm, w_rg, b_rg, w_re, b_re):
    NR = NG + NE
    with ExitStack() as ctx:
        raw = [c.sb(ctx, f"o_raw{s}", [P, D], F32) for s in range(2)]
        wh = c.sb(ctx, "o_wh", [P, KD, D], F32R)
        wl = c.sb(ctx, "o_wl", [P, KD, D], F32R)
        mh = [c.sb(ctx, f"o_mh{s}", [P, KD, P], F32R) for s in range(2)]
        ml = [c.sb(ctx, f"o_ml{s}", [P, KD, P], F32R) for s in range(2)]
        xt = [c.sb(ctx, f"o_x{s}", [P, D], F32) for s in range(2)]
        z2 = [c.sb(ctx, f"o_z2{s}", [P, D], F32) for s in range(2)]
        z2t = [c.sb(ctx, f"o_z2t{s}", [P, D], F32) for s in range(2)]
        gain = c.sb(ctx, "o_gain", [P, D], F32)
        wr = c.sb(ctx, "o_wr", [P, KD, NR], F32)
        br = c.sb(ctx, "o_br", [P, NR], F32)
        ss, ms, rs = (c.sb(ctx, "o_" + n, [P, 2], F32) for n in ("ss", "ms", "rs"))
        ph = [c.ps(ctx, f"o_ph{s}", [P, D]) for s in range(2)]
        pz = c.ps(ctx, "o_pz", [P, D])
        pl = c.ps(ctx, "o_pl", [P, BANK])
        S = {n: c.sem("o_" + n) for n in ("w_hi", "w_lo", "m_hi", "m_lo", "multiplied", "h2_done", "squared", "z2_done",
                                          "turned", "t_copied", "logits", "logits_out", "own", "own_a", "passed")}
        raw_in = [c.sem(f"o_raw_in{s}") for s in range(2)]
        x_in = [c.sem(f"o_x_in{s}") for s in range(2)]
        stored = [c.sem(f"o_stored{s}") for s in range(2)]
        small_in = c.sem("o_small_in")

        def mix_tile(i, u):
            return c.mx[:, :, bass.ds(i * (2 * P) + u * P, P)]

        def three(buf):
            return buf[:].rearrange("p (k t) -> p k t", k=KD)

        with nc.Block() as block:
            @block.sync
            def _(sp):
                for k in range(KD):
                    if k >= 2:
                        sp.wait_ge(S["w_lo"], k - 1)
                    sp.dma_start(raw[k % 2][:], w_out[0, k * P:(k + 1) * P, :]).then_inc(raw_in[k % 2], 16)
                sp.dma_start(gain[:], ffn_norm[0, :].partition_broadcast(P)).then_inc(small_in, 16)
                sp.dma_start(wr[:, :, 0:NG], w_rg[0].rearrange("(k p) n -> p k n", p=P)).then_inc(small_in, 16)
                sp.dma_start(wr[:, :, NG:NR], w_re[0].rearrange("(k p) n -> p k n", p=P)).then_inc(small_in, 16)
                sp.dma_start(br[:, 0:NG], b_rg[0, :].partition_broadcast(P)).then_inc(small_in, 16)
                sp.dma_start(br[:, NG:NR], b_re[0, :].partition_broadcast(P)).then_inc(small_in, 16)
                with sp.Fori(0, NT // 2) as i:
                    for u in range(2):
                        sp.wait_ge(S["h2_done"], i * 2 + (u + 1))
                        sp.dma_start(xt[u][:], x[0, bass.ds(i * (2 * P) + u * P, P), :]).then_inc(x_in[u], 16)
                    for u in range(2):
                        sp.wait_ge(S["z2_done"], i * 2 + (u + 1))
                        sp.dma_start(c.z2rows[bass.ds(i * (2 * P) + u * P, P), :], z2[u][:]).then_inc(stored[u], 16)
                for u in range(2):
                    sp.wait_ge(stored[u], 16 * (NT // 2 + 1))

            @block.scalar
            def _(act):
                chain = Chain(act, S["own_a"])
                for k in range(KD):
                    act.wait_ge(raw_in[k % 2], 16 * (k // 2 + 1))
                    nc.scalar.activation(wh[:, k, :], raw[k % 2][:], ACT.Copy).then_inc(S["w_hi"], 1)
                with act.Fori(0, NT // 2) as i:
                    chain.enter(i, 2)
                    for u in range(2):
                        wait_apart(act, S["multiplied"], i * 2 + (u + 1), S["passed"])
                        nc.scalar.activation(mh[u][:], mix_tile(i, u), ACT.Copy).then_inc(S["m_hi"], 1)
                    for u in range(2):
                        act.wait_ge(S["h2_done"], i * 2 + (u + 3))
                        act.wait_ge(stored[u], i * 16 + 16)
                        wait_apart(act, S["turned"], i * 2 + (u + 1), S["passed"])
                        chain.link(nc.scalar.activation(three(z2[u]), mix_tile(i, u), ACT.Square,
                                                        accum_out=ss[:, u:u + 1]))
                        nc.scalar.activation(ms[:, u:u + 1], ss[:, u:u + 1], ACT.Sqrt, scale=1.0 / D,
                                             bias=c.eps[:, 0:1]).then_inc(S["squared"], 1)
                    for u in range(2):
                        act.wait_ge(S["turned"], i * 2 + (u + 3))
                        act.wait_ge(S["logits"], i * 2 + (u + 1))
                        nc.scalar.activation(z2t[u][:], pz[:], ACT.Copy).then_inc(S["t_copied"], 1)
                chain.leave(NT // 2)

            @block.vector
            def _(dve):
                chain = Chain(dve, S["own"])
                dve.sem_inc(S["h2_done"], 2)
                for u in range(2):
                    dve.sem_inc(stored[u], 16)
                for k in range(KD):
                    dve.wait_ge(S["w_hi"], k + 1)
                    nc.vector.tensor_tensor(wl[:, k, :], raw[k % 2][:], wh[:, k, :].bitcast(F32),
                                            ALU.subtract).then_inc(S["w_lo"], 1)
                dve.wait_ge(small_in, 16 * 5)
                with dve.Fori(0, NT // 2) as i:
                    chain.enter(i, 2)
                    for u in range(2):
                        dve.wait_ge(S["m_hi"], i * 2 + (u + 1))
                        nc.vector.tensor_tensor(ml[u][:], mix_tile(i, u), mh[u][:].bitcast(F32),
                                                ALU.subtract).then_inc(S["m_lo"], 1)
                    for u in range(2):
                        dve.wait_ge(S["multiplied"], i * 2 + (u + 3))
                        dve.wait_ge(x_in[u], i * 16 + 16)
                        nc.vector.tensor_tensor(mix_tile(i, u), three(xt[u]), three(ph[u]), ALU.add).then_inc(S["h2_done"], 1)
                    for u in range(2):
                        dve.wait_ge(S["squared"], i * 2 + (u + 1))
                        chain.link(nc.vector.reciprocal(rs[:, u:u + 1], ms[:, u:u + 1]))
                        nc.vector.scalar_tensor_tensor(out=three(z2[u]), in0=mix_tile(i, u), scalar=rs[:, u:u + 1],
                                                       in1=three(gain), op0=ALU.mult, op1=ALU.mult).then_inc(S["z2_done"], 1)
                    for u in range(2):
                        dve.wait_ge(S["logits"], i * 2 + (u + 3))
                        nc.vector.tensor_tensor(c.logits[:, bass.ds(i * 2 + u, 1), :].rearrange("p o n -> p (o n)"),
                                                pl[:, u * P:u * P + NR], br[:], ALU.add).then_inc(S["logits_out"], 1)
                chain.leave(NT // 2)

            @block.tensor
            def _(pe):
                pe.sem_inc(S["multiplied"], 2)
                pe.sem_inc(S["turned"], 2)
                pe.sem_inc(S["logits"], 2)
                pe.wait_ge(S["w_lo"], KD)
                with pe.Fori(0, NT // 2) as i:
                    for u in range(2):
                        pe.wait_ge(S["m_lo"], i * 2 + (u + 1))
                        pe.wait_ge(S["h2_done"], i * 2 + (u + 1))
                        for k in range(KD):
                            for b in range(2):
                                n = slice(b * BANK, (b + 1) * BANK)
                                mm = three_passes(nc, ph[u][:, n], mh[u][:, k, :], ml[u][:, k, :], wh[:, k, n],
                                                  wl[:, k, n], k == 0, k == KD - 1)
                        mm.then_inc(S["multiplied"], 1)
                    for u in range(2):
                        pe.wait_ge(S["z2_done"], i * 2 + (u + 1))
                        if u == 1:
                            pe.wait_ge(S["t_copied"], i * 2 + 1)
                        for k in range(KD):
                            mm = nc.tensor.transpose(pz[:, k * P:(k + 1) * P], z2[u][:, k * P:(k + 1) * P], c.ident[:])
                        mm.then_inc(S["turned"], 1)
                    for u in range(2):
                        pe.wait_ge(S["t_copied"], i * 2 + (u + 1))
                        for k in range(KD):
                            mm = nc.tensor.matmul(pl[:, u * P:u * P + NR], z2t[u][:, k * P:(k + 1) * P], wr[:, k, :],
                                                  start=k == 0, stop=k == KD - 1)
                        mm.then_inc(S["logits"], 1)
                        pe.wait_ge(S["logits_out"], i * 2 + (u + 1))


def route(c, nc):
    with ExitStack() as ctx:
        f = lambda name, shape, dt=F32: c.sb(ctx, "r_" + name, shape, dt)
        iota_i = f("iota_i", [P, NE], I32)
        blank = f("blank", [P, OVB * D], F32)
        iota_e = f("iota_e", [P, NE])
        token = f("token", [P, NT], I32)
        limits_i, limits = f("limits_i", [P, NB_LESS], I32), f("limits", [P, NB_LESS])
        zeros = f("zeros", [NBLK + 1, BLK], I32)
        gmax, gsum, gw, gi = (f(n, [P, NT]) for n in ("gmax", "gsum", "gw", "gi"))
        gd, geq, goh, pen = (f(n, [P, NT, NG]) for n in ("gd", "geq", "goh", "pen"))
        masked = [f(f"masked{j}", [P, NT, NE]) for j in range(2)]
        eq = f("eq", [P, NT, NE])
        hot = [f(f"hot{j}", [P, NT, NE]) for j in range(2)]
        both = f("both", [P, NT, NE], BF16)
        emax = [f(f"emax{j}", [P, NT]) for j in range(2)]
        eidx = f("eidx", [P, 2, NT])
        ediff, eexp, eden = (f(n, [P, NT]) for n in ("ediff", "eexp", "eden"))
        rank = f("rank", [P, NT, NE])
        run = f("run", [P, NT + 1, NE])
        over = f("over", [P, NE, NB_LESS])
        nov, ovend, ovstart, onee = (f(n, [P, NE]) for n in ("nov", "ovend", "ovstart", "onee"))
        pick = f("pick", [P, NT, NE])
        r2, ovs, isov, shift = (f(n, [P, 2, NT]) for n in ("r2", "ovs", "isov", "shift"))
        slot = f("slot", [P, 2, NT])
        ovcmp = f("ovcmp", [P, OVB, NE])
        ove_f = f("ove_f", [P, OVB])
        pairs_f = f("pairs_f", [P, 1])
        tab_i, tab_f = f("tab_i", [NBLK + 1, BLK], I32), f("tab_f", [NBLK + 1, BLK])
        p_in = c.ps(ctx, "r_in", [P, BANK])
        p_tot = c.ps(ctx, "r_tot", [P, BANK])
        p_tab = c.ps(ctx, "r_tab", [P, BANK])
        S = {n: c.sem("r_" + n) for n in ("made", "blanked", "blank_out", "cleared", "g_ready", "g_exp", "e_ready", "e_exp", "marked", "counted",
                                          "slots", "scattered", "tab_in", "tab_f", "tab_turned", "own")}
        tile4 = lambda ap: ap.rearrange("p t (g e) -> p t g e", e=EPG)
        with nc.Block() as block:
            @block.gpsimd
            def _(pool):
                nc.gpsimd.iota(iota_i[:], pattern=[[1, NE]], base=0, channel_multiplier=0)
                nc.gpsimd.iota(limits_i[:], pattern=[[CAP, NB_LESS]], base=CAP, channel_multiplier=0)
                nc.gpsimd.iota(token[:], pattern=[[P, NT]], base=0, channel_multiplier=1)
                nc.gpsimd.memset(zeros[:], 0).then_inc(S["made"], 1)
                nc.gpsimd.memset(blank[:], 0.0).then_inc(S["blanked"], 1)
                pool.wait_ge(S["made"], 1)
                pool.wait_ge(S["cleared"], 16)
                pool.wait_ge(S["slots"], 1)
                for j in range(2):
                    for t in range(NT):
                        nc.gpsimd.indirect_dma_start(
                            out=c.table[:, :], out_offset=bass.IndirectOffsetOnAxis(ap=c.slot_of[:, j * NT + t:j * NT + t + 1],
                                                                                    axis=0),
                            in_=token[:, t:t + 1], in_offset=None).then_inc(S["scattered"], 16)

            @block.sync
            def _(sp):
                sp.wait_ge(S["made"], 1)
                sp.dma_start(c.table[:, :].rearrange("(b r) o -> b (r o)", r=BLK), zeros[:]).then_inc(S["cleared"], 16)
                sp.wait_ge(S["blanked"], 1)
                sp.dma_start(c.yrows[NE * BLK:NBLK * BLK, :].rearrange("(p b) n -> p (b n)", p=P), blank[:]).then_inc(S["blank_out"], 16)
                sp.wait_ge(S["blank_out"], 16)
                sp.wait_ge(S["scattered"], 16 * 2 * NT)
                sp.dma_start(tab_i[:], c.table[:, :].rearrange("(b r) o -> b (r o)", r=BLK)).then_inc(S["tab_in"], 16)
                sp.wait_ge(S["tab_in"], 16)

            @block.scalar
            def _(act):
                act.wait_ge(S["g_ready"], 1)
                nc.scalar.activation(gd[:], gd[:], ACT.Exp).then_inc(S["g_exp"], 1)
                act.wait_ge(S["e_ready"], 1)
                nc.scalar.activation(eexp[:], ediff[:], ACT.Exp).then_inc(S["e_exp"], 1)

            @block.tensor
            def _(pe):
                pe.wait_ge(S["marked"], 1)
                nc.tensor.matmul(p_in[:, 0:NT * NE], c.tri[:], both[:].rearrange("p t e -> p (t e)"), start=True, stop=True)
                nc.tensor.matmul(p_tot[:, 0:NT * NE], c.ones_bf[:], both[:].rearrange("p t e -> p (t e)"), start=True,
                                 stop=True).then_inc(S["counted"], 1)
                pe.wait_ge(S["tab_f"], 1)
                nc.tensor.transpose(p_tab[:, 0:NBLK + 1], tab_f[:], c.ident[0:NBLK + 1, 0:NBLK + 1]).then_inc(S["tab_turned"], 1)

            @block.vector
            def _(dve):
                link = Chain(dve, S["own"]).link
                V = nc.vector
                dve.wait_ge(S["made"], 1)
                link(V.tensor_copy(iota_e[:], iota_i[:]))
                link(V.tensor_copy(limits[:], limits_i[:]))
                lg, le = c.logits[:, :, 0:NG], c.logits[:, :, NG:NG + NE]
                wide = lambda ap, n: ap.rearrange("p (t o) -> p t o", o=1).to_broadcast([P, NT, n])
                ids = lambda n: iota_e[:, 0:n].rearrange("p (o e) -> p o e", o=1).to_broadcast([P, NT, n])

                def first_of_max(values, top, eq, index, hot, n):
                    link(V.tensor_reduce(top, values, AX.X, ALU.max))
                    link(V.tensor_tensor(eq, values, wide(top, n), ALU.is_equal))
                    link(V.tensor_scalar(eq, eq, -float(n), float(n), ALU.mult, ALU.add))
                    link(V.tensor_tensor(eq, eq, ids(n), ALU.add))
                    link(V.tensor_reduce(index, eq, AX.X, ALU.min))
                    link(V.tensor_tensor(hot, ids(n), wide(index, n), ALU.is_equal))
                first_of_max(lg, gmax[:], geq[:], gi[:], goh[:], NG)
                V.tensor_tensor(gd[:], lg, wide(gmax[:], NG), ALU.subtract).then_inc(S["g_ready"], 1)
                link(V.tensor_scalar(pen[:], goh[:], -NEG, NEG, ALU.mult, ALU.add))
                link(V.tensor_tensor(tile4(masked[0][:]), tile4(le), pen[:].rearrange("p t (g o) -> p t g o", o=1)
                                     .to_broadcast([P, NT, NG, EPG]), ALU.add))
                first_of_max(masked[0][:], emax[0][:], eq[:], eidx[:, 0, :], hot[0][:], NE)
                link(V.scalar_tensor_tensor(out=masked[1][:], in0=hot[0][:], scalar=2 * NEG, in1=masked[0][:],
                                            op0=ALU.mult, op1=ALU.add))
                first_of_max(masked[1][:], emax[1][:], eq[:], eidx[:, 1, :], hot[1][:], NE)
                V.tensor_tensor(ediff[:], emax[1][:], emax[0][:], ALU.subtract).then_inc(S["e_ready"], 1)
                V.tensor_tensor(both[:], hot[0][:], hot[1][:], ALU.add).then_inc(S["marked"], 1)
                dve.wait_ge(S["g_exp"], 1)
                link(V.tensor_reduce(gsum[:], gd[:], AX.X, ALU.add))
                link(V.reciprocal(gw[:], gsum[:]))
                dve.wait_ge(S["e_exp"], 1)
                link(V.tensor_scalar(eden[:], eexp[:], 1.0, None, ALU.add))
                link(V.reciprocal(eden[:], eden[:]))
                link(V.tensor_tensor(c.weight[:, 0:NT], gw[:], eden[:], ALU.mult))
                link(V.tensor_tensor(c.weight[:, NT:2 * NT], c.weight[:, 0:NT], eexp[:], ALU.mult))
                dve.wait_ge(S["counted"], 1)
                link(V.memset(run[:, 0, :], 0.0))
                for t in range(NT):
                    link(V.tensor_tensor(run[:, t + 1, :], run[:, t, :], p_tot[:, t * NE:(t + 1) * NE], ALU.add))
                link(V.tensor_tensor(rank[:], run[:, 0:NT, :], p_in[:, 0:NT * NE].rearrange("p (t e) -> p t e", e=NE), ALU.add))
                link(V.tensor_tensor(over[:], run[:, NT, :].rearrange("p (e o) -> p e o", o=1).to_broadcast([P, NE, NB_LESS]),
                                     limits[:].rearrange("p (o b) -> p o b", o=1).to_broadcast([P, NE, NB_LESS]), ALU.is_gt))
                link(V.tensor_reduce(nov[:], over[:], AX.X, ALU.add))
                link(V.memset(onee[:], 1.0))
                link(V.tensor_tensor_scan(ovend[:], onee[:], nov[:], 0.0, ALU.mult, ALU.add))
                link(V.tensor_tensor(ovstart[:], ovend[:], nov[:], ALU.subtract))
                for j in range(2):
                    link(V.tensor_tensor(pick[:], hot[j][:], rank[:], ALU.mult))
                    link(V.tensor_reduce(r2[:, j, :], pick[:], AX.X, ALU.add))
                    link(V.tensor_tensor(pick[:], hot[j][:], ovstart[:].rearrange("p (o e) -> p o e", o=1)
                                         .to_broadcast([P, NT, NE]), ALU.mult))
                    link(V.tensor_reduce(ovs[:, j, :], pick[:], AX.X, ALU.add))
                link(V.tensor_scalar(isov[:], r2[:], float(CAP), None, ALU.is_ge))
                link(V.tensor_tensor(shift[:], ovs[:], eidx[:], ALU.subtract))
                link(V.tensor_scalar(shift[:], shift[:], float(BLK), float(BLK * NE - CAP), ALU.mult, ALU.add))
                link(V.tensor_tensor(shift[:], shift[:], isov[:], ALU.mult))
                link(V.scalar_tensor_tensor(out=slot[:], in0=eidx[:], scalar=float(BLK), in1=r2[:], op0=ALU.mult, op1=ALU.add))
                link(V.tensor_tensor(slot[:], slot[:], shift[:], ALU.add))
                V.tensor_copy(c.slot_of[:].rearrange("p (j t) -> p j t", j=2), slot[:]).then_inc(S["slots"], 1)
                link(V.tensor_tensor(ovcmp[:], ovend[:].rearrange("p (o e) -> p o e", o=1).to_broadcast([P, OVB, NE]),
                                     iota_e[:, 0:OVB].rearrange("p (b o) -> p b o", o=1).to_broadcast([P, OVB, NE]), ALU.is_le))
                link(V.tensor_reduce(ove_f[:], ovcmp[:], AX.X, ALU.add))
                link(V.tensor_scalar(ove_f[:], ove_f[:], float(NE - 1), None, ALU.min))
                link(V.tensor_copy(c.over_expert[:, 0:OVB], ove_f[0:1, :]))
                link(V.tensor_scalar(pairs_f[:], ovend[:, NE - 1:NE], 1.0, 0.5, ALU.add, ALU.mult))
                link(V.tensor_tensor(ovcmp[:, 0, 0:OVB // 2 + 1], pairs_f[:, 0:1].to_broadcast([P, OVB // 2 + 1]),
                                     iota_e[:, 1:OVB // 2 + 2], ALU.is_ge))
                link(V.tensor_reduce(pairs_f[:], ovcmp[:, 0, 0:OVB // 2 + 1], AX.X, ALU.add))
                link(V.tensor_copy(c.over_expert[:, OVB:OVB + 1], pairs_f[0:1, :]))
                dve.wait_ge(S["tab_in"], 16)
                V.tensor_copy(tab_f[:], tab_i[:]).then_inc(S["tab_f"], 1)
                dve.wait_ge(S["tab_turned"], 1)
                link(V.tensor_copy(c.row_tokens[:], p_tab[:, 0:NBLK + 1]))


def experts(c, nc, tag, pairs, block0, w_gate, w_up, w_down):
    dynamic = pairs is None
    UNITS = 6
    RING = 4
    ON_POOL = 4
    BY_DVE = [j for j in range(UNITS) if j != ON_POOL]
    ND = len(BY_DVE)
    U = 2048
    with ExitStack() as ctx:
        raw = [c.sb(ctx, f"{tag}_raw{j}", [P, U], F32) for j in range(UNITS)]
        wh = [c.sb(ctx, f"{tag}_wh{s}", [P, U], F32R) for s in range(RING)]
        wl = [c.sb(ctx, f"{tag}_wl{s}", [P, U], F32R) for s in range(RING)]
        xg = [c.sb(ctx, f"{tag}_xg{s}", [P, D], F32) for s in range(2)]
        xh = [c.sb(ctx, f"{tag}_xh{s}", [P, D], F32R) for s in range(2)]
        xl = [c.sb(ctx, f"{tag}_xl{s}", [P, D], F32R) for s in range(2)]
        ids = [c.sb(ctx, f"{tag}_ids{s}", [P, 1], I32) for s in range(2)]
        act_g = c.sb(ctx, tag + "_act_g", [P, DE], F32)
        hid = c.sb(ctx, tag + "_hid", [P, DE], F32)
        hh = c.sb(ctx, tag + "_hh", [P, DE], F32R)
        hl = c.sb(ctx, tag + "_hl", [P, DE], F32R)
        ys = [c.sb(ctx, f"{tag}_ys{s}", [P, D], F32) for s in range(2)]
        pg = c.ps(ctx, tag + "_pg", [P, BANK])
        pu = c.ps(ctx, tag + "_pu", [P, BANK])
        px = c.ps(ctx, tag + "_px", [P, D])
        phid = c.ps(ctx, tag + "_phid", [P, BANK])
        py = c.ps(ctx, tag + "_py", [P, D])
        S = {n: c.sem(f"{tag}_{n}") for n in ("w_hi", "lo_dve", "lo_pool", "unit_used", "x_turned", "x_hi", "x_lo",
                                              "gate_done", "up_done", "silu_done", "h_done", "h_turned", "h_hi", "h_lo",
                                              "down_done", "y_copied", "ids_ready", "passed")}
        raw_in = [c.sem(f"{tag}_raw_in{j}") for j in range(UNITS)]
        gathered = [c.sem(f"{tag}_gathered{s}") for s in range(2)]
        stored = [c.sem(f"{tag}_stored{s}") for s in range(2)]

        def rounds(eng, body, last=None):
            if not dynamic:
                body(0, True)
                with eng.Fori(1, pairs) as i:
                    body(i, False)
                if last:
                    last(pairs)
                return
            n = eng.value_load(c.over_expert[0:1, OVB:OVB + 1], min_val=0, max_val=OVB // 2)
            with eng.If(n > 0):
                body(0, True)
                with eng.If(n > 1):
                    with eng.Fori(1, n) as i:
                        body(i, False)
                with eng.Else():
                    eng.nop()
                if last:
                    last(n)
            with eng.Else():
                eng.nop()

        def done(N):
            return [N * ND + (ND + 1 + BY_DVE.index(j)) if j != ON_POOL else N + 2 for j in range(UNITS)]

        def lo_sem(j):
            return S["lo_pool"] if j == ON_POOL else S["lo_dve"]

        with nc.Block() as block:
            @block.sync
            def _(sp):
                def load(i, first):
                    for u in range(2):
                        N = i * 2 + u
                        if dynamic:
                            e = sp.value_load(c.over_expert[0:1, bass.ds(N, 1)], min_val=0, max_val=NE - 1)
                        else:
                            e = N
                        for j in range(UNITS):
                            sp.wait_ge(lo_sem(j), N * ND + (1 + BY_DVE.index(j)) if j != ON_POOL else N + 1)
                            if j < 4:
                                w = (w_gate, w_up)[j // 2]
                                half = w[0, bass.ds(e, 1), (j % 2) * D // 2:(j % 2 + 1) * D // 2, :]
                                n = DE
                            else:
                                half = w_down[0, bass.ds(e, 1), (j % 2) * DE // 2:(j % 2 + 1) * DE // 2, :]
                                n = D
                            sp.dma_start(raw[j][:].rearrange("p (k n) -> p k n", n=n),
                                         half.rearrange("o (k p) n -> p (o k) n", p=P)).then_inc(raw_in[j], 16)
                rounds(sp, load)

            @block.gpsimd
            def _(pool):
                pool.sem_inc(S["lo_pool"], 1)

                def gather(slot, column, n):
                    nc.gpsimd.tensor_copy(ids[slot][:], c.row_tokens[:, column]).then_inc(S["ids_ready"], 1)
                    wait_apart(pool, S["ids_ready"], n, S["passed"])
                    nc.gpsimd.indirect_dma_start(out=xg[slot][:], out_offset=None, in_=c.z2rows[:, :],
                                                 in_offset=bass.IndirectOffsetOnAxis(ap=ids[slot][:, 0:1], axis=0)
                                                 ).then_inc(gathered[slot], 16)

                def body(i, first):
                    for u in range(2):
                        N = i * 2 + u
                        if first and u == 0:
                            gather(0, slice(block0, block0 + 1), 1)
                        pool.wait_ge(S["x_turned"], N + 1)
                        gather(1 - u, bass.ds(N + (block0 + 1), 1), N + 2)
                        j = ON_POOL
                        s = (UNITS * u + j) % RING
                        pool.wait_ge(S["w_hi"], N * UNITS + (j + 1))
                        nc.gpsimd.tensor_tensor(wl[s][:], raw[j][:], wh[s][:].bitcast(F32),
                                                ALU.subtract).then_inc(S["lo_pool"], 1)

                def last(n):
                    pool.wait_ge(gathered[0], n * 16 + 16)
                rounds(pool, body, last)

            @block.scalar
            def _(act):
                def high(N, u, j):
                    s = (UNITS * u + j) % RING
                    act.wait_ge(raw_in[j], N * 16 + 16)
                    act.wait_ge(S["unit_used"], N * UNITS + (j + 1))
                    nc.scalar.activation(wh[s][:], raw[j][:], ACT.Copy).then_inc(S["w_hi"], 1)

                def x_high(k, slot):
                    act.wait_ge(S["x_turned"], k + 2)
                    act.wait_ge(S["up_done"], k + 1)
                    nc.scalar.activation(xh[slot][:], px[:], ACT.Copy).then_inc(S["x_hi"], 1)

                def y_out(i, u, N):
                    act.wait_ge(S["down_done"], N + 2)
                    act.wait_ge(stored[u], i * 16 + 16)
                    nc.scalar.activation(ys[u][:], py[:], ACT.Copy).then_inc(S["y_copied"], 1)
                    act.wait_ge(S["y_copied"], N + 2)
                    act.dma_start(c.yrows[bass.ds(N * BLK + block0 * BLK, BLK), :], ys[u][:]).then_inc(stored[u], 16)

                def body(i, first):
                    for u in range(2):
                        N = i * 2 + u
                        if first and u == 0:
                            x_high(0, 0)
                        high(N, u, 0)
                        high(N, u, 1)
                        if not (first and u == 0):
                            y_out(i - (1 - u), 1 - u, N - 1)
                        for j in (2, 3, 4):
                            high(N, u, j)
                        act.wait_ge(S["gate_done"], N + 1)
                        act.wait_ge(S["h_done"], N + 1)
                        nc.scalar.activation(act_g[:], pg[:], ACT.Silu).then_inc(S["silu_done"], 1)
                        high(N, u, 5)
                        x_high(N + 1, 1 - u)
                        act.wait_ge(S["h_turned"], N + 2)
                        act.wait_ge(S["down_done"], N + 1)
                        nc.scalar.activation(hh[:], phid[:], ACT.Copy).then_inc(S["h_hi"], 1)

                def last(n):
                    y_out(n - 1, 1, n * 2 - 1)
                    for u in range(2):
                        wait_apart(act, stored[u], n * 16 + 16, S["passed"])
                rounds(act, body, last)

            @block.vector
            def _(dve):
                dve.sem_inc(S["lo_dve"], ND)
                dve.sem_inc(S["x_lo"], 1)
                dve.sem_inc(S["h_done"], 1)
                dve.sem_inc(S["h_lo"], 1)
                for u in range(2):
                    dve.sem_inc(stored[u], 16)
                dve.sem_inc(S["y_copied"], 1)

                def low(N, u, j):
                    s = (UNITS * u + j) % RING
                    dve.wait_ge(S["w_hi"], N * UNITS + (j + 1))
                    nc.vector.tensor_tensor(wl[s][:], raw[j][:], wh[s][:].bitcast(F32), ALU.subtract).then_inc(S["lo_dve"], 1)

                def x_low(k, slot):
                    dve.wait_ge(S["x_hi"], k + 1)
                    nc.vector.tensor_tensor(xl[slot][:], px[:], xh[slot][:].bitcast(F32), ALU.subtract).then_inc(S["x_lo"], 1)

                def body(i, first):
                    for u in range(2):
                        N = i * 2 + u
                        if first and u == 0:
                            x_low(0, 0)
                        for j in BY_DVE:
                            low(N, u, j)
                        dve.wait_ge(S["silu_done"], N + 1)
                        dve.wait_ge(S["up_done"], N + 3)
                        dve.wait_ge(S["h_turned"], N + 1)
                        nc.vector.tensor_tensor(hid[:], act_g[:], pu[:], ALU.mult).then_inc(S["h_done"], 1)
                        x_low(N + 1, 1 - u)
                        dve.wait_ge(S["h_hi"], N + 1)
                        nc.vector.tensor_tensor(hl[:], phid[:], hh[:].bitcast(F32), ALU.subtract).then_inc(S["h_lo"], 1)
                rounds(dve, body)

            @block.tensor
            def _(pe):
                pe.sem_inc(S["unit_used"], RING)
                pe.sem_inc(S["x_turned"], 1)
                pe.sem_inc(S["up_done"], 2)
                pe.sem_inc(S["h_turned"], 1)
                pe.sem_inc(S["down_done"], 1)

                def turn_x(k, slot, arrived):
                    pe.wait_ge(gathered[slot], arrived)
                    pe.wait_ge(S["x_lo"], k + 1)
                    for t in range(KD):
                        mm = nc.tensor.transpose(px[:, t * P:(t + 1) * P], xg[slot][:, t * P:(t + 1) * P], c.ident[:])
                    mm.then_inc(S["x_turned"], 1)

                def body(i, first):
                    for u in range(2):
                        N = i * 2 + u
                        if first and u == 0:
                            turn_x(0, 0, 16)
                        ready = done(N)
                        pe.wait_ge(S["x_lo"], N + 2)
                        pe.wait_ge(S["h_done"], N + 1)
                        for j in range(4):
                            s = (UNITS * u + j) % RING
                            out = (pg, pu)[j // 2]
                            pe.wait_ge(lo_sem(j), ready[j])
                            for b in range(4):
                                k = (j % 2) * 4 + b
                                n = slice(b * DE, (b + 1) * DE)
                                mm = three_passes(nc, out[:], xh[u][:, k * P:(k + 1) * P], xl[u][:, k * P:(k + 1) * P],
                                                  wh[s][:, n], wl[s][:, n], k == 0, k == KD - 1)
                            mm.then_inc(S["unit_used"], 1)
                            if j % 2:
                                pe.wait_ge(S["unit_used"], N * UNITS + (RING + j + 1))
                                pe.sem_inc(S[("gate_done", "up_done")[j // 2]], 1)
                        turn_x(N + 1, 1 - u, i * 16 + 16 * (u + 1))
                        pe.wait_ge(S["h_done"], N + 2)
                        pe.wait_ge(S["h_lo"], N + 1)
                        for t in range(DE // P):
                            mm = nc.tensor.transpose(phid[:, t * P:(t + 1) * P], hid[:, t * P:(t + 1) * P], c.ident[:])
                        mm.then_inc(S["h_turned"], 1)
                        pe.wait_ge(S["h_lo"], N + 2)
                        pe.wait_ge(S["y_copied"], N + 1)
                        for j in (4, 5):
                            s = (UNITS * u + j) % RING
                            pe.wait_ge(lo_sem(j), ready[j])
                            for b in range(2):
                                k = (j - 4) * 2 + b
                                for half in range(2):
                                    n = slice(b * D + half * BANK, b * D + (half + 1) * BANK)
                                    mm = three_passes(nc, py[:, half * BANK:(half + 1) * BANK], hh[:, k * P:(k + 1) * P],
                                                      hl[:, k * P:(k + 1) * P], wh[s][:, n], wl[s][:, n], k == 0, k == 3)
                            mm.then_inc(S["unit_used"], 1)
                        pe.wait_ge(S["unit_used"], N * UNITS + (RING + UNITS))
                        pe.sem_inc(S["down_done"], 1)
                rounds(pe, body)


def combine(c, nc, final_norm, out):
    with ExitStack() as ctx:
        ids = [[c.sb(ctx, f"e_ids{u}{j}", [P, 1], I32) for j in range(2)] for u in range(2)]
        y = [[c.sb(ctx, f"e_y{u}{j}", [P, D], F32) for j in range(2)] for u in range(2)]
        acc = [c.sb(ctx, f"e_acc{u}", [P, D], F32) for u in range(2)]
        res = [c.sb(ctx, f"e_res{u}", [P, D], F32) for u in range(2)]
        gain = c.sb(ctx, "e_gain", [P, D], F32)
        ss, ms, rs = (c.sb(ctx, "e_" + n, [P, 2], F32) for n in ("ss", "ms", "rs"))
        S = {n: c.sem("e_" + n) for n in ("gain_in", "ids_ready", "summed", "rooted", "done", "own", "own_a", "passed")}
        y_in = [[c.sem(f"e_y_in{u}{j}") for j in range(2)] for u in range(2)]
        stored = [c.sem(f"e_stored{u}") for u in range(2)]
        flat = lambda ap: ap.rearrange("p (k t) -> p k t", k=KD)
        with nc.Block() as block:
            @block.gpsimd
            def _(pool):
                with pool.Fori(0, NT // 2) as i:
                    for u in range(2):
                        pool.wait_ge(S["summed"], i * 2 + (u + 1))
                        for j in range(2):
                            nc.gpsimd.tensor_copy(ids[u][j][:], c.slot_of[:, bass.ds(i * 2 + (u + j * NT), 1)]
                                                  ).then_inc(S["ids_ready"], 1)
                            wait_apart(pool, S["ids_ready"], i * 4 + (2 * u + j + 1), S["passed"])
                            nc.gpsimd.indirect_dma_start(out=y[u][j][:], out_offset=None, in_=c.yrows[:, :],
                                                         in_offset=bass.IndirectOffsetOnAxis(ap=ids[u][j][:, 0:1], axis=0)
                                                         ).then_inc(y_in[u][j], 16)

            @block.sync
            def _(sp):
                sp.dma_start(gain[:], final_norm[:].partition_broadcast(P)).then_inc(S["gain_in"], 16)
                with sp.Fori(0, NT // 2) as i:
                    for u in range(2):
                        sp.wait_ge(S["done"], i * 2 + (u + 1))
                        sp.dma_start(out[0, bass.ds(i * (2 * P) + u * P, P), :], res[u][:]).then_inc(stored[u], 16)
                for u in range(2):
                    sp.wait_ge(stored[u], 16 * (NT // 2 + 1))

            @block.scalar
            def _(act):
                chain = Chain(act, S["own_a"])
                with act.Fori(0, NT // 2) as i:
                    chain.enter(i, 2)
                    for u in range(2):
                        act.wait_ge(S["summed"], i * 2 + (u + 3))
                        act.wait_ge(stored[u], i * 16 + 16)
                        chain.link(nc.scalar.activation(res[u][:], acc[u][:], ACT.Square, accum_out=ss[:, u:u + 1]))
                        nc.scalar.activation(ms[:, u:u + 1], ss[:, u:u + 1], ACT.Sqrt, scale=1.0 / D,
                                             bias=c.eps[:, 0:1]).then_inc(S["rooted"], 1)
                chain.leave(NT // 2)

            @block.vector
            def _(dve):
                chain = Chain(dve, S["own"])
                dve.sem_inc(S["summed"], 2)
                for u in range(2):
                    dve.sem_inc(stored[u], 16)
                dve.wait_ge(S["gain_in"], 16)
                with dve.Fori(0, NT // 2) as i:
                    chain.enter(i, 4)
                    for u in range(2):
                        h2 = c.mx[:, :, bass.ds(i * (2 * P) + u * P, P)]
                        w = [c.weight[:, bass.ds(i * 2 + (u + j * NT), 1)] for j in range(2)]
                        for j in range(2):
                            dve.wait_ge(y_in[u][j], i * 16 + 16)
                        chain.link(nc.vector.scalar_tensor_tensor(out=flat(acc[u][:]), in0=flat(y[u][0][:]), scalar=w[0],
                                                                  in1=h2, op0=ALU.mult, op1=ALU.add))
                        nc.vector.scalar_tensor_tensor(out=acc[u][:], in0=y[u][1][:], scalar=w[1], in1=acc[u][:],
                                                       op0=ALU.mult, op1=ALU.add).then_inc(S["summed"], 1)
                    for u in range(2):
                        dve.wait_ge(S["rooted"], i * 2 + (u + 1))
                        chain.link(nc.vector.reciprocal(rs[:, u:u + 1], ms[:, u:u + 1]))
                        nc.vector.scalar_tensor_tensor(out=res[u][:], in0=acc[u][:], scalar=rs[:, u:u + 1], in1=gain[:],
                                                       op0=ALU.mult, op1=ALU.mult).then_inc(S["done"], 1)
                chain.leave(NT // 2)


def program(nc, x, meta_tokens, attn_norm, w_in, b_forget, conv_w, mix_norm, w_out, ffn_norm, w_router_group,
            b_router_group, w_router_expert, b_router_expert, w_gate, w_up, w_down, final_norm, out, debug=None):
    with ExitStack() as ctx:
        c = Core(nc)
        c.ident = c.sb(ctx, "ident", [P, P], F32)
        c.ident_bf = c.sb(ctx, "ident_bf", [P, P], BF16)
        c.maskneg = c.sb(ctx, "maskneg", [P, P], BF16)
        c.blkavg = c.sb(ctx, "blkavg", [P, P], F32)
        c.tri = c.sb(ctx, "tri", [P, P], BF16)
        c.ones_bf = c.sb(ctx, "ones_bf", [P, P], BF16)
        c.mixg = c.sb(ctx, "mixg", [P, KD], F32)
        c.eps = c.sb(ctx, "eps", [P, 1], F32)
        c.mx = c.sb(ctx, "mx", [P, KD, SEQ], F32)
        c.negcum = nc.dram_tensor("negcum", [HEADS, L], F32, kind="Internal").ap()
        with c.stage():
            constants(c, nc, mix_norm)
        with ExitStack() as zctx:
            c.zh = c.sb(zctx, "zh", [P, KD, L], F32R)
            c.zl = c.sb(zctx, "zl", [P, KD, L], F32R)
            with c.stage():
                norm_and_transpose(c, nc, x, meta_tokens, attn_norm)
            if debug == "z":
                return dump(c, nc, out, c.zh[:, :, META:].bitcast(F32))
            with c.stage():
                forget_gates(c, nc, w_in, b_forget)
            with c.stage():
                attention(c, nc, w_in)
            if debug == "attn":
                return dump(c, nc, out, c.mx[:, 0:PAIRS, :], PAIRS)
            with c.stage():
                convolution(c, nc, w_in, conv_w)
            if debug == "mix":
                return dump(c, nc, out, c.mx[:])
        c.logits = c.sb(ctx, "logits", [P, NT, NG + NE], F32)
        c.z2rows = nc.dram_tensor("z2rows", [SEQ, D], F32, kind="Internal").ap()
        with c.stage():
            output_projection(c, nc, x, w_out, ffn_norm, w_router_group, b_router_group, w_router_expert, b_router_expert)
        if debug == "h2":
            return dump(c, nc, out, c.mx[:])
        c.weight = c.sb(ctx, "weight", [P, 2 * NT], F32)
        c.slot_of = c.sb(ctx, "slot_of", [P, 2 * NT], I32)
        c.over_expert = c.sb(ctx, "over_expert", [1, OVB + 1], I32)
        c.row_tokens = c.sb(ctx, "row_tokens", [P, NBLK + 1], I32)
        c.table = nc.dram_tensor("table", [(NBLK + 1) * BLK, 1], I32, kind="Internal").ap()
        c.yrows = nc.dram_tensor("yrows", [NBLK * BLK, D], F32, kind="Internal").ap()
        with c.stage():
            route(c, nc)
        with c.stage():
            experts(c, nc, "m", NE // 2, 0, w_gate, w_up, w_down)
        with c.stage():
            experts(c, nc, "x", None, NE, w_gate, w_up, w_down)
        with c.stage():
            combine(c, nc, final_norm, out)


def dump(c, nc, out, src, n=KD):
    s = nc.alloc_semaphore(name="dump")
    with nc.Block() as block:
        @block.sync
        def _(sp):
            sp.dma_start(out[0].rearrange("(p k) t -> p k t", k=KD)[:, 0:n, :], src).then_inc(s, 16)
            sp.wait_ge(s, 16)


_INS = ["x", "meta_tokens", "attn_norm", "w_in", "b_forget", "conv_w", "mix_norm", "w_out", "ffn_norm", "w_router_group",
        "b_router_group", "w_router_expert", "b_router_expert", "w_gate", "w_up", "w_down", "final_norm"]


def kernel(**inputs):
    import numpy as _np
    import concourse.bacc as _bacc
    from concourse import mybir as _mybir
    from concourse.bass_utils import run_bass_kernel_spmd as _run

    nc = _bacc.Bacc("TRN2", target_bir_lowering=False, num_devices=1)
    arrays, args = {}, []
    for name in _INS:
        a = _np.ascontiguousarray(inputs[name])
        arrays[f"in_{name}_dram"] = a
        args.append(nc.dram_tensor(f"in_{name}_dram", a.shape, _mybir.dt.from_np(a.dtype), kind="ExternalInput").ap())
    out = nc.dram_tensor("out_0_dram", (1, SEQ, D), F32, kind="ExternalOutput").ap()
    program(nc, *args, out)
    r = _run(nc, [arrays], core_ids=[0])
    return r.results[0]["out_0_dram"]
```

```python
import concourse.bass as bass
from concourse import mybir
from contextlib import ExitStack, contextmanager

F32 = mybir.dt.float32
F32R = mybir.dt.float32r
BF16 = mybir.dt.bfloat16
I32 = mybir.dt.int32
U32 = mybir.dt.uint32
ACT = mybir.ActivationFunctionType
ALU = mybir.AluOpType
AX = mybir.AxisListType

P = 128
SEQ, META, D = 1024, 16, 1024
L = SEQ + META
NT = SEQ // P
KD = D // P
HEADS, HD = 8, 64
PAIRS = HEADS // 2
AW, CW = 512, 512
Q0, K0, V0, F0, X0, B0, C0 = 0, 512, 1024, 1536, 1544, 2056, 2568
NG, EPG, NE, DE = 4, 8, 32, 512
EPS = 1e-6
NEG = -1e30
BLK = P
CAP = BLK
OVB = 2 * SEQ // CAP
NBLK = NE + OVB
NB_LESS = SEQ // CAP
BANK = 512
CH = 348
LP = 3 * CH
CHUNKS = [(b * CH, CH) for b in range(3)]


class Chain:

    def __init__(self, eng, sem):
        self.eng, self.sem, self.base, self.n, self.off = eng, sem, 0, 0, None

    def link(self, ins):
        ins.then_inc(self.sem, 1)
        self.n += 1
        self.eng.wait_ge(self.sem, self.base + self.n if self.off is None else self.off + (self.base + self.n))

    def enter(self, i, per):
        self.base, self.n, self.off, self.per = self.base + self.n, 0, i * per, per

    def leave(self, trips):
        assert self.n == self.per, (self.n, self.per)
        self.base, self.n, self.off = self.base + trips * self.per, 0, None


def wait_apart(eng, sem, value, passed):
    eng.wait_ge(sem, value)
    eng.sem_inc(passed, 1)


class Core:

    def __init__(self, nc):
        self.nc = nc

    def sem(self, name):
        return self.sems.enter_context(self.nc.semaphore(name))

    @contextmanager
    def stage(self):
        used = []
        with ExitStack() as self.sems:
            named = self.sem
            self.sem = lambda name: used.append(named(name)) or used[-1]
            yield
            self.sem = named
            with self.nc.Block() as block:
                @block.gpsimd
                def _(pool):
                    for sem in used:
                        pool.sem_clear(sem)

    def sb(self, ctx, name, shape, dt):
        return ctx.enter_context(self.nc.sbuf_tensor(name, shape, dt))

    def ps(self, ctx, name, shape, dt=F32):
        return ctx.enter_context(self.nc.psum_tensor(name, shape, dt))


def constants(c, nc, mix_norm):
    made = c.sem("const_made")
    load = c.sem("const_load")
    steps = [
        (c.ident, 0.0), (c.maskneg, 0.0), (c.blkavg, 0.0), (c.tri, 1.0), (c.ones_bf, 1.0), (c.ident_bf, 0.0)]
    with nc.Block() as block:
        @block.sync
        def _(sp):
            for j in range(KD):
                sp.dma_start(c.mixg[:, j:j + 1], mix_norm[0, j * P:(j + 1) * P].rearrange("(p o) -> p o", o=1)).then_inc(load, 16)
            sp.wait_ge(load, 16 * KD)

        @block.gpsimd
        def _(pool):
            for buf, value in steps:
                nc.gpsimd.memset(buf[:], value).then_inc(made, 1)
            pool.wait_ge(made, len(steps))
            nc.gpsimd.affine_select(out=c.ident[:], in_=c.ident[:], compare_op=ALU.not_equal, fill=1.0, base=0,
                                    pattern=[[-1, P]], channel_multiplier=1)
            nc.gpsimd.affine_select(out=c.ident_bf[:], in_=c.ident_bf[:], compare_op=ALU.not_equal, fill=1.0, base=0,
                                    pattern=[[-1, P]], channel_multiplier=1)
            nc.gpsimd.affine_select(out=c.maskneg[:], in_=c.maskneg[:], compare_op=ALU.is_ge, fill=NEG, base=0,
                                    pattern=[[-1, P]], channel_multiplier=1)
            nc.gpsimd.affine_select(out=c.tri[:], in_=c.tri[:], compare_op=ALU.is_gt, fill=0.0, base=0,
                                    pattern=[[1, P]], channel_multiplier=-1).then_inc(made, 1)

        @block.vector
        def _(dve):
            dve.wait_ge(made, len(steps))
            nc.vector.memset(c.blkavg[0:HD, 0:HD], 1.0 / HD)
            nc.vector.memset(c.blkavg[HD:P, HD:P], 1.0 / HD)
            nc.vector.memset(c.eps[:], EPS)


def norm_and_transpose(c, nc, x, meta_tokens, attn_norm):
    with ExitStack() as ctx:
        xt = [c.sb(ctx, f"n_x{s}", [P, D], F32) for s in range(2)]
        zt = [c.sb(ctx, f"n_z{s}", [P, D], F32) for s in range(2)]
        gain = c.sb(ctx, "n_gain", [P, D], F32)
        ss = c.sb(ctx, "n_ss", [P, 2], F32)
        ms = c.sb(ctx, "n_ms", [P, 2], F32)
        rs = c.sb(ctx, "n_rs", [P, 2], F32)
        pz = [c.ps(ctx, f"n_pz{s}", [P, D]) for s in range(2)]
        gain_in = c.sem("n_gain_in")
        x_in = [c.sem(f"n_x_in{s}") for s in range(2)]
        squared, scaled, turned, hi_done, lo_done = (c.sem("n_" + n) for n in
                                                     ("squared", "scaled", "turned", "hi_done", "lo_done"))
        own_a, passed = c.sem("n_own_a"), c.sem("n_passed")
        with nc.Block() as block:
            @block.sync
            def _(sp):
                sp.dma_start(gain[:], attn_norm[0, :].partition_broadcast(P)).then_inc(gain_in, 16)
                sp.dma_start(xt[1][0:META, :], meta_tokens[:, :]).then_inc(x_in[1], 16)
                with sp.Fori(0, NT // 2) as i:
                    for u in range(2):
                        sp.wait_ge(scaled, i * 2 + (1 + u))
                        sp.dma_start(xt[u][:], x[0, bass.ds(i * (2 * P) + u * P, P), :]).then_inc(x_in[u], 16)

            @block.scalar
            def _(act):
                chain_a = Chain(act, own_a)
                link_a = chain_a.link

                def square(slot, n, m, arrived):
                    act.wait_ge(x_in[slot], arrived)
                    if n is not None:
                        act.wait_ge(turned, n)
                    link_a(nc.scalar.activation(zt[slot][0:m, :], xt[slot][0:m, :], ACT.Square,
                                                accum_out=ss[0:m, slot:slot + 1]))
                    link_a(nc.scalar.activation(ms[0:m, slot:slot + 1], ss[0:m, slot:slot + 1], ACT.Ln, scale=1.0 / D,
                                                bias=c.eps[0:m, 0:1]))
                    nc.scalar.activation(rs[0:m, slot:slot + 1], ms[0:m, slot:slot + 1], ACT.Exp, scale=-0.5).then_inc(squared, 1)

                def high(slot, n, m, col):
                    wait_apart(act, turned, n, passed)
                    nc.scalar.activation(c.zh[:, :, bass.ds(col, m)],
                                         pz[slot][:].rearrange("p (k t) -> p k t", t=P)[:, :, 0:m],
                                         ACT.Copy).then_inc(hi_done, 1)
                square(1, None, META, 16)
                high(1, 2, META, 0)
                with act.Fori(0, NT // 2) as i:
                    chain_a.enter(i, 4)
                    for u in range(2):
                        square(u, i * 2 + (1 + u), P, i * 16 + 16 * (u + 1))
                    for u in range(2):
                        high(u, i * 2 + (3 + u), P, i * (2 * P) + META + u * P)
                chain_a.leave(NT // 2)

            @block.vector
            def _(dve):
                def scale(slot, n, m):
                    dve.wait_ge(squared, n)
                    nc.vector.scalar_tensor_tensor(out=zt[slot][0:m, :], in0=xt[slot][0:m, :],
                                                   scalar=rs[0:m, slot:slot + 1], in1=gain[0:m, :],
                                                   op0=ALU.mult, op1=ALU.mult).then_inc(scaled, 1)

                def low(slot, n, m, col):
                    dve.wait_ge(hi_done, n)
                    nc.vector.tensor_tensor(c.zl[:, :, bass.ds(col, m)],
                                            pz[slot][:].rearrange("p (k t) -> p k t", t=P)[:, :, 0:m],
                                            c.zh[:, :, bass.ds(col, m)].bitcast(F32), ALU.subtract).then_inc(lo_done, 1)
                dve.sem_inc(scaled, 1)
                dve.sem_inc(lo_done, 1)
                nc.vector.memset(c.zh[:, :, L:LP].bitcast(F32), 0.0)
                nc.vector.memset(c.zl[:, :, L:LP].bitcast(F32), 0.0)
                dve.wait_ge(gain_in, 16)
                scale(1, 1, META)
                low(1, 1, META, 0)
                with dve.Fori(0, NT // 2) as i:
                    for u in range(2):
                        scale(u, i * 2 + (2 + u), P)
                    for u in range(2):
                        low(u, i * 2 + (2 + u), P, i * (2 * P) + META + u * P)

            @block.tensor
            def _(pe):
                def turn(slot, n, m):
                    pe.wait_ge(scaled, n)
                    for k in range(KD):
                        last = nc.tensor.transpose(pz[slot][:, k * P:k * P + m], zt[slot][0:m, k * P:(k + 1) * P],
                                                   c.ident[0:m, 0:m])
                    last.then_inc(turned, 1)
                pe.sem_inc(turned, 1)
                turn(1, 2, META)
                with pe.Fori(0, NT // 2) as i:
                    for u in range(2):
                        pe.wait_ge(lo_done, i * 2 + (1 + u))
                        turn(u, i * 2 + (3 + u), P)


def three_passes(nc, out, xh, xl, wh, wl, first, last):
    nc.tensor.matmul(out, xh, wh, start=first, stop=False)
    nc.tensor.matmul(out, xh, wl, start=False, stop=False)
    return nc.tensor.matmul(out, xl, wh, start=False, stop=last)


PASSES = 3 * KD


def project(nc, c, outs, wh, wl, cols, m=P, a=0, b=PASSES):
    for n_pass in range(a, b):
        k = n_pass // 3
        w, z = ((wh, c.zh), (wh, c.zl), (wl, c.zh))[n_pass % 3]
        for out, (at, n) in zip(outs, cols):
            mm = nc.tensor.matmul(out, w[:, k, 0:m], z[:, k, at:at + n], start=n_pass == 0, stop=n_pass == PASSES - 1)
    return mm


def forget_gates(c, nc, w_in, b_forget):
    with ExitStack() as ctx:
        w = c.sb(ctx, "f_w", [P, KD, HEADS], F32)
        wh = c.sb(ctx, "f_wh", [P, KD, HEADS], F32R)
        wl = c.sb(ctx, "f_wl", [P, KD, HEADS], F32R)
        bias = c.sb(ctx, "f_bias", [HEADS, 1], F32)
        y, mag, e, sp1, logf, cum, one = (c.sb(ctx, "f_" + n, [HEADS, L], F32) for n in
                                          ("y", "mag", "e", "sp1", "logf", "cum", "one"))
        pf = c.ps(ctx, "f_p", [P, 3 * BANK])
        w_ld, hi_done, lo_done, mm_done, y_done, soft_done, cum_done, stored, own, own_a = (
            c.sem("f_" + n) for n in ("w_in", "hi_done", "lo_done", "mm_done", "y_done", "soft_done", "cum_done",
                                      "stored", "own", "own_a"))
        with nc.Block() as block:
            @block.sync
            def _(sp):
                sp.dma_start(w[:], w_in[0, :, F0:F0 + HEADS].rearrange("(k p) n -> p k n", p=P)).then_inc(w_ld, 16)
                sp.dma_start(bias[:], b_forget[0, :].rearrange("(p o) -> p o", o=1)).then_inc(w_ld, 16)
                sp.wait_ge(cum_done, 1)
                sp.dma_start(c.negcum[:, :], cum[:]).then_inc(stored, 16)
                sp.wait_ge(stored, 16)

            @block.scalar
            def _(act):
                act.wait_ge(w_ld, 32)
                nc.scalar.activation(wh[:], w[:], ACT.Copy).then_inc(hi_done, 1)
                act.wait_ge(y_done, 1)
                nc.scalar.activation(mag[:], y[:], ACT.Abs).then_inc(own_a, 1)
                act.wait_ge(own_a, 1)
                nc.scalar.activation(e[:], mag[:], ACT.Exp, scale=-1.0).then_inc(own_a, 1)
                act.wait_ge(own_a, 2)
                nc.scalar.activation(sp1[:], e[:], ACT.Ln, bias=1.0).then_inc(soft_done, 1)

            @block.vector
            def _(dve):
                link = Chain(dve, own).link
                link(nc.vector.memset(one[:], 1.0))
                dve.wait_ge(w_ld, 32)
                dve.wait_ge(hi_done, 1)
                nc.vector.tensor_tensor(wl[:], w[:], wh[:].bitcast(F32), ALU.subtract).then_inc(lo_done, 1)
                dve.wait_ge(mm_done, 1)
                for b, (at, n) in enumerate((at, min(n, L - at)) for at, n in CHUNKS):
                    last = nc.vector.tensor_scalar(y[:, at:at + n], pf[0:HEADS, b * BANK:b * BANK + n], bias[:, 0:1],
                                                   None, ALU.add)
                last.then_inc(y_done, 1)
                dve.wait_ge(soft_done, 1)
                link(nc.vector.scalar_tensor_tensor(out=logf[:], in0=y[:], scalar=0.0, in1=sp1[:], op0=ALU.min,
                                                    op1=ALU.subtract))
                nc.vector.tensor_tensor_scan(cum[:], one[:], logf[:], 0.0, ALU.mult, ALU.subtract).then_inc(cum_done, 1)

            @block.tensor
            def _(pe):
                pe.wait_ge(hi_done, 1)
                pe.wait_ge(lo_done, 1)
                project(nc, c, [pf[0:HEADS, b * BANK:b * BANK + n] for b, (_, n) in enumerate(CHUNKS)], wh, wl, CHUNKS,
                        HEADS).then_inc(mm_done, 1)


def tile_groups(i):
    full = list(range(i + 1))
    groups = [full[a:a + 4] for a in range(0, i + 1, 4)]
    if i % 2:
        if len(groups[-1]) <= 2:
            groups[-1].append("meta")
        else:
            groups.append(["meta"])
    return groups


def mixers(c, nc, w_in, conv_w):
    GR = [tile_groups(i) for i in range(NT)] * 2
    STEPS = 2 * NT
    before = [sum(len(g) for g in GR[:s]) for s in range(STEPS + 1)]
    NGR = before[-1]
    NPV = STEPS // 2
    TAPS = 3
    FT = CW // P
    assert FT == PAIRS
    WT = 6
    filler = {5 * t + a: (3 + t, 5 * a, min(5 * a + 5, PASSES)) for t in range(3) for a in range(5)}
    with ExitStack() as ctx:
        raw = [c.sb(ctx, f"a_raw{s}", [P, KD, P], F32) for s in range(2)]
        wh = [c.sb(ctx, f"a_wh{t}", [P, KD, P], F32R) for t in range(2)]
        wl = [c.sb(ctx, f"a_wl{t}", [P, KD, P], F32R) for t in range(2)]
        qs = c.sb(ctx, "a_qs", [P, 2, SEQ], F32R)
        kh = c.sb(ctx, "a_kh", [P, 2, LP], F32R)
        kl = c.sb(ctx, "a_kl", [P, LP], F32R)
        v2 = c.sb(ctx, "a_v2", [P, NT + 1, 2, P], F32R)
        o = c.sb(ctx, "a_o", [P, LP], F32)
        pth = c.sb(ctx, "a_pth", [P, NT + 1, 2 * P], F32R)
        ptl = c.sb(ctx, "a_ptl", [P, NT + 1, 2 * P], F32R)
        tp = [c.sb(ctx, f"a_tp{s}", [P, L], F32) for s in range(2)]
        meta_probs = c.sb(ctx, "a_meta_probs", [P, META], F32)
        cb = c.sb(ctx, "a_cb", [P, L], F32)
        half = [c.sb(ctx, f"a_half{s}", [P, 2 * P], F32) for s in range(2)]
        top = c.sb(ctx, "a_top", [P, STEPS], F32)
        ntop = c.sb(ctx, "a_ntop", [P, STEPS], F32)
        den = c.sb(ctx, "a_den", [P, STEPS], F32)
        rden = c.sb(ctx, "a_rden", [P, STEPS], F32)
        taps = c.sb(ctx, "v_taps", [P, TAPS * FT], F32)
        u = c.sb(ctx, "v_u", [P, LP], F32)
        cv = c.sb(ctx, "v_cv", [P, LP], F32)
        s3 = c.ps(ctx, "a_s3", [P, 3 * BANK])
        pj = c.ps(ctx, "a_pj", [P, 3 * BANK])
        pt = c.ps(ctx, "a_pt", [P, BANK])
        po = c.ps(ctx, "a_po", [P, BANK])
        names = ("split_hi", "split_lo", "projected", "q_hi", "q_lo", "k_hi", "k_lo", "v_copied", "v_turned", "v_hi",
                 "v_lo", "scored", "topped", "probs", "turned", "pt_hi", "pt_lo", "pv_done", "half_copied", "o_added",
                 "rden_done", "spread", "meta_kept", "o_scaled", "squared", "averaged", "rooted", "mixed", "cb_in", "taps_in",
                 "x_copied", "u_done", "gated", "c_squared", "c_averaged", "c_rooted", "own", "own_a", "passed")
        S = {n: c.sem("a_" + n) for n in names}
        raw_in = [c.sem(f"a_raw_in{s}") for s in range(2)]

        def banks(ps):
            return [ps[:, b * BANK:b * BANK + CH] for b in range(3)]

        def in_chunks(sb):
            return sb.rearrange("p (b n) -> p b n", n=CH)

        def by_chunk(ps):
            return ps.rearrange("p (b n) -> p b n", n=BANK)[:, :, 0:CH]
        halves = [s3[:, 0:BANK], s3[:, BANK:2 * BANK]]
        q_cols = [(META, BANK), (META + BANK, BANK)]
        OUTS = [halves, banks(pj), banks(s3), banks(pj), banks(pj), [pj[:, 0:BANK], pj[:, BANK:2 * BANK]]]
        COLS = [q_cols, CHUNKS, CHUNKS, CHUNKS, CHUNKS, q_cols]
        lower, upper = slice(0, HD), slice(HD, P)
        own_half = [lower, upper]
        other_half = [upper, lower]

        def width(i):
            return META + P * (i + 1)

        with nc.Block() as block:
            @block.sync
            def _(sp):
                for t in range(TAPS):
                    for f in range(FT):
                        sp.dma_start(taps[:, t * FT + f:t * FT + f + 1],
                                     conv_w[0, t, f * P:(f + 1) * P].rearrange("(p o) -> p o", o=1)).then_inc(S["taps_in"], 16)
                with sp.Fori(0, PAIRS) as i:
                    def load(t):
                        sp.wait_ge(S["split_lo"], i * WT + (t + 1))
                        sp.dma_start(raw[t % 2][:], w_in[0, :, bass.ds(i * P + (Q0, K0, V0, X0, C0, B0)[t], P)].rearrange(
                            "(k p) n -> p k n", p=P)).then_inc(raw_in[t % 2], 16)

                    def bias(h):
                        sp.wait_ge(S["topped"], i * STEPS + (STEPS + NT * h))
                        sp.dma_start(cb[:], c.negcum[bass.ds(i * 2 + h, 1), :].partition_broadcast(P).rearrange(
                            "p o l -> p (o l)")).then_inc(S["cb_in"], 16)
                    for t in range(3):
                        load(t)
                    bias(0)
                    for t in range(3, WT):
                        load(t)
                    bias(1)

            @block.scalar
            def _(act):
                chain = Chain(act, S["own_a"])
                with act.Fori(0, PAIRS) as i:
                    chain.enter(i, 2)

                    def split(t):
                        act.wait_ge(raw_in[t % 2], i * (16 * WT // 2) + 16 * (t // 2 + 1))
                        act.wait_ge(S["projected"], i * WT + (t + 1))
                        nc.scalar.activation(wh[t % 2][:], raw[t % 2][:], ACT.Copy).then_inc(S["split_hi"], 1)

                    def projected(t):
                        act.wait_ge(S["projected"], i * WT + (t + 3))
                    split(0)
                    split(1)
                    projected(0)
                    nc.scalar.activation(qs[lower, 0, :], s3[lower, 0:SEQ], ACT.Copy, scale=HD ** -0.5)
                    nc.scalar.activation(qs[upper, 1, :], s3[upper, 0:SEQ], ACT.Copy, scale=HD ** -0.5).then_inc(S["q_hi"], 1)
                    split(2)
                    projected(1)
                    for h in range(2):
                        for to in (own_half[h], other_half[h]):
                            last = nc.scalar.activation(in_chunks(kh[to, h, :]), by_chunk(pj[own_half[h], :]), ACT.Copy)
                    last.then_inc(S["k_hi"], 1)
                    split(3)
                    projected(2)
                    act.wait_ge(S["mixed"], i + 1)
                    nc.scalar.activation(in_chunks(o[:]), by_chunk(s3[:]), ACT.Copy).then_inc(S["v_copied"], 1)
                    act.wait_ge(S["v_turned"], i + 1)
                    vt = pj[:, 0:SEQ].rearrange("p (t f) -> p t f", f=P)
                    for h in range(2):
                        f = own_half[h]
                        nc.scalar.activation(v2[:, 0:NT, h, f], vt[:, :, f], ACT.Copy)
                        last = nc.scalar.activation(v2[0:META, NT, h, f], pj[0:META, 2 * BANK + f.start:2 * BANK + f.stop],
                                                    ACT.Copy)
                    last.then_inc(S["v_hi"], 1)
                    split(4)
                    for s in range(STEPS + 2):
                        if s == 5:
                            projected(3)
                            nc.scalar.activation(in_chunks(cv[:]), by_chunk(pj[:]), ACT.Copy).then_inc(S["x_copied"], 1)
                            split(5)
                        if s >= 3 and s % 2 == 1:
                            g = (s - 3) // 2
                            h = g // (NPV // 2)
                            act.wait_ge(S["pv_done"], i * NPV + (g + 1))
                            nc.scalar.activation(half[g % 2][own_half[h], :],
                                                 po[other_half[h], 0:2 * P],
                                                 ACT.Copy).then_inc(S["half_copied"], 1)
                        if s < STEPS:
                            w = width(s % NT)
                            act.wait_ge(S["topped"], i * STEPS + (STEPS + s + 1))
                            nc.scalar.activation(tp[s % 2][:, 0:w], tp[s % 2][:, 0:w], ACT.Exp, bias=ntop[:, s:s + 1],
                                                 accum_out=den[:, s:s + 1]).then_inc(S["probs"], 1)
                        if 1 <= s <= STEPS:
                            r = s - 1
                            if r % 2 == 0 and r >= 2:
                                act.wait_ge(S["pv_done"], i * NPV + r // 2)
                            for a, group in enumerate(GR[r]):
                                n = before[r] + a
                                act.wait_ge(S["turned"], i * NGR + (n + 1))
                                cols = slice((r % 2) * P, (r % 2) * P + P)
                                tiles = [kt for kt in group if kt != "meta"]
                                if tiles:
                                    ins = nc.scalar.activation(
                                        pth[:, tiles[0]:tiles[-1] + 1, cols],
                                        pt[:, 0:len(tiles) * P].rearrange("p (t q) -> p t q", q=P), ACT.Copy)
                                if "meta" in group:
                                    at = len(tiles) * P
                                    ins = nc.scalar.activation(pth[0:META, NT, :], pt[0:META, at:at + 2 * P], ACT.Copy)
                                ins.then_inc(S["pt_hi"], 1)
                        if s == STEPS:
                            act.wait_ge(S["gated"], i + 1)
                            nc.scalar.activation(u[:, 0:SEQ], cv[:, 0:SEQ], ACT.Square).then_inc(S["c_squared"], 1)
                    act.wait_ge(S["c_averaged"], i + 1)
                    chain.link(nc.scalar.activation(u[:, 0:SEQ], pj[:, 0:SEQ], ACT.Ln, bias=c.eps[:, 0:1]))
                    nc.scalar.activation(u[:, 0:SEQ], u[:, 0:SEQ], ACT.Exp, scale=-0.5).then_inc(S["c_rooted"], 1)
                    act.wait_ge(S["o_scaled"], i + 1)
                    nc.scalar.activation(tp[0][:, 0:SEQ], o[:, 0:SEQ], ACT.Square).then_inc(S["squared"], 1)
                    act.wait_ge(S["averaged"], i + 1)
                    chain.link(nc.scalar.activation(tp[1][:, 0:SEQ], s3[:, 0:SEQ], ACT.Ln, bias=c.eps[:, 0:1]))
                    nc.scalar.activation(tp[1][:, 0:SEQ], tp[1][:, 0:SEQ], ACT.Exp, scale=-0.5).then_inc(S["rooted"], 1)
                chain.leave(PAIRS)

            @block.vector
            def _(dve):
                chain = Chain(dve, S["own"])
                link = chain.link
                dve.sem_inc(S["split_lo"], 2)
                dve.sem_inc(S["topped"], STEPS)
                dve.sem_inc(S["o_added"], 1)
                dve.sem_inc(S["mixed"], 1)
                dve.wait_ge(S["taps_in"], 16 * TAPS * FT)
                with dve.Fori(0, PAIRS) as i:
                    chain.enter(i, STEPS + 5)

                    def split(t):
                        dve.wait_ge(S["split_hi"], i * WT + (t + 1))
                        nc.vector.tensor_tensor(wl[t % 2][:], raw[t % 2][:], wh[t % 2][:].bitcast(F32),
                                                ALU.subtract).then_inc(S["split_lo"], 1)
                    split(0)
                    split(1)
                    dve.wait_ge(S["q_hi"], i + 1)
                    nc.vector.scalar_tensor_tensor(out=qs[upper, 0, :], in0=s3[lower, 0:SEQ], scalar=HD ** -0.5,
                                                   in1=qs[lower, 0, :].bitcast(F32), op0=ALU.mult, op1=ALU.subtract)
                    nc.vector.scalar_tensor_tensor(out=qs[lower, 1, :], in0=s3[upper, 0:SEQ], scalar=HD ** -0.5,
                                                   in1=qs[upper, 1, :].bitcast(F32), op0=ALU.mult,
                                                   op1=ALU.subtract).then_inc(S["q_lo"], 1)
                    split(2)
                    dve.wait_ge(S["k_hi"], i + 1)
                    for h in range(2):
                        f = own_half[h]
                        last = nc.vector.tensor_tensor(in_chunks(kl[f, :]), by_chunk(pj[f, :]),
                                                       in_chunks(kh[f, h, :]).bitcast(F32), ALU.subtract)
                    last.then_inc(S["k_lo"], 1)
                    split(3)
                    dve.wait_ge(S["v_hi"], i + 1)
                    vt = pj[:, 0:SEQ].rearrange("p (t f) -> p t f", f=P)
                    for h in range(2):
                        f, g = own_half[h], other_half[h]
                        nc.vector.tensor_tensor(v2[:, 0:NT, h, g], vt[:, :, f], v2[:, 0:NT, h, f].bitcast(F32),
                                                ALU.subtract)
                        last = nc.vector.tensor_tensor(v2[0:META, NT, h, g],
                                                       pj[0:META, 2 * BANK + f.start:2 * BANK + f.stop],
                                                       v2[0:META, NT, h, f].bitcast(F32), ALU.subtract)
                    last.then_inc(S["v_lo"], 1)
                    split(4)
                    for s in range(STEPS + 2):
                        if s >= 2 and s <= STEPS:
                            dve.wait_ge(S["turned"], i * NGR + before[s - 1])
                            if s % 2 == 0:
                                nc.vector.tensor_copy(meta_probs[:], tp[0][:, 0:META]).then_inc(S["meta_kept"], 1)
                        if s < STEPS:
                            h, w = s // NT, width(s % NT)
                            dve.wait_ge(S["scored"], i * STEPS + (s + 1))
                            if s % NT == 0:
                                dve.wait_ge(S["cb_in"], i * 32 + (16 * h + 16))
                            if s % 2 == 0 and s >= 2:
                                dve.wait_ge(S["meta_kept"], i * NPV + s // 2)
                            dve.sem_inc(S["passed"], 1)
                            link(nc.vector.tensor_tensor_reduce(tp[s % 2][:, 0:w], s3[:, 0:w], cb[:, 0:w], 1.0, NEG,
                                                                ALU.add, ALU.max, top[:, s:s + 1]))
                            nc.vector.tensor_scalar(ntop[:, s:s + 1], top[:, s:s + 1], -1.0, None,
                                                    ALU.mult).then_inc(S["topped"], 1)
                        if s == 10:
                            dve.wait_ge(S["x_copied"], i + 1)
                            dve.wait_ge(S["projected"], i * WT + 7)
                            nc.vector.tensor_tensor(in_chunks(u[:]), in_chunks(cv[:]), by_chunk(pj[:]),
                                                    ALU.mult).then_inc(S["u_done"], 1)
                        if s >= 3 and s % 2 == 1:
                            g = (s - 3) // 2
                            f = own_half[g // (NPV // 2)]
                            at = (g % (NPV // 2)) * 2 * P
                            dve.wait_ge(S["half_copied"], i * NPV + (g + 1))
                            nc.vector.tensor_tensor(o[f, at:at + 2 * P], po[f, 0:2 * P],
                                                    half[g % 2][f, :], ALU.add).then_inc(S["o_added"], 1)
                        if 1 <= s <= STEPS:
                            r = s - 1
                            for a, group in enumerate(GR[r]):
                                n = before[r] + a
                                dve.wait_ge(S["pt_hi"], i * NGR + (n + 1))
                                cols = slice((r % 2) * P, (r % 2) * P + P)
                                tiles = [kt for kt in group if kt != "meta"]
                                if tiles:
                                    kt = slice(tiles[0], tiles[-1] + 1)
                                    ins = nc.vector.tensor_tensor(
                                        ptl[:, kt, cols], pt[:, 0:len(tiles) * P].rearrange("p (t q) -> p t q", q=P),
                                        pth[:, kt, cols].bitcast(F32), ALU.subtract)
                                if "meta" in group:
                                    at = len(tiles) * P
                                    ins = nc.vector.tensor_tensor(ptl[0:META, NT, :], pt[0:META, at:at + 2 * P],
                                                                  pth[0:META, NT, :].bitcast(F32), ALU.subtract)
                                ins.then_inc(S["pt_lo"], 1)
                        if s == 6:
                            split(5)
                        if s in (11, 12, 13):
                            t = s - 11
                            src = u[:, META - (TAPS - 1) + t:META - (TAPS - 1) + t + SEQ]
                            w = taps[:, bass.ds(i + t * FT, 1)]
                            if t == 0:
                                dve.wait_ge(S["u_done"], i + 1)
                                link(nc.vector.tensor_scalar(cv[:, 0:SEQ], src, w, None, ALU.mult))
                            else:
                                link(nc.vector.scalar_tensor_tensor(out=cv[:, 0:SEQ], in0=src, scalar=w,
                                                                    in1=cv[:, 0:SEQ], op0=ALU.mult, op1=ALU.add))
                        if s == 15:
                            dve.wait_ge(S["projected"], i * WT + 8)
                            nc.vector.tensor_tensor(cv[:, 0:SEQ], cv[:, 0:SEQ], pj[:, 0:SEQ], ALU.mult).then_inc(S["gated"], 1)
                    dve.wait_ge(S["probs"], i * STEPS + STEPS)
                    link(nc.vector.reciprocal(rden[:], den[:]))
                    dve.wait_ge(S["turned"], i * NGR + NGR)
                    nc.vector.tensor_copy(tp[0][:, 0:SEQ].rearrange("p (t h f) -> p t h f", t=NT, h=2),
                                          rden[:].rearrange("p (h t o) -> p t h o", h=2, o=1).to_broadcast(
                                              [P, NT, 2, HD])).then_inc(S["rden_done"], 1)

                    def mix(value, root, col):
                        nc_ins = nc.vector.scalar_tensor_tensor(
                            out=c.mx[:, bass.ds(i + col, 1), :].rearrange("p o t -> p (o t)"), in0=value[:, 0:SEQ],
                            scalar=c.mixg[:, bass.ds(i + col, 1)], in1=root[:, 0:SEQ], op0=ALU.mult, op1=ALU.mult)
                        return nc_ins
                    dve.wait_ge(S["spread"], i + 1)
                    dve.wait_ge(S["o_added"], i * NPV + (NPV + 1))
                    nc.vector.tensor_tensor(o[:, 0:SEQ], o[:, 0:SEQ], s3[:, 0:SEQ], ALU.mult).then_inc(S["o_scaled"], 1)
                    dve.wait_ge(S["c_rooted"], i + 1)
                    link(mix(cv, u, PAIRS))
                    dve.wait_ge(S["rooted"], i + 1)
                    mix(o, tp[1], 0).then_inc(S["mixed"], 1)
                chain.leave(PAIRS)

            @block.tensor
            def _(pe):
                pe.sem_inc(S["projected"], 2)

                def scores(s):
                    h, q = s // NT, s % NT
                    ps, w, f = s3, width(q), own_half[h]
                    pieces = [(a, min(BANK, w - a)) for a in range(0, w, BANK)]
                    for at, n in pieces:
                        nc.tensor.matmul(ps[:, at:at + n], qs[:, h, q * P:(q + 1) * P], kh[:, h, at:at + n],
                                         start=True, stop=False)
                        mm = nc.tensor.matmul(ps[:, at:at + n], qs[f, h, q * P:(q + 1) * P], kl[f, at:at + n],
                                              start=False, stop=True)
                        a = max(at, w - P)
                        if a < at + n:
                            mm = nc.tensor.matmul(ps[:, a:at + n], c.ident_bf[:], c.maskneg[:, a - (w - P):at + n - (w - P)],
                                                  start=False, stop=True, skip_group_check=True)
                    mm.then_inc(S["scored"], 1)

                with pe.Fori(0, PAIRS) as i:
                    def tile(t, a=0, b=PASSES):
                        if a == 0:
                            pe.wait_ge(S["split_lo"], i * WT + (t + 3))
                        mm = project(nc, c, OUTS[t], wh[t % 2], wl[t % 2], COLS[t], a=a, b=b)
                        if b == PASSES:
                            mm.then_inc(S["projected"], 1)

                    def filler_parts(s):
                        if s not in filler:
                            return [None] * 3
                        t, a, b = filler[s]
                        n = len(GR[s - 1]) if s >= 1 else 1
                        cuts = [a, a + 1, a + 3, b] if n >= 2 else [a, a + 2, b, b]
                        return [(t, x, y) if x < y else None for x, y in zip(cuts, cuts[1:])]

                    def fill(part):
                        if part:
                            t, a, b = part
                            if a == 0:
                                pe.wait_ge(S[("v_lo", "x_copied", "u_done")[t - 3]], i + 1)
                            tile(t, a, b)
                    pe.wait_ge(S["mixed"], i + 1)
                    tile(0)
                    tile(1)
                    pe.wait_ge(S["q_lo"], i + 1)
                    tile(2)
                    for name in ("v_copied", "k_lo"):
                        pe.wait_ge(S[name], i + 1)
                    for t in range(NT):
                        nc.tensor.transpose(pj[:, t * P:(t + 1) * P], o[:, META + t * P:META + (t + 1) * P], c.ident[:])
                    nc.tensor.transpose(pj[0:META, 2 * BANK:2 * BANK + P], o[:, 0:META], c.ident[:]).then_inc(S["v_turned"], 1)
                    for s in range(STEPS + 2):
                        if s < STEPS:
                            if s >= 1:
                                pe.wait_ge(S["topped"], i * STEPS + (STEPS + s))
                            scores(s)
                        parts = filler_parts(s)
                        fill(parts[0])
                        if s >= 3 and s % 2 == 1:
                            g = (s - 3) // 2
                            h, ga = g // (NPV // 2), g % (NPV // 2)
                            pe.wait_ge(S["pt_lo"], i * NGR + before[2 * g + 2])
                            pe.wait_ge(S["o_added"], i * NPV + (g + 1))
                            out = po[:, 0:2 * P]
                            for kt in range(2 * ga + 2):
                                a = P if kt == 2 * ga + 1 else 0
                                for probs in (pth, ptl):
                                    nc.tensor.matmul(out[:, a:2 * P], v2[:, kt, h, :], probs[:, kt, a:2 * P],
                                                     start=kt == 0 and probs is pth, stop=False, skip_group_check=True)
                            nc.tensor.matmul(out, v2[0:META, NT, h, :], pth[0:META, NT, :], start=False, stop=False,
                                             skip_group_check=True)
                            nc.tensor.matmul(out, v2[0:META, NT, h, :], ptl[0:META, NT, :], start=False, stop=True,
                                             skip_group_check=True).then_inc(S["pv_done"], 1)
                        if 1 <= s <= STEPS:
                            r = s - 1
                            pe.wait_ge(S["probs"], i * STEPS + (r + 1))
                            for a, group in enumerate(GR[r]):
                                n = before[r] + a
                                if n >= 1:
                                    pe.wait_ge(S["pt_lo"], i * NGR + n)
                                at = 0
                                for kt in group:
                                    if kt == "meta":
                                        pe.wait_ge(S["meta_kept"], i * NPV + (r + 1) // 2)
                                        for b, probs in enumerate((meta_probs[:], tp[1][:, 0:META])):
                                            mm = nc.tensor.transpose(pt[0:META, at + b * P:at + (b + 1) * P],
                                                                     probs, c.ident[:])
                                    else:
                                        mm = nc.tensor.transpose(pt[:, at:at + P],
                                                                 tp[r % 2][:, META + kt * P:META + (kt + 1) * P],
                                                                 c.ident[:])
                                    at += P
                                mm.then_inc(S["turned"], 1)
                                fill(parts[1 + a] if a < 2 else None)
                        else:
                            fill(parts[1])
                            fill(parts[2])

                    def average(out, sq, done):
                        for b in range(2):
                            mm = nc.tensor.matmul(out[:, b * BANK:(b + 1) * BANK], c.blkavg[:], sq[:, b * BANK:(b + 1) * BANK],
                                                  start=True, stop=True)
                        mm.then_inc(S[done], 1)
                    pe.wait_ge(S["rden_done"], i + 1)
                    for t in range(NT):
                        mm = nc.tensor.transpose(s3[:, t * P:(t + 1) * P], tp[0][:, t * P:(t + 1) * P], c.ident[:])
                    mm.then_inc(S["spread"], 1)
                    pe.wait_ge(S["c_squared"], i + 1)
                    average(pj, u, "c_averaged")
                    pe.wait_ge(S["squared"], i + 1)
                    average(s3, tp[0], "averaged")


def output_projection(c, nc, x, w_out, ffn_norm, w_rg, b_rg, w_re, b_re):
    NR = NG + NE
    with ExitStack() as ctx:
        raw = [c.sb(ctx, f"o_raw{s}", [P, D], F32) for s in range(2)]
        wh = c.sb(ctx, "o_wh", [P, KD, D], F32R)
        wl = c.sb(ctx, "o_wl", [P, KD, D], F32R)
        mh = [c.sb(ctx, f"o_mh{s}", [P, KD, P], F32R) for s in range(2)]
        ml = [c.sb(ctx, f"o_ml{s}", [P, KD, P], F32R) for s in range(2)]
        xt = [c.sb(ctx, f"o_x{s}", [P, D], F32) for s in range(2)]
        z2 = [c.sb(ctx, f"o_z2{s}", [P, D], F32) for s in range(2)]
        z2t = [c.sb(ctx, f"o_z2t{s}", [P, D], F32) for s in range(2)]
        gain = c.sb(ctx, "o_gain", [P, D], F32)
        blank = c.sb(ctx, "o_blank", [P, D], F32)
        no_token = c.sb(ctx, "o_no_token", [NBLK + 1, BLK], I32)
        wr = c.sb(ctx, "o_wr", [P, KD, NR], F32)
        br = c.sb(ctx, "o_br", [P, NR], F32)
        ss, ms, rs = (c.sb(ctx, "o_" + n, [P, 2], F32) for n in ("ss", "ms", "rs"))
        ph = [c.ps(ctx, f"o_ph{s}", [P, D]) for s in range(2)]
        pz = c.ps(ctx, "o_pz", [P, D])
        pl = c.ps(ctx, "o_pl", [P, BANK])
        S = {n: c.sem("o_" + n) for n in ("w_hi", "w_lo", "m_hi", "m_lo", "multiplied", "h2_done", "squared", "z2_done",
                                          "turned", "t_copied", "logits", "logits_out", "blanked", "blank_out", "own_a", "passed")}
        raw_in = [c.sem(f"o_raw_in{s}") for s in range(2)]
        x_in = [c.sem(f"o_x_in{s}") for s in range(2)]
        stored = [c.sem(f"o_stored{s}") for s in range(2)]
        small_in = c.sem("o_small_in")

        def mix_tile(i, n):
            return c.mx[:, :, bass.ds(i * (2 * P) + n * P, P)]

        def three(buf):
            return buf[:].rearrange("p (k t) -> p k t", k=KD)

        ROUNDS = NT // 2

        with nc.Block() as block:
            @block.sync
            def _(sp):
                def weights(k):
                    if k >= 2:
                        sp.wait_ge(S["w_lo"], k - 1)
                    sp.dma_start(raw[k % 2][:], w_out[0, k * P:(k + 1) * P, :]).then_inc(raw_in[k % 2], 16)
                for k in range(2):
                    weights(k)
                for n in range(2):
                    sp.dma_start(xt[n][:], x[0, n * P:(n + 1) * P, :]).then_inc(x_in[n], 16)
                for k in range(2, KD):
                    weights(k)
                sp.dma_start(gain[:], ffn_norm[0, :].partition_broadcast(P)).then_inc(small_in, 16)
                sp.dma_start(wr[:, :, 0:NG], w_rg[0].rearrange("(k p) n -> p k n", p=P)).then_inc(small_in, 16)
                sp.dma_start(wr[:, :, NG:NR], w_re[0].rearrange("(k p) n -> p k n", p=P)).then_inc(small_in, 16)
                sp.dma_start(br[:, 0:NG], b_rg[0, :].partition_broadcast(P)).then_inc(small_in, 16)
                sp.dma_start(br[:, NG:NR], b_re[0, :].partition_broadcast(P)).then_inc(small_in, 16)

                def step(i, n, ahead):
                    if ahead:
                        sp.wait_ge(S["h2_done"], i * 2 + (n + 1))
                        sp.dma_start(xt[n][:], x[0, bass.ds(i * (2 * P) + (n + 2) * P, P), :]).then_inc(x_in[n], 16)
                    sp.wait_ge(S["z2_done"], i * 2 + (n + 1))
                    sp.dma_start(c.z2rows[bass.ds(i * (2 * P) + n * P, P), :], z2[n][:]).then_inc(stored[n], 16)
                with sp.Fori(0, ROUNDS - 1) as i:
                    for n in range(2):
                        step(i, n, True)
                for n in range(2):
                    step(ROUNDS - 1, n, False)
                for n in range(2):
                    sp.wait_ge(stored[n], 16 * (ROUNDS + 1))

            @block.gpsimd
            def _(pool):
                nc.gpsimd.memset(no_token[:], 0).then_inc(S["blanked"], 1)
                nc.gpsimd.memset(blank[:], 0.0).then_inc(S["blanked"], 1)
                pool.wait_ge(S["blanked"], 2)
                pool.dma_start(c.table[:, :].rearrange("(b r) o -> b (r o)", r=BLK), no_token[:]).then_inc(S["blank_out"], 16)
                for b in range(NE, NBLK):
                    pool.dma_start(c.yrows[b * BLK:(b + 1) * BLK, :], blank[:]).then_inc(S["blank_out"], 16)
                pool.wait_ge(S["blank_out"], 16 * (1 + OVB))

            @block.scalar
            def _(act):
                chain = Chain(act, S["own_a"])

                def mix_high(i, n):
                    wait_apart(act, S["multiplied"], i * 2 + (n + 1), S["passed"])
                    nc.scalar.activation(mh[n % 2][:], mix_tile(i, n), ACT.Copy).then_inc(S["m_hi"], 1)

                def step(i, n, ahead):
                    act.wait_ge(S["h2_done"], i * 2 + (n + 1))
                    act.wait_ge(stored[n], i * 16 + 16)
                    wait_apart(act, S["turned"], i * 2 + (n + 1), S["passed"])
                    chain.link(nc.scalar.activation(three(z2[n]), mix_tile(i, n), ACT.Square, accum_out=ss[:, n:n + 1]))
                    chain.link(nc.scalar.activation(ms[:, n:n + 1], ss[:, n:n + 1], ACT.Ln, scale=1.0 / D,
                                                    bias=c.eps[:, 0:1]))
                    nc.scalar.activation(rs[:, n:n + 1], ms[:, n:n + 1], ACT.Exp, scale=-0.5).then_inc(S["squared"], 1)
                    if ahead:
                        mix_high(i, n + 2)
                    act.wait_ge(S["turned"], i * 2 + (n + 3))
                    act.wait_ge(S["logits"], i * 2 + (n + 1))
                    nc.scalar.activation(z2t[n][:], pz[:], ACT.Copy).then_inc(S["t_copied"], 1)
                for n in range(2):
                    mix_high(0, n)
                for k in range(KD):
                    act.wait_ge(raw_in[k % 2], 16 * (k // 2 + 1))
                    nc.scalar.activation(wh[:, k, :], raw[k % 2][:], ACT.Copy).then_inc(S["w_hi"], 1)
                with act.Fori(0, ROUNDS - 1) as i:
                    chain.enter(i, 4)
                    for n in range(2):
                        step(i, n, True)
                chain.leave(ROUNDS - 1)
                for n in range(2):
                    step(ROUNDS - 1, n, False)

            @block.vector
            def _(dve):
                for n in range(2):
                    dve.sem_inc(stored[n], 16)

                def mix_low(i, n):
                    dve.wait_ge(S["m_hi"], i * 2 + (n + 1))
                    nc.vector.tensor_tensor(ml[n % 2][:], mix_tile(i, n), mh[n % 2][:].bitcast(F32),
                                            ALU.subtract).then_inc(S["m_lo"], 1)

                def step(i, n, ahead):
                    dve.wait_ge(S["multiplied"], i * 2 + (n + 3))
                    dve.wait_ge(x_in[n], i * 16 + 16)
                    nc.vector.tensor_tensor(mix_tile(i, n), three(xt[n]), three(ph[n]), ALU.add).then_inc(S["h2_done"], 1)
                    if ahead:
                        mix_low(i, n + 2)
                    dve.wait_ge(S["squared"], i * 2 + (n + 1))
                    nc.vector.scalar_tensor_tensor(out=three(z2[n]), in0=mix_tile(i, n), scalar=rs[:, n:n + 1],
                                                   in1=three(gain), op0=ALU.mult, op1=ALU.mult).then_inc(S["z2_done"], 1)
                    dve.wait_ge(S["logits"], i * 2 + (n + 3))
                    nc.vector.tensor_tensor(c.logits[:, bass.ds(i * 2 + n, 1), :].rearrange("p o n -> p (o n)"),
                                            pl[:, n * P:n * P + NR], br[:], ALU.add).then_inc(S["logits_out"], 1)
                for n in range(2):
                    mix_low(0, n)
                for k in range(KD):
                    dve.wait_ge(S["w_hi"], k + 1)
                    nc.vector.tensor_tensor(wl[:, k, :], raw[k % 2][:], wh[:, k, :].bitcast(F32),
                                            ALU.subtract).then_inc(S["w_lo"], 1)
                dve.wait_ge(small_in, 16 * 5)
                with dve.Fori(0, ROUNDS - 1) as i:
                    for n in range(2):
                        step(i, n, True)
                for n in range(2):
                    step(ROUNDS - 1, n, False)

            @block.tensor
            def _(pe):
                pe.sem_inc(S["multiplied"], 2)
                pe.sem_inc(S["turned"], 2)
                pe.sem_inc(S["logits"], 2)

                def product(u, k, b):
                    n = slice(b * BANK, (b + 1) * BANK)
                    return three_passes(nc, ph[u][:, n], mh[u][:, k, :], ml[u][:, k, :], wh[:, k, n], wl[:, k, n],
                                        k == 0, k == KD - 1)

                def step(i, n, ahead):
                    u = (n + 1) % 2
                    if ahead:
                        pe.wait_ge(S["m_lo"], i * 2 + (n + 2))
                        pe.wait_ge(S["h2_done"], i * 2 + n)
                        for k in range(KD):
                            product(u, k, 0)
                    pe.wait_ge(S["z2_done"], i * 2 + (n + 1))
                    pe.wait_ge(S["t_copied"], i * 2 + (n + 1))
                    for k in range(KD):
                        mm = nc.tensor.transpose(pz[:, k * P:(k + 1) * P], z2[n][:, k * P:(k + 1) * P], c.ident[:])
                    mm.then_inc(S["turned"], 1)
                    if ahead:
                        for k in range(KD):
                            mm = product(u, k, 1)
                        mm.then_inc(S["multiplied"], 1)
                    pe.wait_ge(S["t_copied"], i * 2 + (n + 2))
                    pe.wait_ge(S["logits_out"], i * 2 + (n + 1))
                    for k in range(KD):
                        mm = nc.tensor.matmul(pl[:, n * P:n * P + NR], z2t[n][:, k * P:(k + 1) * P], wr[:, k, :],
                                              start=k == 0, stop=k == KD - 1)
                    mm.then_inc(S["logits"], 1)
                pe.sem_inc(S["t_copied"], 1)
                pe.sem_inc(S["logits_out"], 1)
                pe.wait_ge(S["m_lo"], 1)
                for k in range(KD):
                    pe.wait_ge(S["w_lo"], k + 1)
                    for b in range(2):
                        mm = product(0, k, b)
                mm.then_inc(S["multiplied"], 1)
                with pe.Fori(0, ROUNDS - 1) as i:
                    for n in range(2):
                        step(i, n, True)
                step(ROUNDS - 1, 0, True)
                step(ROUNDS - 1, 1, False)


def route(c, nc):
    with ExitStack() as ctx:
        f = lambda name, shape, dt=F32: c.sb(ctx, "r_" + name, shape, dt)
        iota_i = f("iota_i", [P, NE], I32)
        iota_e = f("iota_e", [P, NE])
        token = f("token", [P, NT], I32)
        limits_i, limits = f("limits_i", [P, NB_LESS], I32), f("limits", [P, NB_LESS])
        gmax, gsum, gw, gi = (f(n, [P, NT]) for n in ("gmax", "gsum", "gw", "gi"))
        gd, geq, goh, pen = (f(n, [P, NT, NG]) for n in ("gd", "geq", "goh", "pen"))
        masked = [f(f"masked{j}", [P, NT, NE]) for j in range(2)]
        eq = f("eq", [P, NT, NE])
        hot = [f(f"hot{j}", [P, NT, NE]) for j in range(2)]
        both = f("both", [P, NT, NE], BF16)
        emax = [f(f"emax{j}", [P, NT]) for j in range(2)]
        eidx = f("eidx", [P, 2, NT])
        ediff, eexp, eden = (f(n, [P, NT]) for n in ("ediff", "eexp", "eden"))
        rank = f("rank", [P, NT, NE])
        run = f("run", [P, NT + 1, NE])
        over = f("over", [P, NE, NB_LESS])
        nov, ovend, ovstart, onee = (f(n, [P, NE]) for n in ("nov", "ovend", "ovstart", "onee"))
        pick = f("pick", [P, NT, NE])
        r2, ovs, isov, shift = (f(n, [P, 2, NT]) for n in ("r2", "ovs", "isov", "shift"))
        slot = f("slot", [P, 2, NT])
        ovcmp = f("ovcmp", [P, OVB, NE])
        ove_f = f("ove_f", [P, OVB])
        pairs_f = f("pairs_f", [P, 1])
        tab_i, tab_f = f("tab_i", [NBLK + 1, BLK], I32), f("tab_f", [NBLK + 1, BLK])
        p_in = c.ps(ctx, "r_in", [P, BANK])
        p_tot = c.ps(ctx, "r_tot", [P, BANK])
        p_tab = c.ps(ctx, "r_tab", [P, BANK])
        S = {n: c.sem("r_" + n) for n in ("made", "g_ready", "g_exp", "e_ready", "e_exp", "marked", "counted",
                                          "slots", "scattered", "tab_in", "tab_f", "tab_turned", "own")}
        tile4 = lambda ap: ap.rearrange("p t (g e) -> p t g e", e=EPG)
        with nc.Block() as block:
            @block.gpsimd
            def _(pool):
                nc.gpsimd.iota(iota_i[:], pattern=[[1, NE]], base=0, channel_multiplier=0)
                nc.gpsimd.iota(limits_i[:], pattern=[[CAP, NB_LESS]], base=CAP, channel_multiplier=0)
                nc.gpsimd.iota(token[:], pattern=[[P, NT]], base=0, channel_multiplier=1).then_inc(S["made"], 1)
                pool.wait_ge(S["made"], 1)
                pool.wait_ge(S["slots"], 1)
                for j in range(2):
                    for t in range(NT):
                        nc.gpsimd.indirect_dma_start(
                            out=c.table[:, :], out_offset=bass.IndirectOffsetOnAxis(ap=c.slot_of[:, j * NT + t:j * NT + t + 1],
                                                                                    axis=0),
                            in_=token[:, t:t + 1], in_offset=None).then_inc(S["scattered"], 16)

            @block.sync
            def _(sp):
                sp.wait_ge(S["scattered"], 16 * 2 * NT)
                sp.dma_start(tab_i[:], c.table[:, :].rearrange("(b r) o -> b (r o)", r=BLK)).then_inc(S["tab_in"], 16)
                sp.wait_ge(S["tab_in"], 16)

            @block.scalar
            def _(act):
                act.wait_ge(S["g_ready"], 1)
                nc.scalar.activation(gd[:], gd[:], ACT.Exp).then_inc(S["g_exp"], 1)
                act.wait_ge(S["e_ready"], 1)
                nc.scalar.activation(eexp[:], ediff[:], ACT.Exp).then_inc(S["e_exp"], 1)

            @block.tensor
            def _(pe):
                pe.wait_ge(S["marked"], 1)
                nc.tensor.matmul(p_in[:, 0:NT * NE], c.tri[:], both[:].rearrange("p t e -> p (t e)"), start=True, stop=True)
                nc.tensor.matmul(p_tot[:, 0:NT * NE], c.ones_bf[:], both[:].rearrange("p t e -> p (t e)"), start=True,
                                 stop=True).then_inc(S["counted"], 1)
                pe.wait_ge(S["tab_f"], 1)
                nc.tensor.transpose(p_tab[:, 0:NBLK + 1], tab_f[:], c.ident[0:NBLK + 1, 0:NBLK + 1]).then_inc(S["tab_turned"], 1)

            @block.vector
            def _(dve):
                link = Chain(dve, S["own"]).link
                V = nc.vector
                dve.wait_ge(S["made"], 1)
                link(V.tensor_copy(iota_e[:], iota_i[:]))
                link(V.tensor_copy(limits[:], limits_i[:]))
                lg, le = c.logits[:, :, 0:NG], c.logits[:, :, NG:NG + NE]
                wide = lambda ap, n: ap.rearrange("p (t o) -> p t o", o=1).to_broadcast([P, NT, n])
                ids = lambda n: iota_e[:, 0:n].rearrange("p (o e) -> p o e", o=1).to_broadcast([P, NT, n])

                def first_of_max(values, top, eq, index, hot, n):
                    link(V.tensor_reduce(top, values, AX.X, ALU.max))
                    link(V.tensor_tensor(eq, values, wide(top, n), ALU.is_equal))
                    link(V.tensor_scalar(eq, eq, -float(n), float(n), ALU.mult, ALU.add))
                    link(V.tensor_tensor(eq, eq, ids(n), ALU.add))
                    link(V.tensor_reduce(index, eq, AX.X, ALU.min))
                    link(V.tensor_tensor(hot, ids(n), wide(index, n), ALU.is_equal))
                first_of_max(lg, gmax[:], geq[:], gi[:], goh[:], NG)
                V.tensor_tensor(gd[:], lg, wide(gmax[:], NG), ALU.subtract).then_inc(S["g_ready"], 1)
                link(V.tensor_scalar(pen[:], goh[:], -NEG, NEG, ALU.mult, ALU.add))
                link(V.tensor_tensor(tile4(masked[0][:]), tile4(le), pen[:].rearrange("p t (g o) -> p t g o", o=1)
                                     .to_broadcast([P, NT, NG, EPG]), ALU.add))
                first_of_max(masked[0][:], emax[0][:], eq[:], eidx[:, 0, :], hot[0][:], NE)
                link(V.scalar_tensor_tensor(out=masked[1][:], in0=hot[0][:], scalar=2 * NEG, in1=masked[0][:],
                                            op0=ALU.mult, op1=ALU.add))
                first_of_max(masked[1][:], emax[1][:], eq[:], eidx[:, 1, :], hot[1][:], NE)
                V.tensor_tensor(ediff[:], emax[1][:], emax[0][:], ALU.subtract).then_inc(S["e_ready"], 1)
                V.tensor_tensor(both[:], hot[0][:], hot[1][:], ALU.add).then_inc(S["marked"], 1)
                dve.wait_ge(S["g_exp"], 1)
                link(V.tensor_reduce(gsum[:], gd[:], AX.X, ALU.add))
                link(V.reciprocal(gw[:], gsum[:]))
                dve.wait_ge(S["e_exp"], 1)
                link(V.tensor_scalar(eden[:], eexp[:], 1.0, None, ALU.add))
                link(V.reciprocal(eden[:], eden[:]))
                link(V.tensor_tensor(c.weight[:, 0:NT], gw[:], eden[:], ALU.mult))
                link(V.tensor_tensor(c.weight[:, NT:2 * NT], c.weight[:, 0:NT], eexp[:], ALU.mult))
                dve.wait_ge(S["counted"], 1)
                link(V.memset(run[:, 0, :], 0.0))
                for t in range(NT):
                    link(V.tensor_tensor(run[:, t + 1, :], run[:, t, :], p_tot[:, t * NE:(t + 1) * NE], ALU.add))
                link(V.tensor_tensor(rank[:], run[:, 0:NT, :], p_in[:, 0:NT * NE].rearrange("p (t e) -> p t e", e=NE), ALU.add))
                link(V.tensor_tensor(over[:], run[:, NT, :].rearrange("p (e o) -> p e o", o=1).to_broadcast([P, NE, NB_LESS]),
                                     limits[:].rearrange("p (o b) -> p o b", o=1).to_broadcast([P, NE, NB_LESS]), ALU.is_gt))
                link(V.tensor_reduce(nov[:], over[:], AX.X, ALU.add))
                link(V.memset(onee[:], 1.0))
                link(V.tensor_tensor_scan(ovend[:], onee[:], nov[:], 0.0, ALU.mult, ALU.add))
                link(V.tensor_tensor(ovstart[:], ovend[:], nov[:], ALU.subtract))
                for j in range(2):
                    link(V.tensor_tensor(pick[:], hot[j][:], rank[:], ALU.mult))
                    link(V.tensor_reduce(r2[:, j, :], pick[:], AX.X, ALU.add))
                    link(V.tensor_tensor(pick[:], hot[j][:], ovstart[:].rearrange("p (o e) -> p o e", o=1)
                                         .to_broadcast([P, NT, NE]), ALU.mult))
                    link(V.tensor_reduce(ovs[:, j, :], pick[:], AX.X, ALU.add))
                link(V.tensor_scalar(isov[:], r2[:], float(CAP), None, ALU.is_ge))
                link(V.tensor_tensor(shift[:], ovs[:], eidx[:], ALU.subtract))
                link(V.tensor_scalar(shift[:], shift[:], float(BLK), float(BLK * NE - CAP), ALU.mult, ALU.add))
                link(V.tensor_tensor(shift[:], shift[:], isov[:], ALU.mult))
                link(V.scalar_tensor_tensor(out=slot[:], in0=eidx[:], scalar=float(BLK), in1=r2[:], op0=ALU.mult, op1=ALU.add))
                link(V.tensor_tensor(slot[:], slot[:], shift[:], ALU.add))
                V.tensor_copy(c.slot_of[:].rearrange("p (j t) -> p j t", j=2), slot[:]).then_inc(S["slots"], 1)
                link(V.tensor_tensor(ovcmp[:], ovend[:].rearrange("p (o e) -> p o e", o=1).to_broadcast([P, OVB, NE]),
                                     iota_e[:, 0:OVB].rearrange("p (b o) -> p b o", o=1).to_broadcast([P, OVB, NE]), ALU.is_le))
                link(V.tensor_reduce(ove_f[:], ovcmp[:], AX.X, ALU.add))
                link(V.tensor_scalar(ove_f[:], ove_f[:], float(NE - 1), None, ALU.min))
                link(V.tensor_copy(c.over_expert[:, 0:OVB], ove_f[0:1, :]))
                link(V.tensor_scalar(pairs_f[:], ovend[:, NE - 1:NE], 1.0, 0.5, ALU.add, ALU.mult))
                link(V.tensor_tensor(ovcmp[:, 0, 0:OVB // 2 + 1], pairs_f[:, 0:1].to_broadcast([P, OVB // 2 + 1]),
                                     iota_e[:, 1:OVB // 2 + 2], ALU.is_ge))
                link(V.tensor_reduce(pairs_f[:], ovcmp[:, 0, 0:OVB // 2 + 1], AX.X, ALU.add))
                link(V.tensor_copy(c.over_expert[:, OVB:OVB + 1], pairs_f[0:1, :]))
                dve.wait_ge(S["tab_in"], 16)
                V.tensor_copy(tab_f[:], tab_i[:]).then_inc(S["tab_f"], 1)
                dve.wait_ge(S["tab_turned"], 1)
                link(V.tensor_copy(c.row_tokens[:], p_tab[:, 0:NBLK + 1]))


def experts(c, nc, tag, pairs, block0, w_gate, w_up, w_down):
    dynamic = pairs is None
    UNITS = 6
    RING = 4
    ON_POOL = 4
    BY_DVE = [j for j in range(UNITS) if j != ON_POOL]
    ND = len(BY_DVE)
    U = 2048
    with ExitStack() as ctx:
        raw = [c.sb(ctx, f"{tag}_raw{j}", [P, U], F32) for j in range(UNITS)]
        wh = [c.sb(ctx, f"{tag}_wh{s}", [P, U], F32R) for s in range(RING)]
        wl = [c.sb(ctx, f"{tag}_wl{s}", [P, U], F32R) for s in range(RING)]
        xg = [c.sb(ctx, f"{tag}_xg{s}", [P, D], F32) for s in range(2)]
        xh = [c.sb(ctx, f"{tag}_xh{s}", [P, D], F32R) for s in range(2)]
        xl = [c.sb(ctx, f"{tag}_xl{s}", [P, D], F32R) for s in range(2)]
        ids = [c.sb(ctx, f"{tag}_ids{s}", [P, 1], I32) for s in range(2)]
        act_g = c.sb(ctx, tag + "_act_g", [P, DE], F32)
        hid = c.sb(ctx, tag + "_hid", [P, DE], F32)
        hh = c.sb(ctx, tag + "_hh", [P, DE], F32R)
        hl = c.sb(ctx, tag + "_hl", [P, DE], F32R)
        ys = [c.sb(ctx, f"{tag}_ys{s}", [P, D], F32) for s in range(2)]
        pg = c.ps(ctx, tag + "_pg", [P, BANK])
        pu = c.ps(ctx, tag + "_pu", [P, BANK])
        px = c.ps(ctx, tag + "_px", [P, D])
        phid = c.ps(ctx, tag + "_phid", [P, BANK])
        py = c.ps(ctx, tag + "_py", [P, D])
        S = {n: c.sem(f"{tag}_{n}") for n in ("w_hi", "lo_dve", "lo_pool", "unit_used", "x_turned", "x_hi", "x_lo",
                                              "gate_done", "up_done", "silu_done", "h_done", "h_turned", "h_hi", "h_lo",
                                              "down_done", "y_copied", "ids_ready", "passed")}
        raw_in = [c.sem(f"{tag}_raw_in{j}") for j in range(UNITS)]
        gathered = [c.sem(f"{tag}_gathered{s}") for s in range(2)]
        stored = [c.sem(f"{tag}_stored{s}") for s in range(2)]

        def rounds(eng, body, last=None):
            if not dynamic:
                body(0, True)
                with eng.Fori(1, pairs) as i:
                    body(i, False)
                if last:
                    last(pairs)
                return
            n = eng.value_load(c.over_expert[0:1, OVB:OVB + 1], min_val=0, max_val=OVB // 2)
            with eng.If(n > 0):
                body(0, True)
                with eng.If(n > 1):
                    with eng.Fori(1, n) as i:
                        body(i, False)
                with eng.Else():
                    eng.nop()
                if last:
                    last(n)
            with eng.Else():
                eng.nop()

        def done(N):
            return [N * ND + (ND + 1 + BY_DVE.index(j)) if j != ON_POOL else N + 2 for j in range(UNITS)]

        def lo_sem(j):
            return S["lo_pool"] if j == ON_POOL else S["lo_dve"]

        with nc.Block() as block:
            @block.sync
            def _(sp):
                def load(i, first):
                    for u in range(2):
                        N = i * 2 + u
                        if dynamic:
                            e = sp.value_load(c.over_expert[0:1, bass.ds(N, 1)], min_val=0, max_val=NE - 1)
                        else:
                            e = N
                        for j in range(UNITS):
                            sp.wait_ge(lo_sem(j), N * ND + (1 + BY_DVE.index(j)) if j != ON_POOL else N + 1)
                            if j < 4:
                                w = (w_gate, w_up)[j // 2]
                                half = w[0, bass.ds(e, 1), (j % 2) * D // 2:(j % 2 + 1) * D // 2, :]
                                n = DE
                            else:
                                half = w_down[0, bass.ds(e, 1), (j % 2) * DE // 2:(j % 2 + 1) * DE // 2, :]
                                n = D
                            sp.dma_start(raw[j][:].rearrange("p (k n) -> p k n", n=n),
                                         half.rearrange("o (k p) n -> p (o k) n", p=P)).then_inc(raw_in[j], 16)
                rounds(sp, load)

            @block.gpsimd
            def _(pool):
                pool.sem_inc(S["lo_pool"], 1)

                def gather(slot, column, n):
                    nc.gpsimd.tensor_copy(ids[slot][:], c.row_tokens[:, column]).then_inc(S["ids_ready"], 1)
                    wait_apart(pool, S["ids_ready"], n, S["passed"])
                    nc.gpsimd.indirect_dma_start(out=xg[slot][:], out_offset=None, in_=c.z2rows[:, :],
                                                 in_offset=bass.IndirectOffsetOnAxis(ap=ids[slot][:, 0:1], axis=0)
                                                 ).then_inc(gathered[slot], 16)

                def body(i, first):
                    for u in range(2):
                        N = i * 2 + u
                        if first and u == 0:
                            gather(0, slice(block0, block0 + 1), 1)
                        pool.wait_ge(S["x_turned"], N + 1)
                        gather(1 - u, bass.ds(N + (block0 + 1), 1), N + 2)
                        j = ON_POOL
                        s = (UNITS * u + j) % RING
                        pool.wait_ge(S["w_hi"], N * UNITS + (j + 1))
                        nc.gpsimd.tensor_tensor(wl[s][:], raw[j][:], wh[s][:].bitcast(F32),
                                                ALU.subtract).then_inc(S["lo_pool"], 1)

                def last(n):
                    pool.wait_ge(gathered[0], n * 16 + 16)
                rounds(pool, body, last)

            @block.scalar
            def _(act):
                def high(N, u, j):
                    s = (UNITS * u + j) % RING
                    act.wait_ge(raw_in[j], N * 16 + 16)
                    act.wait_ge(S["unit_used"], N * UNITS + (j + 1))
                    nc.scalar.activation(wh[s][:], raw[j][:], ACT.Copy).then_inc(S["w_hi"], 1)

                def x_high(k, slot):
                    act.wait_ge(S["x_turned"], k + 2)
                    act.wait_ge(S["up_done"], k + 1)
                    nc.scalar.activation(xh[slot][:], px[:], ACT.Copy).then_inc(S["x_hi"], 1)

                def y_out(i, u, N):
                    act.wait_ge(S["down_done"], N + 2)
                    act.wait_ge(stored[u], i * 16 + 16)
                    nc.scalar.activation(ys[u][:], py[:], ACT.Copy).then_inc(S["y_copied"], 1)
                    act.wait_ge(S["y_copied"], N + 2)
                    act.dma_start(c.yrows[bass.ds(N * BLK + block0 * BLK, BLK), :], ys[u][:]).then_inc(stored[u], 16)

                def body(i, first):
                    for u in range(2):
                        N = i * 2 + u
                        if first and u == 0:
                            x_high(0, 0)
                        high(N, u, 0)
                        high(N, u, 1)
                        if not (first and u == 0):
                            y_out(i - (1 - u), 1 - u, N - 1)
                        for j in (2, 3, 4):
                            high(N, u, j)
                        act.wait_ge(S["gate_done"], N + 1)
                        act.wait_ge(S["h_done"], N + 1)
                        nc.scalar.activation(act_g[:], pg[:], ACT.Silu).then_inc(S["silu_done"], 1)
                        high(N, u, 5)
                        x_high(N + 1, 1 - u)
                        act.wait_ge(S["h_turned"], N + 2)
                        act.wait_ge(S["down_done"], N + 1)
                        nc.scalar.activation(hh[:], phid[:], ACT.Copy).then_inc(S["h_hi"], 1)

                def last(n):
                    y_out(n - 1, 1, n * 2 - 1)
                    for u in range(2):
                        wait_apart(act, stored[u], n * 16 + 16, S["passed"])
                rounds(act, body, last)

            @block.vector
            def _(dve):
                dve.sem_inc(S["lo_dve"], ND)
                dve.sem_inc(S["x_lo"], 1)
                dve.sem_inc(S["h_done"], 1)
                dve.sem_inc(S["h_lo"], 1)
                for u in range(2):
                    dve.sem_inc(stored[u], 16)
                dve.sem_inc(S["y_copied"], 1)

                def low(N, u, j):
                    s = (UNITS * u + j) % RING
                    dve.wait_ge(S["w_hi"], N * UNITS + (j + 1))
                    nc.vector.tensor_tensor(wl[s][:], raw[j][:], wh[s][:].bitcast(F32), ALU.subtract).then_inc(S["lo_dve"], 1)

                def x_low(k, slot):
                    dve.wait_ge(S["x_hi"], k + 1)
                    nc.vector.tensor_tensor(xl[slot][:], px[:], xh[slot][:].bitcast(F32), ALU.subtract).then_inc(S["x_lo"], 1)

                def body(i, first):
                    for u in range(2):
                        N = i * 2 + u
                        if first and u == 0:
                            x_low(0, 0)
                        for j in BY_DVE:
                            low(N, u, j)
                        dve.wait_ge(S["silu_done"], N + 1)
                        dve.wait_ge(S["up_done"], N + 3)
                        dve.wait_ge(S["h_turned"], N + 1)
                        nc.vector.tensor_tensor(hid[:], act_g[:], pu[:], ALU.mult).then_inc(S["h_done"], 1)
                        x_low(N + 1, 1 - u)
                        dve.wait_ge(S["h_hi"], N + 1)
                        nc.vector.tensor_tensor(hl[:], phid[:], hh[:].bitcast(F32), ALU.subtract).then_inc(S["h_lo"], 1)
                rounds(dve, body)

            @block.tensor
            def _(pe):
                pe.sem_inc(S["unit_used"], RING)
                pe.sem_inc(S["x_turned"], 1)
                pe.sem_inc(S["up_done"], 2)
                pe.sem_inc(S["h_turned"], 1)
                pe.sem_inc(S["down_done"], 1)

                def turn_x(k, slot, arrived):
                    pe.wait_ge(gathered[slot], arrived)
                    pe.wait_ge(S["x_lo"], k + 1)
                    for t in range(KD):
                        mm = nc.tensor.transpose(px[:, t * P:(t + 1) * P], xg[slot][:, t * P:(t + 1) * P], c.ident[:])
                    mm.then_inc(S["x_turned"], 1)

                def body(i, first):
                    for u in range(2):
                        N = i * 2 + u
                        if first and u == 0:
                            turn_x(0, 0, 16)
                        ready = done(N)
                        pe.wait_ge(S["x_lo"], N + 2)
                        pe.wait_ge(S["h_done"], N + 1)
                        for j in range(4):
                            s = (UNITS * u + j) % RING
                            out = (pg, pu)[j // 2]
                            pe.wait_ge(lo_sem(j), ready[j])
                            for b in range(4):
                                k = (j % 2) * 4 + b
                                n = slice(b * DE, (b + 1) * DE)
                                mm = three_passes(nc, out[:], xh[u][:, k * P:(k + 1) * P], xl[u][:, k * P:(k + 1) * P],
                                                  wh[s][:, n], wl[s][:, n], k == 0, k == KD - 1)
                            mm.then_inc(S["unit_used"], 1)
                            if j % 2:
                                pe.wait_ge(S["unit_used"], N * UNITS + (RING + j + 1))
                                pe.sem_inc(S[("gate_done", "up_done")[j // 2]], 1)
                        turn_x(N + 1, 1 - u, i * 16 + 16 * (u + 1))
                        pe.wait_ge(S["h_done"], N + 2)
                        pe.wait_ge(S["h_lo"], N + 1)
                        for t in range(DE // P):
                            mm = nc.tensor.transpose(phid[:, t * P:(t + 1) * P], hid[:, t * P:(t + 1) * P], c.ident[:])
                        mm.then_inc(S["h_turned"], 1)
                        pe.wait_ge(S["h_lo"], N + 2)
                        pe.wait_ge(S["y_copied"], N + 1)
                        for j in (4, 5):
                            s = (UNITS * u + j) % RING
                            pe.wait_ge(lo_sem(j), ready[j])
                            for b in range(2):
                                k = (j - 4) * 2 + b
                                for half in range(2):
                                    n = slice(b * D + half * BANK, b * D + (half + 1) * BANK)
                                    mm = three_passes(nc, py[:, half * BANK:(half + 1) * BANK], hh[:, k * P:(k + 1) * P],
                                                      hl[:, k * P:(k + 1) * P], wh[s][:, n], wl[s][:, n], k == 0, k == 3)
                            mm.then_inc(S["unit_used"], 1)
                        pe.wait_ge(S["unit_used"], N * UNITS + (RING + UNITS))
                        pe.sem_inc(S["down_done"], 1)
                rounds(pe, body)


def combine(c, nc, final_norm, out):
    U = 4
    with ExitStack() as ctx:
        ids = [[c.sb(ctx, f"e_ids{u}{j}", [P, 1], I32) for j in range(2)] for u in range(U)]
        y = [[c.sb(ctx, f"e_y{u}{j}", [P, D], F32) for j in range(2)] for u in range(U)]
        acc = [c.sb(ctx, f"e_acc{u}", [P, D], F32) for u in range(U)]
        res = [c.sb(ctx, f"e_res{u}", [P, D], F32) for u in range(U)]
        gain = c.sb(ctx, "e_gain", [P, D], F32)
        ss, ms, rs = (c.sb(ctx, "e_" + n, [P, U], F32) for n in ("ss", "ms", "rs"))
        S = {n: c.sem("e_" + n) for n in ("gain_in", "ids_ready", "summed", "rooted", "done", "own", "own_a", "passed")}
        y_in = [[c.sem(f"e_y_in{u}{j}") for j in range(2)] for u in range(U)]
        stored = [c.sem(f"e_stored{u}") for u in range(U)]
        flat = lambda ap: ap.rearrange("p (k t) -> p k t", k=KD)
        with nc.Block() as block:
            @block.gpsimd
            def _(pool):
                with pool.Fori(0, NT // U) as i:
                    for u in range(U):
                        pool.wait_ge(S["summed"], i * U + (u + 1))
                        for j in range(2):
                            nc.gpsimd.tensor_copy(ids[u][j][:], c.slot_of[:, bass.ds(i * U + (u + j * NT), 1)]
                                                  ).then_inc(S["ids_ready"], 1)
                            wait_apart(pool, S["ids_ready"], i * (2 * U) + (2 * u + j + 1), S["passed"])
                            nc.gpsimd.indirect_dma_start(out=y[u][j][:], out_offset=None, in_=c.yrows[:, :],
                                                         in_offset=bass.IndirectOffsetOnAxis(ap=ids[u][j][:, 0:1], axis=0)
                                                         ).then_inc(y_in[u][j], 16)

            @block.sync
            def _(sp):
                sp.dma_start(gain[:], final_norm[:].partition_broadcast(P)).then_inc(S["gain_in"], 16)
                with sp.Fori(0, NT // U) as i:
                    for u in range(U):
                        sp.wait_ge(S["done"], i * U + (U + u + 1))
                        sp.dma_start(out[0, bass.ds(i * (U * P) + u * P, P), :], res[u][:]).then_inc(stored[u], 16)
                for u in range(U):
                    sp.wait_ge(stored[u], 16 * (NT // U + 1))

            @block.scalar
            def _(act):
                chain = Chain(act, S["own_a"])
                with act.Fori(0, NT // U) as i:
                    chain.enter(i, 2 * U)
                    for u in range(U):
                        act.wait_ge(S["summed"], i * U + (U + u + 1))
                        act.wait_ge(stored[u], i * 16 + 16)
                        chain.link(nc.scalar.activation(res[u][:], acc[u][:], ACT.Square, accum_out=ss[:, u:u + 1]))
                        chain.link(nc.scalar.activation(ms[:, u:u + 1], ss[:, u:u + 1], ACT.Ln, scale=1.0 / D,
                                                        bias=c.eps[:, 0:1]))
                        nc.scalar.activation(rs[:, u:u + 1], ms[:, u:u + 1], ACT.Exp, scale=-0.5).then_inc(S["rooted"], 1)
                chain.leave(NT // U)

            @block.vector
            def _(dve):
                chain = Chain(dve, S["own"])
                dve.sem_inc(S["summed"], U)
                dve.sem_inc(S["done"], U)
                for u in range(U):
                    dve.sem_inc(stored[u], 16)
                dve.wait_ge(S["gain_in"], 16)

                def finish(i, u):
                    dve.wait_ge(S["rooted"], i * U + (u + 1))
                    nc.vector.scalar_tensor_tensor(out=res[u][:], in0=acc[u][:], scalar=rs[:, u:u + 1], in1=gain[:],
                                                   op0=ALU.mult, op1=ALU.mult).then_inc(S["done"], 1)
                with dve.Fori(0, NT // U) as i:
                    chain.enter(i, U)
                    for u in range(U):
                        h2 = c.mx[:, :, bass.ds(i * (U * P) + u * P, P)]
                        w = [c.weight[:, bass.ds(i * U + (u + j * NT), 1)] for j in range(2)]
                        for j in range(2):
                            dve.wait_ge(y_in[u][j], i * 16 + 16)
                        dve.wait_ge(S["done"], i * U + (u + 1))
                        chain.link(nc.vector.scalar_tensor_tensor(out=flat(acc[u][:]), in0=flat(y[u][0][:]), scalar=w[0],
                                                                  in1=h2, op0=ALU.mult, op1=ALU.add))
                        nc.vector.scalar_tensor_tensor(out=acc[u][:], in0=y[u][1][:], scalar=w[1], in1=acc[u][:],
                                                       op0=ALU.mult, op1=ALU.add).then_inc(S["summed"], 1)
                        if u >= 1:
                            finish(i, u - 1)
                    finish(i, U - 1)
                chain.leave(NT // U)


def program(nc, x, meta_tokens, attn_norm, w_in, b_forget, conv_w, mix_norm, w_out, ffn_norm, w_router_group,
            b_router_group, w_router_expert, b_router_expert, w_gate, w_up, w_down, final_norm, out, debug=None):
    with ExitStack() as ctx:
        c = Core(nc)
        c.ident = c.sb(ctx, "ident", [P, P], F32)
        c.ident_bf = c.sb(ctx, "ident_bf", [P, P], BF16)
        c.maskneg = c.sb(ctx, "maskneg", [P, P], BF16)
        c.blkavg = c.sb(ctx, "blkavg", [P, P], F32)
        c.tri = c.sb(ctx, "tri", [P, P], BF16)
        c.ones_bf = c.sb(ctx, "ones_bf", [P, P], BF16)
        c.mixg = c.sb(ctx, "mixg", [P, KD], F32)
        c.eps = c.sb(ctx, "eps", [P, 1], F32)
        c.mx = c.sb(ctx, "mx", [P, KD, SEQ], F32)
        c.negcum = nc.dram_tensor("negcum", [HEADS, L], F32, kind="Internal").ap()
        with c.stage():
            constants(c, nc, mix_norm)
        with ExitStack() as zctx:
            c.zh = c.sb(zctx, "zh", [P, KD, LP], F32R)
            c.zl = c.sb(zctx, "zl", [P, KD, LP], F32R)
            with c.stage():
                norm_and_transpose(c, nc, x, meta_tokens, attn_norm)
            if debug == "z":
                return dump(c, nc, out, c.zh[:, :, META:L].bitcast(F32))
            with c.stage():
                forget_gates(c, nc, w_in, b_forget)
            with c.stage():
                mixers(c, nc, w_in, conv_w)
            if debug == "mix":
                return dump(c, nc, out, c.mx[:])
        c.logits = c.sb(ctx, "logits", [P, NT, NG + NE], F32)
        c.z2rows = nc.dram_tensor("z2rows", [SEQ, D], F32, kind="Internal").ap()
        c.table = nc.dram_tensor("table", [(NBLK + 1) * BLK, 1], I32, kind="Internal").ap()
        c.yrows = nc.dram_tensor("yrows", [NBLK * BLK, D], F32, kind="Internal").ap()
        with c.stage():
            output_projection(c, nc, x, w_out, ffn_norm, w_router_group, b_router_group, w_router_expert, b_router_expert)
        if debug == "h2":
            return dump(c, nc, out, c.mx[:])
        c.weight = c.sb(ctx, "weight", [P, 2 * NT], F32)
        c.slot_of = c.sb(ctx, "slot_of", [P, 2 * NT], I32)
        c.over_expert = c.sb(ctx, "over_expert", [1, OVB + 1], I32)
        c.row_tokens = c.sb(ctx, "row_tokens", [P, NBLK + 1], I32)
        with c.stage():
            route(c, nc)
        with c.stage():
            experts(c, nc, "m", NE // 2, 0, w_gate, w_up, w_down)
        with c.stage():
            experts(c, nc, "x", None, NE, w_gate, w_up, w_down)
        with c.stage():
            combine(c, nc, final_norm, out)


def dump(c, nc, out, src, n=KD):
    s = nc.alloc_semaphore(name="dump")
    with nc.Block() as block:
        @block.sync
        def _(sp):
            sp.dma_start(out[0].rearrange("(p k) t -> p k t", k=KD)[:, 0:n, :], src).then_inc(s, 16)
            sp.wait_ge(s, 16)


_INS = ["x", "meta_tokens", "attn_norm", "w_in", "b_forget", "conv_w", "mix_norm", "w_out", "ffn_norm", "w_router_group",
        "b_router_group", "w_router_expert", "b_router_expert", "w_gate", "w_up", "w_down", "final_norm"]


def kernel(**inputs):
    import numpy as _np
    import concourse.bacc as _bacc
    from concourse import mybir as _mybir
    from concourse.bass_utils import run_bass_kernel_spmd as _run

    nc = _bacc.Bacc("TRN2", target_bir_lowering=False, num_devices=1)
    arrays, args = {}, []
    for name in _INS:
        a = _np.ascontiguousarray(inputs[name])
        arrays[f"in_{name}_dram"] = a
        args.append(nc.dram_tensor(f"in_{name}_dram", a.shape, _mybir.dt.from_np(a.dtype), kind="ExternalInput").ap())
    out = nc.dram_tensor("out_0_dram", (1, SEQ, D), F32, kind="ExternalOutput").ap()
    program(nc, *args, out)
    r = _run(nc, [arrays], core_ids=[0])
    return r.results[0]["out_0_dram"]
```

```python
import concourse.bass as bass
from concourse import mybir
from contextlib import ExitStack, contextmanager

F32 = mybir.dt.float32
F32R = mybir.dt.float32r
BF16 = mybir.dt.bfloat16
I32 = mybir.dt.int32
ACT = mybir.ActivationFunctionType
ALU = mybir.AluOpType
AX = mybir.AxisListType

P = 128
SEQ, META, D = 1024, 16, 1024
L = SEQ + META
NT = SEQ // P
KD = D // P
HEADS, HD = 8, 64
PAIRS = HEADS // 2
AW, CW = 512, 512
Q0, K0, V0, F0, X0, B0, C0 = 0, 512, 1024, 1536, 1544, 2056, 2568
NG, EPG, NE, DE = 4, 8, 32, 512
EPS = 1e-6
NEG = -1e30
LN_AND_EXP = "natural_log_exp_and_others"
BLK = 96
OVB = 2 * SEQ // BLK // 2 * 2 + 2
NBLK = NE + OVB
UNITS, UNIT = 6, 2048
NB_LESS = SEQ // BLK
BANK = 512
CH = 348
LP = 3 * CH
CHUNKS = [(b * CH, CH) for b in range(3)]


class Chain:

    def __init__(self, eng, sem):
        self.eng, self.sem, self.base, self.n, self.off = eng, sem, 0, 0, None

    def link(self, ins):
        ins.then_inc(self.sem, 1)
        self.n += 1
        self.eng.wait_ge(self.sem, self.base + self.n if self.off is None else self.off + (self.base + self.n))

    def enter(self, i, per):
        self.base, self.n, self.off, self.per = self.base + self.n, 0, i * per, per

    def leave(self, trips):
        assert self.n == self.per, (self.n, self.per)
        self.base, self.n, self.off = self.base + trips * self.per, 0, None


def wait_apart(eng, sem, value, passed):
    eng.wait_ge(sem, value)
    eng.sem_inc(passed, 1)


class Core:

    def __init__(self, nc, ctx):
        self.nc, self.ctx = nc, ctx

    def sem(self, name):
        return self.sems.enter_context(self.nc.semaphore(name))

    def lasting_sem(self, name):
        return self.ctx.enter_context(self.nc.semaphore(name))

    @contextmanager
    def semaphores(self):
        used = []
        with ExitStack() as self.sems:
            named = self.sem
            self.sem = lambda name: used.append(named(name)) or used[-1]
            yield
            self.sem = named
            with self.nc.Block() as block:
                @block.gpsimd
                def _(pool):
                    for sem in used:
                        pool.sem_clear(sem)

    def sb(self, ctx, name, shape, dt):
        return ctx.enter_context(self.nc.sbuf_tensor(name, shape, dt))

    def ps(self, ctx, name, shape, dt=F32):
        return ctx.enter_context(self.nc.psum_tensor(name, shape, dt))


def constants(c, nc, mix_norm):
    made = c.sem("const_made")
    load = c.sem("const_load")
    steps = [
        (c.ident, 0.0), (c.maskneg, 0.0), (c.blkavg, 0.0), (c.tri, 1.0), (c.ones_bf, 1.0), (c.ident_bf, 0.0)]
    with nc.Block() as block:
        @block.sync
        def _(sp):
            for j in range(KD):
                sp.dma_start(c.mixg[:, j:j + 1], mix_norm[0, j * P:(j + 1) * P].rearrange("(p o) -> p o", o=1)).then_inc(load, 16)
            sp.wait_ge(load, 16 * KD)

        @block.gpsimd
        def _(pool):
            for buf, value in steps:
                nc.gpsimd.memset(buf[:], value).then_inc(made, 1)
            pool.wait_ge(made, len(steps))
            nc.gpsimd.affine_select(out=c.ident[:], in_=c.ident[:], compare_op=ALU.not_equal, fill=1.0, base=0,
                                    pattern=[[-1, P]], channel_multiplier=1)
            nc.gpsimd.affine_select(out=c.ident_bf[:], in_=c.ident_bf[:], compare_op=ALU.not_equal, fill=1.0, base=0,
                                    pattern=[[-1, P]], channel_multiplier=1)
            nc.gpsimd.affine_select(out=c.maskneg[:], in_=c.maskneg[:], compare_op=ALU.is_ge, fill=NEG, base=0,
                                    pattern=[[-1, P]], channel_multiplier=1)
            nc.gpsimd.affine_select(out=c.tri[:], in_=c.tri[:], compare_op=ALU.is_gt, fill=0.0, base=0,
                                    pattern=[[1, P]], channel_multiplier=-1).then_inc(made, 1)

        @block.vector
        def _(dve):
            dve.wait_ge(made, len(steps))
            nc.vector.memset(c.blkavg[0:HD, 0:HD], 1.0 / HD)
            nc.vector.memset(c.blkavg[HD:P, HD:P], 1.0 / HD)
            nc.vector.memset(c.eps[:], EPS)


def norm_and_transpose(c, nc, x, meta_tokens, attn_norm):
    with ExitStack() as ctx:
        xt = [c.sb(ctx, f"n_x{s}", [P, D], F32) for s in range(2)]
        zt = [c.sb(ctx, f"n_z{s}", [P, D], F32) for s in range(2)]
        gain = c.sb(ctx, "n_gain", [P, D], F32)
        ss = c.sb(ctx, "n_ss", [P, 2], F32)
        ms = c.sb(ctx, "n_ms", [P, 2], F32)
        rs = c.sb(ctx, "n_rs", [P, 2], F32)
        pz = [c.ps(ctx, f"n_pz{s}", [P, D]) for s in range(2)]
        gain_in = c.sem("n_gain_in")
        x_in = [c.sem(f"n_x_in{s}") for s in range(2)]
        squared, scaled, turned, hi_done, lo_done = (c.sem("n_" + n) for n in
                                                     ("squared", "scaled", "turned", "hi_done", "lo_done"))
        own_a, passed = c.sem("n_own_a"), c.sem("n_passed")
        ROUNDS = NT // 2
        with nc.Block() as block:
            @block.sync
            def _(sp):
                sp.dma_start(xt[1][0:META, :], meta_tokens[:, :]).then_inc(x_in[1], 16)
                sp.dma_start(xt[0][:], x[0, 0:P, :]).then_inc(x_in[0], 16)
                sp.dma_start(gain[:], attn_norm[0, :].partition_broadcast(P)).then_inc(gain_in, 16)

                def load(i, u):
                    sp.wait_ge(scaled, i * 2 + (1 + u))
                    sp.dma_start(xt[u % 2][:], x[0, bass.ds(i * (2 * P) + u * P, P), :]).then_inc(x_in[u % 2], 16)
                load(0, 1)
                with sp.Fori(0, ROUNDS - 1) as i:
                    for u in range(2, 4):
                        load(i, u)

            @block.scalar
            def _(act):
                nc.scalar.preload_act_table_set(LN_AND_EXP)
                chain_a = Chain(act, own_a)
                link_a = chain_a.link

                def root(slot, m, arrived, before):
                    act.wait_ge(x_in[slot], arrived)
                    if before is not None:
                        act.wait_ge(turned, before)
                    link_a(nc.scalar.activation(zt[slot][0:m, :], xt[slot][0:m, :], ACT.Square,
                                                accum_out=ss[0:m, slot:slot + 1]))
                    link_a(nc.scalar.activation(ms[0:m, slot:slot + 1], ss[0:m, slot:slot + 1], ACT.Ln, scale=1.0 / D,
                                                bias=c.eps[0:m, 0:1]))
                    nc.scalar.activation(rs[0:m, slot:slot + 1], ms[0:m, slot:slot + 1], ACT.Exp, scale=-0.5).then_inc(squared, 1)

                def root_tile(i, u):
                    root(u % 2, P, i * 16 + 16 * (u // 2 + 1 + u % 2), i * 2 + (1 + u))

                def high(slot, n, m, col):
                    wait_apart(act, turned, n, passed)
                    nc.scalar.activation(c.zh[:, :, bass.ds(col, m)],
                                         pz[slot][:].rearrange("p (k t) -> p k t", t=P)[:, :, 0:m],
                                         ACT.Copy).then_inc(hi_done, 1)

                def high_tile(i, u):
                    high(u, i * 2 + (3 + u), P, i * (2 * P) + META + u * P)
                root(1, META, 16, None)
                root_tile(0, 0)
                high(1, 2, META, 0)
                with act.Fori(0, ROUNDS - 1) as i:
                    chain_a.enter(i, 4)
                    for u in range(2):
                        root_tile(i, u + 1)
                        high_tile(i, u)
                chain_a.leave(ROUNDS - 1)
                root_tile(ROUNDS - 1, 1)
                for u in range(2):
                    high_tile(ROUNDS - 1, u)

            @block.vector
            def _(dve):
                def scale(slot, n, m):
                    dve.wait_ge(squared, n)
                    nc.vector.scalar_tensor_tensor(out=zt[slot][0:m, :], in0=xt[slot][0:m, :],
                                                   scalar=rs[0:m, slot:slot + 1], in1=gain[0:m, :],
                                                   op0=ALU.mult, op1=ALU.mult).then_inc(scaled, 1)

                def low(slot, n, m, col):
                    dve.wait_ge(hi_done, n)
                    nc.vector.tensor_tensor(c.zl[:, :, bass.ds(col, m)],
                                            pz[slot][:].rearrange("p (k t) -> p k t", t=P)[:, :, 0:m],
                                            c.zh[:, :, bass.ds(col, m)].bitcast(F32), ALU.subtract).then_inc(lo_done, 1)

                def scale_tile(i, u):
                    scale(u % 2, i * 2 + (2 + u), P)

                def low_tile(i, u):
                    low(u, i * 2 + (2 + u), P, i * (2 * P) + META + u * P)
                dve.sem_inc(scaled, 1)
                dve.sem_inc(lo_done, 1)
                nc.vector.memset(c.zh[:, :, L:LP].bitcast(F32), 0.0)
                nc.vector.memset(c.zl[:, :, L:LP].bitcast(F32), 0.0)
                dve.wait_ge(gain_in, 16)
                scale(1, 1, META)
                scale_tile(0, 0)
                low(1, 1, META, 0)
                with dve.Fori(0, ROUNDS - 1) as i:
                    for u in range(2):
                        scale_tile(i, u + 1)
                        low_tile(i, u)
                scale_tile(ROUNDS - 1, 1)
                for u in range(2):
                    low_tile(ROUNDS - 1, u)

            @block.tensor
            def _(pe):
                def turn(slot, n, m):
                    pe.wait_ge(scaled, n)
                    for k in range(KD):
                        last = nc.tensor.transpose(pz[slot][:, k * P:k * P + m], zt[slot][0:m, k * P:(k + 1) * P],
                                                   c.ident[0:m, 0:m])
                    last.then_inc(turned, 1)
                pe.sem_inc(turned, 1)
                turn(1, 2, META)
                with pe.Fori(0, ROUNDS) as i:
                    for u in range(2):
                        pe.wait_ge(lo_done, i * 2 + (1 + u))
                        turn(u, i * 2 + (3 + u), P)


def three_passes(nc, out, xh, xl, wh, wl, first, last):
    nc.tensor.matmul(out, xh, wh, start=first, stop=False)
    nc.tensor.matmul(out, xh, wl, start=False, stop=False)
    return nc.tensor.matmul(out, xl, wh, start=False, stop=last)


PASSES = 3 * KD


def project(nc, c, outs, wh, wl, cols, m=P, a=0, b=PASSES):
    for n_pass in range(a, b):
        k = n_pass // 3
        w, z = ((wh, c.zh), (wh, c.zl), (wl, c.zh))[n_pass % 3]
        for out, (at, n) in zip(outs, cols):
            mm = nc.tensor.matmul(out, w[:, k, 0:m], z[:, k, at:at + n], start=n_pass == 0, stop=n_pass == PASSES - 1)
    return mm


def tile_groups(i):
    full = list(range(i + 1))
    groups = [full[a:a + 4] for a in range(0, i + 1, 4)]
    if i % 2:
        if len(groups[-1]) <= 2:
            groups[-1].append("meta")
        else:
            groups.append(["meta"])
    return groups


def mixers(c, nc, w_in, b_forget, conv_w):
    GR = [tile_groups(i) for i in range(NT)] * 2
    STEPS = 2 * NT
    before = [sum(len(g) for g in GR[:s]) for s in range(STEPS + 1)]
    NGR = before[-1]
    NPV = STEPS // 2
    TAPS = 3
    FT = CW // P
    assert FT == PAIRS
    WT = 6
    NEXT = WT
    cuts = [(0, 8, 12, 16, 20, PASSES)] + [(0, 5, 10, 15, 20, PASSES)] * 2
    filler = {5 * t + a: (3 + t, cuts[t][a], cuts[t][a + 1]) for t in range(3) for a in range(5)}
    filler.update({STEPS - 1: (NEXT, 0, 7), STEPS: (NEXT, 7, 16), STEPS + 1: (NEXT, 16, PASSES)})
    with ExitStack() as ctx:
        raw = [c.sb(ctx, f"a_raw{s}", [P, KD, P], F32) for s in range(2)]
        wh = [c.sb(ctx, f"a_wh{t}", [P, KD, P], F32R) for t in range(2)]
        wl = [c.sb(ctx, f"a_wl{t}", [P, KD, P], F32R) for t in range(2)]
        qs = c.sb(ctx, "a_qs", [P, 2, SEQ], F32R)
        kh = c.sb(ctx, "a_kh", [P, 2, LP], F32R)
        kl = c.sb(ctx, "a_kl", [P, LP], F32R)
        v2 = c.sb(ctx, "a_v2", [P, NT + 1, 2, P], F32R)
        o = c.sb(ctx, "a_o", [P, LP], F32)
        pth = c.sb(ctx, "a_pth", [P, NT + 1, 2 * P], F32R)
        ptl = c.sb(ctx, "a_ptl", [P, NT + 1, 2 * P], F32R)
        tp = [c.sb(ctx, f"a_tp{s}", [P, L], F32) for s in range(2)]
        meta_probs = c.sb(ctx, "a_meta_probs", [P, META], F32)
        cb = c.sb(ctx, "a_cb", [P, L], F32)
        half = [c.sb(ctx, f"a_half{s}", [P, 2 * P], F32) for s in range(2)]
        top = c.sb(ctx, "a_top", [P, STEPS], F32)
        ntop = c.sb(ctx, "a_ntop", [P, STEPS], F32)
        den = c.sb(ctx, "a_den", [P, STEPS], F32)
        rden = c.sb(ctx, "a_rden", [P, STEPS], F32)
        taps = c.sb(ctx, "v_taps", [P, TAPS * FT], F32)
        u = c.sb(ctx, "v_u", [P, LP], F32)
        cv = c.sb(ctx, "v_cv", [P, LP], F32)
        f_w, f_wh, f_wl = (c.sb(ctx, "f_" + n, [P, KD, HEADS], dt) for n, dt in (("w", F32), ("wh", F32R), ("wl", F32R)))
        f_bias = c.sb(ctx, "f_bias", [HEADS, 1], F32)
        f_y, f_mag, f_soft, f_log, f_cum, f_one = (b[0:HEADS, 0:L] for b in (u, cv, tp[0], o, tp[1], cb))
        F = {n: c.sem("f_" + n) for n in ("w_in", "w_hi", "w_lo", "multiplied", "y_done", "mag_done", "exp_done",
                                          "soft_done", "log_done", "cum_done", "stored")}
        s3 = c.ps(ctx, "a_s3", [P, 3 * BANK])
        pj = c.ps(ctx, "a_pj", [P, 3 * BANK])
        pt = c.ps(ctx, "a_pt", [P, BANK])
        po = c.ps(ctx, "a_po", [P, BANK])
        names = ("split_hi", "split_lo", "projected", "q_hi", "q_lo", "k_hi", "k_lo", "v_copied", "v_turned", "v_hi",
                 "v_lo", "scored", "topped", "probs", "turned", "pt_hi", "pt_lo", "pv_done", "half_copied", "o_added",
                 "rden_done", "spread", "meta_kept", "o_scaled", "squared", "averaged", "rooted", "mixed", "cb_in", "taps_in",
                 "x_copied", "u_done", "gated", "c_squared", "c_averaged", "c_rooted", "c_ln", "o_ln", "own", "passed")
        S = {n: c.sem("a_" + n) for n in names}
        raw_in = [c.sem(f"a_raw_in{s}") for s in range(2)]

        def banks(ps):
            return [ps[:, b * BANK:b * BANK + CH] for b in range(3)]

        def in_chunks(sb):
            return sb.rearrange("p (b n) -> p b n", n=CH)

        def by_chunk(ps):
            return ps.rearrange("p (b n) -> p b n", n=BANK)[:, :, 0:CH]
        halves = [pj[:, 0:BANK], pj[:, BANK:2 * BANK]]
        q_cols = [(META, BANK), (META + BANK, BANK)]
        OUTS = [halves, banks(s3), banks(pj), banks(pj), banks(pj), halves, halves]
        COLS = [q_cols, CHUNKS, CHUNKS, CHUNKS, CHUNKS, q_cols, q_cols]
        lower, upper = slice(0, HD), slice(HD, P)
        own_half = [lower, upper]
        other_half = [upper, lower]

        def width(i):
            return META + P * (i + 1)

        with nc.Block() as block:
            @block.sync
            def _(sp):

                def load(i, t):
                    sp.wait_ge(S["split_lo"], i * WT + (t + 1))
                    col = (Q0, K0, V0, X0, C0, B0, Q0 + P, K0 + P)[t]
                    sp.dma_start(raw[t % 2][:], w_in[0, :, bass.ds(i * P + col, P)].rearrange("(k p) n -> p k n", p=P)
                                 ).then_inc(raw_in[t % 2], 16)
                sp.dma_start(f_w[:], w_in[0, :, F0:F0 + HEADS].rearrange("(k p) n -> p k n", p=P)).then_inc(F["w_in"], 16)
                sp.dma_start(f_bias[:], b_forget[0, :].rearrange("(p o) -> p o", o=1)).then_inc(F["w_in"], 16)
                for t in range(2):
                    load(0, t)
                for t in range(TAPS):
                    for f in range(FT):
                        sp.dma_start(taps[:, t * FT + f:t * FT + f + 1],
                                     conv_w[0, t, f * P:(f + 1) * P].rearrange("(p o) -> p o", o=1)).then_inc(S["taps_in"], 16)
                sp.wait_ge(F["cum_done"], 1)
                sp.dma_start(c.negcum[:, :], f_cum).then_inc(F["stored"], 16)
                sp.wait_ge(F["stored"], 16)
                with sp.Fori(0, PAIRS) as i:

                    def bias(h):
                        sp.wait_ge(S["topped"], i * STEPS + (STEPS + NT * h))
                        sp.dma_start(cb[:], c.negcum[bass.ds(i * 2 + h, 1), :].partition_broadcast(P).rearrange(
                            "p o l -> p (o l)")).then_inc(S["cb_in"], 16)
                    load(i, 2)
                    bias(0)
                    for t in range(3, WT):
                        load(i, t)
                    bias(1)
                    for t in range(WT, WT + 2):
                        load(i, t)

            @block.scalar
            def _(act):
                nc.scalar.preload_act_table_set(LN_AND_EXP)

                def split_high(i, t):
                    act.wait_ge(raw_in[t % 2], i * (16 * WT // 2) + 16 * (t // 2 + 1))
                    act.wait_ge(S["projected"], i * WT + (t + 1))
                    nc.scalar.activation(wh[t % 2][:], raw[t % 2][:], ACT.Copy).then_inc(S["split_hi"], 1)
                act.wait_ge(F["w_in"], 32)
                nc.scalar.activation(f_wh[:], f_w[:], ACT.Copy).then_inc(F["w_hi"], 1)
                for t in range(2):
                    split_high(0, t)
                act.wait_ge(F["y_done"], 1)
                nc.scalar.activation(f_mag, f_y, ACT.Abs).then_inc(F["mag_done"], 1)
                act.wait_ge(F["mag_done"], 1)
                nc.scalar.activation(f_mag, f_mag, ACT.Exp, scale=-1.0).then_inc(F["exp_done"], 1)
                act.wait_ge(F["exp_done"], 1)
                nc.scalar.activation(f_soft, f_mag, ACT.Ln, bias=1.0).then_inc(F["soft_done"], 1)
                with act.Fori(0, PAIRS) as i:
                    def split(t):
                        split_high(i, t)

                    def projected(t):
                        act.wait_ge(S["projected"], i * WT + (t + 3))

                    def softmax(s):
                        w = width(s % NT)
                        act.wait_ge(S["topped"], i * STEPS + (STEPS + s + 1))
                        nc.scalar.activation(tp[s % 2][:, 0:w], tp[s % 2][:, 0:w], ACT.Exp, bias=ntop[:, s:s + 1],
                                             accum_out=den[:, s:s + 1]).then_inc(S["probs"], 1)
                    projected(0)
                    nc.scalar.activation(qs[lower, 0, :], pj[lower, 0:SEQ], ACT.Copy, scale=HD ** -0.5)
                    nc.scalar.activation(qs[upper, 1, :], pj[upper, 0:SEQ], ACT.Copy, scale=HD ** -0.5).then_inc(S["q_hi"], 1)
                    split(2)
                    projected(1)
                    for h in range(2):
                        for to in (own_half[h], other_half[h]):
                            last = nc.scalar.activation(in_chunks(kh[to, h, :]), by_chunk(s3[own_half[h], :]), ACT.Copy)
                    last.then_inc(S["k_hi"], 1)
                    split(3)
                    projected(2)
                    act.wait_ge(S["mixed"], i + 1)
                    nc.scalar.activation(in_chunks(o[:]), by_chunk(pj[:]), ACT.Copy).then_inc(S["v_copied"], 1)
                    act.wait_ge(S["v_turned"], i + 1)
                    vt = s3[:, 0:SEQ].rearrange("p (t f) -> p t f", f=P)
                    for h in range(2):
                        f = own_half[h]
                        nc.scalar.activation(v2[:, 0:NT, h, f], vt[:, :, f], ACT.Copy)
                        last = nc.scalar.activation(v2[0:META, NT, h, f], s3[0:META, 2 * BANK + f.start:2 * BANK + f.stop],
                                                    ACT.Copy)
                    last.then_inc(S["v_hi"], 1)
                    split(4)
                    for s in range(STEPS + 2):
                        if s == 5:
                            projected(3)
                            nc.scalar.activation(in_chunks(cv[:]), by_chunk(pj[:]), ACT.Copy).then_inc(S["x_copied"], 1)
                            split(5)
                        if s >= 3 and s % 2 == 1:
                            g = (s - 3) // 2
                            h = g // (NPV // 2)
                            act.wait_ge(S["pv_done"], i * NPV + (g + 1))
                            nc.scalar.activation(half[g % 2][own_half[h], :],
                                                 po[other_half[h], 0:2 * P],
                                                 ACT.Copy).then_inc(S["half_copied"], 1)
                        if s == 0:
                            softmax(0)
                        if 1 <= s <= STEPS:
                            r = s - 1
                            if r % 2 == 0 and r >= 2:
                                act.wait_ge(S["pv_done"], i * NPV + r // 2)
                            for a, group in enumerate(GR[r]):
                                n = before[r] + a
                                act.wait_ge(S["turned"], i * NGR + (n + 1))
                                cols = slice((r % 2) * P, (r % 2) * P + P)
                                tiles = [kt for kt in group if kt != "meta"]
                                if tiles:
                                    ins = nc.scalar.activation(
                                        pth[:, tiles[0]:tiles[-1] + 1, cols],
                                        pt[:, 0:len(tiles) * P].rearrange("p (t q) -> p t q", q=P), ACT.Copy)
                                if "meta" in group:
                                    at = len(tiles) * P
                                    ins = nc.scalar.activation(pth[0:META, NT, :], pt[0:META, at:at + 2 * P], ACT.Copy)
                                ins.then_inc(S["pt_hi"], 1)
                                if a == 0 and s < STEPS:
                                    softmax(s)
                        if s == 10:
                            split(NEXT)
                        if s == STEPS - 1:
                            act.wait_ge(S["gated"], i + 1)
                            nc.scalar.activation(u[:, 0:SEQ], cv[:, 0:SEQ], ACT.Square).then_inc(S["c_squared"], 1)
                            split(NEXT + 1)
                        if s == STEPS:
                            act.wait_ge(S["c_averaged"], i + 1)
                            nc.scalar.activation(u[:, 0:SEQ], s3[:, 0:SEQ], ACT.Ln, bias=c.eps[:, 0:1]).then_inc(S["c_ln"], 1)
                            act.wait_ge(S["c_ln"], i + 1)
                            nc.scalar.activation(u[:, 0:SEQ], u[:, 0:SEQ], ACT.Exp, scale=-0.5).then_inc(S["c_rooted"], 1)
                    act.wait_ge(S["o_scaled"], i + 1)
                    nc.scalar.activation(tp[0][:, 0:SEQ], o[:, 0:SEQ], ACT.Square).then_inc(S["squared"], 1)
                    act.wait_ge(S["averaged"], i + 1)
                    nc.scalar.activation(tp[1][:, 0:SEQ], s3[:, 0:SEQ], ACT.Ln, bias=c.eps[:, 0:1]).then_inc(S["o_ln"], 1)
                    act.wait_ge(S["o_ln"], i + 1)
                    nc.scalar.activation(tp[1][:, 0:SEQ], tp[1][:, 0:SEQ], ACT.Exp, scale=-0.5).then_inc(S["rooted"], 1)

            @block.vector
            def _(dve):
                chain = Chain(dve, S["own"])
                link = chain.link
                dve.sem_inc(S["split_lo"], 2)
                dve.sem_inc(S["topped"], STEPS)
                dve.sem_inc(S["o_added"], 1)

                def split_low(i, t):
                    dve.wait_ge(S["split_hi"], i * WT + (t + 1))
                    nc.vector.tensor_tensor(wl[t % 2][:], raw[t % 2][:], wh[t % 2][:].bitcast(F32),
                                            ALU.subtract).then_inc(S["split_lo"], 1)
                link(nc.vector.memset(f_one, 1.0))
                dve.wait_ge(F["w_hi"], 1)
                nc.vector.tensor_tensor(f_wl[:], f_w[:], f_wh[:].bitcast(F32), ALU.subtract).then_inc(F["w_lo"], 1)
                for t in range(2):
                    split_low(0, t)
                dve.wait_ge(F["multiplied"], 1)
                for b, (at, n) in enumerate((at, min(n, L - at)) for at, n in CHUNKS):
                    last = nc.vector.tensor_scalar(f_y[:, at:at + n], s3[0:HEADS, b * BANK:b * BANK + n], f_bias[:, 0:1],
                                                   None, ALU.add)
                last.then_inc(F["y_done"], 1)
                dve.wait_ge(F["soft_done"], 1)
                nc.vector.scalar_tensor_tensor(out=f_log, in0=f_y, scalar=0.0, in1=f_soft, op0=ALU.min,
                                               op1=ALU.subtract).then_inc(F["log_done"], 1)
                dve.wait_ge(F["log_done"], 1)
                nc.vector.tensor_tensor_scan(f_cum, f_one, f_log, 0.0, ALU.mult, ALU.subtract).then_inc(F["cum_done"], 1)
                dve.wait_ge(F["cum_done"], 1)
                dve.sem_inc(S["mixed"], 1)
                dve.wait_ge(S["taps_in"], 16 * TAPS * FT)
                with dve.Fori(0, PAIRS) as i:
                    chain.enter(i, STEPS + 5)

                    def split(t):
                        split_low(i, t)
                    dve.wait_ge(S["q_hi"], i + 1)
                    nc.vector.scalar_tensor_tensor(out=qs[upper, 0, :], in0=pj[lower, 0:SEQ], scalar=HD ** -0.5,
                                                   in1=qs[lower, 0, :].bitcast(F32), op0=ALU.mult, op1=ALU.subtract)
                    nc.vector.scalar_tensor_tensor(out=qs[lower, 1, :], in0=pj[upper, 0:SEQ], scalar=HD ** -0.5,
                                                   in1=qs[upper, 1, :].bitcast(F32), op0=ALU.mult,
                                                   op1=ALU.subtract).then_inc(S["q_lo"], 1)
                    split(2)
                    dve.wait_ge(S["k_hi"], i + 1)
                    for h in range(2):
                        f = own_half[h]
                        last = nc.vector.tensor_tensor(in_chunks(kl[f, :]), by_chunk(s3[f, :]),
                                                       in_chunks(kh[f, h, :]).bitcast(F32), ALU.subtract)
                    last.then_inc(S["k_lo"], 1)
                    split(3)
                    dve.wait_ge(S["v_hi"], i + 1)
                    vt = s3[:, 0:SEQ].rearrange("p (t f) -> p t f", f=P)
                    for h in range(2):
                        f, g = own_half[h], other_half[h]
                        nc.vector.tensor_tensor(v2[:, 0:NT, h, g], vt[:, :, f], v2[:, 0:NT, h, f].bitcast(F32),
                                                ALU.subtract)
                        last = nc.vector.tensor_tensor(v2[0:META, NT, h, g],
                                                       s3[0:META, 2 * BANK + f.start:2 * BANK + f.stop],
                                                       v2[0:META, NT, h, f].bitcast(F32), ALU.subtract)
                    last.then_inc(S["v_lo"], 1)
                    split(4)
                    for s in range(STEPS + 2):
                        if s >= 2 and s <= STEPS:
                            dve.wait_ge(S["turned"], i * NGR + before[s - 1])
                            if s % 2 == 0:
                                nc.vector.tensor_copy(meta_probs[:], tp[0][:, 0:META]).then_inc(S["meta_kept"], 1)
                        if s < STEPS:
                            h, w = s // NT, width(s % NT)
                            dve.wait_ge(S["scored"], i * STEPS + (s + 1))
                            if s % NT == 0:
                                dve.wait_ge(S["cb_in"], i * 32 + (16 * h + 16))
                            if s % 2 == 0 and s >= 2:
                                dve.wait_ge(S["meta_kept"], i * NPV + s // 2)
                            dve.sem_inc(S["passed"], 1)
                            link(nc.vector.tensor_tensor_reduce(tp[s % 2][:, 0:w], s3[:, 0:w], cb[:, 0:w], 1.0, NEG,
                                                                ALU.add, ALU.max, top[:, s:s + 1]))
                            nc.vector.tensor_scalar(ntop[:, s:s + 1], top[:, s:s + 1], -1.0, None,
                                                    ALU.mult).then_inc(S["topped"], 1)
                        if s >= 3 and s % 2 == 1:
                            g = (s - 3) // 2
                            f = own_half[g // (NPV // 2)]
                            at = (g % (NPV // 2)) * 2 * P
                            dve.wait_ge(S["half_copied"], i * NPV + (g + 1))
                            nc.vector.tensor_tensor(o[f, at:at + 2 * P], po[f, 0:2 * P],
                                                    half[g % 2][f, :], ALU.add).then_inc(S["o_added"], 1)
                        if 1 <= s <= STEPS:
                            r = s - 1
                            for a, group in enumerate(GR[r]):
                                n = before[r] + a
                                dve.wait_ge(S["pt_hi"], i * NGR + (n + 1))
                                cols = slice((r % 2) * P, (r % 2) * P + P)
                                tiles = [kt for kt in group if kt != "meta"]
                                if tiles:
                                    kt = slice(tiles[0], tiles[-1] + 1)
                                    ins = nc.vector.tensor_tensor(
                                        ptl[:, kt, cols], pt[:, 0:len(tiles) * P].rearrange("p (t q) -> p t q", q=P),
                                        pth[:, kt, cols].bitcast(F32), ALU.subtract)
                                if "meta" in group:
                                    at = len(tiles) * P
                                    ins = nc.vector.tensor_tensor(ptl[0:META, NT, :], pt[0:META, at:at + 2 * P],
                                                                  pth[0:META, NT, :].bitcast(F32), ALU.subtract)
                                ins.then_inc(S["pt_lo"], 1)
                        if s == 6:
                            split(5)
                        if s == 9:
                            dve.wait_ge(S["x_copied"], i + 1)
                            dve.wait_ge(S["projected"], i * WT + 7)
                            nc.vector.tensor_tensor(in_chunks(u[:]), in_chunks(cv[:]), by_chunk(pj[:]),
                                                    ALU.mult).then_inc(S["u_done"], 1)
                        if s in (10, 11, 12):
                            t = s - 10
                            src = u[:, META - (TAPS - 1) + t:META - (TAPS - 1) + t + SEQ]
                            w = taps[:, bass.ds(i + t * FT, 1)]
                            if t == 0:
                                dve.wait_ge(S["u_done"], i + 1)
                                link(nc.vector.tensor_scalar(cv[:, 0:SEQ], src, w, None, ALU.mult))
                            else:
                                link(nc.vector.scalar_tensor_tensor(out=cv[:, 0:SEQ], in0=src, scalar=w,
                                                                    in1=cv[:, 0:SEQ], op0=ALU.mult, op1=ALU.add))
                        if s == 13:
                            split(NEXT)
                        if s == STEPS - 2:
                            dve.wait_ge(S["projected"], i * WT + 8)
                            nc.vector.tensor_tensor(cv[:, 0:SEQ], cv[:, 0:SEQ], pj[:, 0:SEQ], ALU.mult).then_inc(S["gated"], 1)
                        if s == STEPS:
                            dve.wait_ge(S["probs"], i * STEPS + STEPS)
                            link(nc.vector.reciprocal(rden[:], den[:]))
                            dve.wait_ge(S["meta_kept"], i * NPV + NPV)
                            nc.vector.tensor_copy(tp[0][:, 0:SEQ].rearrange("p (t h f) -> p t h f", t=NT, h=2),
                                                  rden[:].rearrange("p (h t o) -> p t h o", h=2, o=1).to_broadcast(
                                                      [P, NT, 2, HD])).then_inc(S["rden_done"], 1)
                            split(NEXT + 1)

                    def mix(value, root, col):
                        return nc.vector.scalar_tensor_tensor(
                            out=c.mx[:, bass.ds(i + col, 1), :].rearrange("p o t -> p (o t)"), in0=value[:, 0:SEQ],
                            scalar=c.mixg[:, bass.ds(i + col, 1)], in1=root[:, 0:SEQ], op0=ALU.mult, op1=ALU.mult)
                    dve.wait_ge(S["spread"], i + 1)
                    dve.wait_ge(S["o_added"], i * NPV + (NPV + 1))
                    nc.vector.tensor_tensor(o[:, 0:BANK], o[:, 0:BANK], s3[:, 2 * BANK:3 * BANK], ALU.mult)
                    nc.vector.tensor_tensor(o[:, BANK:SEQ], o[:, BANK:SEQ], pt[:], ALU.mult).then_inc(S["o_scaled"], 1)
                    dve.wait_ge(S["c_rooted"], i + 1)
                    link(mix(cv, u, PAIRS))
                    dve.wait_ge(S["rooted"], i + 1)
                    mix(o, tp[1], 0).then_inc(S["mixed"], 1)
                chain.leave(PAIRS)

            @block.tensor
            def _(pe):
                pe.sem_inc(S["projected"], 2)

                def scores(s):
                    h, q = s // NT, s % NT
                    ps, w, f = s3, width(q), own_half[h]
                    pieces = [(a, min(BANK, w - a)) for a in range(0, w, BANK)]
                    for at, n in pieces:
                        nc.tensor.matmul(ps[:, at:at + n], qs[:, h, q * P:(q + 1) * P], kh[:, h, at:at + n],
                                         start=True, stop=False)
                        mm = nc.tensor.matmul(ps[:, at:at + n], qs[f, h, q * P:(q + 1) * P], kl[f, at:at + n],
                                              start=False, stop=True)
                        a = max(at, w - P)
                        if a < at + n:
                            mm = nc.tensor.matmul(ps[:, a:at + n], c.ident_bf[:], c.maskneg[:, a - (w - P):at + n - (w - P)],
                                                  start=False, stop=True, skip_group_check=True)
                    mm.then_inc(S["scored"], 1)

                def tile(i, t, a=0, b=PASSES):
                    if a == 0:
                        pe.wait_ge(S["split_lo"], i * WT + (t + 3))
                    mm = project(nc, c, OUTS[t], wh[t % 2], wl[t % 2], COLS[t], a=a, b=b)
                    if b == PASSES:
                        mm.then_inc(S["projected"], 1)
                pe.wait_ge(F["w_lo"], 1)
                project(nc, c, [s3[0:HEADS, b * BANK:b * BANK + n] for b, (_, n) in enumerate(CHUNKS)], f_wh, f_wl, CHUNKS,
                        HEADS).then_inc(F["multiplied"], 1)
                tile(0, 0)
                pe.wait_ge(F["y_done"], 1)
                with pe.Fori(0, PAIRS) as i:
                    def average(sq, done):
                        for b in range(2):
                            mm = nc.tensor.matmul(s3[:, b * BANK:(b + 1) * BANK], c.blkavg[:],
                                                  sq[:, b * BANK:(b + 1) * BANK], start=True, stop=True)
                        mm.then_inc(S[done], 1)

                    def filler_parts(s):
                        if s not in filler:
                            return [None] * 3
                        t, a, b = filler[s]
                        n = len(GR[s - 1]) if 1 <= s <= STEPS else 1
                        ahead = 0 if a == 0 and s >= 1 else 1
                        cuts = [a, b, b, b] if s == 0 else [a, a + ahead, a + 3, b] if n >= 2 else [a, a + 2 * ahead, b, b]
                        return [(t, x, y) if x < y else None for x, y in zip(cuts, cuts[1:])]

                    def fill(part):
                        if part:
                            t, a, b = part
                            if a == 0:
                                pe.wait_ge(S[("v_copied", "x_copied", "u_done", "gated")[t - 3]], i + 1)
                            tile(i, t, a, b)
                    pe.wait_ge(S["o_ln"], i)
                    tile(i, 1)
                    pe.wait_ge(S["q_lo"], i + 1)
                    tile(i, 2)
                    for name in ("v_copied", "k_lo"):
                        pe.wait_ge(S[name], i + 1)
                    for t in range(NT):
                        nc.tensor.transpose(s3[:, t * P:(t + 1) * P], o[:, META + t * P:META + (t + 1) * P], c.ident[:])
                    nc.tensor.transpose(s3[0:META, 2 * BANK:2 * BANK + P], o[:, 0:META], c.ident[:]).then_inc(S["v_turned"], 1)
                    for s in range(STEPS + 2):
                        parts = filler_parts(s)
                        if s == 0:
                            fill(parts[0])
                            pe.wait_ge(S["v_lo"], i + 1)
                        if s < STEPS:
                            if s >= 1:
                                pe.wait_ge(S["topped"], i * STEPS + (STEPS + s))
                            scores(s)
                        if s >= 1:
                            fill(parts[0])
                        if s >= 3 and s % 2 == 1:
                            g = (s - 3) // 2
                            h, ga = g // (NPV // 2), g % (NPV // 2)
                            pe.wait_ge(S["pt_lo"], i * NGR + before[2 * g + 2])
                            pe.wait_ge(S["o_added"], i * NPV + (g + 1))
                            out = po[:, 0:2 * P]
                            for kt in range(2 * ga + 2):
                                a = P if kt == 2 * ga + 1 else 0
                                for probs in (pth, ptl):
                                    nc.tensor.matmul(out[:, a:2 * P], v2[:, kt, h, :], probs[:, kt, a:2 * P],
                                                     start=kt == 0 and probs is pth, stop=False, skip_group_check=True)
                            nc.tensor.matmul(out, v2[0:META, NT, h, :], pth[0:META, NT, :], start=False, stop=False,
                                             skip_group_check=True)
                            nc.tensor.matmul(out, v2[0:META, NT, h, :], ptl[0:META, NT, :], start=False, stop=True,
                                             skip_group_check=True).then_inc(S["pv_done"], 1)
                        if 1 <= s <= STEPS:
                            r = s - 1
                            pe.wait_ge(S["probs"], i * STEPS + (r + 1))
                            for a, group in enumerate(GR[r]):
                                n = before[r] + a
                                if n >= 1:
                                    pe.wait_ge(S["pt_lo"], i * NGR + n)
                                at = 0
                                for kt in group:
                                    if kt == "meta":
                                        pe.wait_ge(S["meta_kept"], i * NPV + (r + 1) // 2)
                                        for b, probs in enumerate((meta_probs[:], tp[1][:, 0:META])):
                                            mm = nc.tensor.transpose(pt[0:META, at + b * P:at + (b + 1) * P],
                                                                     probs, c.ident[:])
                                    else:
                                        mm = nc.tensor.transpose(pt[:, at:at + P],
                                                                 tp[r % 2][:, META + kt * P:META + (kt + 1) * P],
                                                                 c.ident[:])
                                    at += P
                                mm.then_inc(S["turned"], 1)
                                fill(parts[1 + a] if a < 2 else None)
                        elif s > STEPS:
                            pe.wait_ge(S["rden_done"], i + 1)
                            pe.wait_ge(S["pt_lo"], i * NGR + NGR)
                            for t in range(NT):
                                out = s3[:, 2 * BANK + t * P:2 * BANK + (t + 1) * P] if t < NT // 2 else \
                                    pt[:, (t - NT // 2) * P:(t - NT // 2 + 1) * P]
                                mm = nc.tensor.transpose(out, tp[0][:, t * P:(t + 1) * P], c.ident[:])
                            mm.then_inc(S["spread"], 1)
                            fill(parts[1])
                            fill(parts[2])
                        else:
                            fill(parts[1])
                            fill(parts[2])
                        if s == STEPS:
                            pe.wait_ge(S["topped"], i * STEPS + (STEPS + STEPS))
                            pe.wait_ge(S["c_squared"], i + 1)
                            average(u, "c_averaged")
                    pe.wait_ge(S["c_ln"], i + 1)
                    pe.wait_ge(S["squared"], i + 1)
                    average(tp[0], "averaged")


def output_projection(c, nc, x, w_out, ffn_norm, w_rg, b_rg, w_re, b_re):
    NR = NG + NE
    SLOTS = 4
    with ExitStack() as ctx:
        raw = [c.sb(ctx, f"o_raw{s}", [P, D], F32) for s in range(SLOTS)]
        wh = c.sb(ctx, "o_wh", [P, KD, D], F32R)
        wl = c.sb(ctx, "o_wl", [P, KD, D], F32R)
        mh = [c.sb(ctx, f"o_mh{s}", [P, KD, P], F32R) for s in range(2)]
        ml = [c.sb(ctx, f"o_ml{s}", [P, KD, P], F32R) for s in range(2)]
        xt = [c.sb(ctx, f"o_x{s}", [P, D], F32) for s in range(2)]
        z2 = [c.sb(ctx, f"o_z2{s}", [P, D], F32) for s in range(2)]
        z2t = [c.sb(ctx, f"o_z2t{s}", [P, D], F32) for s in range(2)]
        gain = c.sb(ctx, "o_gain", [P, D], F32)
        blank = c.sb(ctx, "o_blank", [BLK, D], F32)
        wr = c.sb(ctx, "o_wr", [P, KD, NR], F32)
        br = c.sb(ctx, "o_br", [P, NR], F32)
        ss, ms, rs = (c.sb(ctx, "o_" + n, [P, 2], F32) for n in ("ss", "ms", "rs"))
        ph = [c.ps(ctx, f"o_ph{s}", [P, D]) for s in range(2)]
        pz = c.ps(ctx, "o_pz", [P, D])
        pl = c.ps(ctx, "o_pl", [P, BANK])
        S = {n: c.sem("o_" + n) for n in ("w_hi", "w_lo", "m_hi", "m_lo", "multiplied", "h2_done", "squared", "z2_done",
                                          "turned", "t_copied", "logits", "logits_out", "blanked", "own_a", "passed")}
        raw_in = [c.sem(f"o_raw_in{s}") for s in range(SLOTS)]
        x_in = [c.sem(f"o_x_in{s}") for s in range(2)]
        stored = [c.sem(f"o_stored{s}") for s in range(2)]
        small_in = c.sem("o_small_in")
        S["blank_out"] = c.lasting_sem("o_blank_out")

        def mix_tile(i, n):
            return c.mx[:, :, bass.ds(i * (2 * P) + n * P, P)]

        def three(buf):
            return buf[:].rearrange("p (k t) -> p k t", k=KD)

        ROUNDS = NT // 2

        with nc.Block() as block:
            @block.sync
            def _(sp):
                def weights(k):
                    if k >= SLOTS:
                        sp.wait_ge(S["w_lo"], k - SLOTS + 1)
                    sp.dma_start(raw[k % SLOTS][:], w_out[0, k * P:(k + 1) * P, :]).then_inc(raw_in[k % SLOTS], 16)
                for k in range(SLOTS):
                    weights(k)
                for n in range(2):
                    sp.dma_start(xt[n][:], x[0, n * P:(n + 1) * P, :]).then_inc(x_in[n], 16)
                for k in range(SLOTS, KD):
                    weights(k)
                sp.dma_start(gain[:], ffn_norm[0, :].partition_broadcast(P)).then_inc(small_in, 16)
                sp.dma_start(wr[:, :, 0:NG], w_rg[0].rearrange("(k p) n -> p k n", p=P)).then_inc(small_in, 16)
                sp.dma_start(wr[:, :, NG:NR], w_re[0].rearrange("(k p) n -> p k n", p=P)).then_inc(small_in, 16)
                sp.dma_start(br[:, 0:NG], b_rg[0, :].partition_broadcast(P)).then_inc(small_in, 16)
                sp.dma_start(br[:, NG:NR], b_re[0, :].partition_broadcast(P)).then_inc(small_in, 16)

                def step(i, n, ahead):
                    if ahead:
                        sp.wait_ge(S["h2_done"], i * 2 + (n + 1))
                        sp.dma_start(xt[n][:], x[0, bass.ds(i * (2 * P) + (n + 2) * P, P), :]).then_inc(x_in[n], 16)
                    sp.wait_ge(S["z2_done"], i * 2 + (n + 1))
                    sp.dma_start(c.z2rows[bass.ds(i * (2 * P) + n * P, P), :], z2[n][:]).then_inc(stored[n], 16)
                with sp.Fori(0, ROUNDS - 1) as i:
                    for n in range(2):
                        step(i, n, True)
                for n in range(2):
                    step(ROUNDS - 1, n, False)
                for n in range(2):
                    sp.wait_ge(stored[n], 16 * (ROUNDS + 1))

            @block.gpsimd
            def _(pool):
                nc.gpsimd.memset(blank[:], 0.0).then_inc(S["blanked"], 1)
                pool.wait_ge(S["blanked"], 1)
                for b in range(NE, NBLK):
                    pool.wait_ge(S["multiplied"], 2 + 1 + (b - NE) * (NT - 1) // OVB)
                    pool.dma_start(c.yrows[b * BLK:(b + 1) * BLK, :], blank[:]).then_inc(S["blank_out"], 16)
                pool.wait_ge(S["blank_out"], 16 * OVB)

            @block.scalar
            def _(act):
                nc.scalar.preload_act_table_set(LN_AND_EXP)
                chain = Chain(act, S["own_a"])

                def mix_high(i, n):
                    wait_apart(act, S["multiplied"], i * 2 + (n + 1), S["passed"])
                    nc.scalar.activation(mh[n % 2][:], mix_tile(i, n), ACT.Copy).then_inc(S["m_hi"], 1)

                def step(i, n, ahead):
                    act.wait_ge(S["h2_done"], i * 2 + (n + 1))
                    act.wait_ge(stored[n], i * 16 + 16)
                    wait_apart(act, S["turned"], i * 2 + (n + 1), S["passed"])
                    chain.link(nc.scalar.activation(three(z2[n]), mix_tile(i, n), ACT.Square, accum_out=ss[:, n:n + 1]))
                    chain.link(nc.scalar.activation(ms[:, n:n + 1], ss[:, n:n + 1], ACT.Ln, scale=1.0 / D,
                                                    bias=c.eps[:, 0:1]))
                    nc.scalar.activation(rs[:, n:n + 1], ms[:, n:n + 1], ACT.Exp, scale=-0.5).then_inc(S["squared"], 1)
                    if ahead:
                        mix_high(i, n + 2)
                    act.wait_ge(S["turned"], i * 2 + (n + 3))
                    act.wait_ge(S["logits"], i * 2 + (n + 1))
                    nc.scalar.activation(z2t[n][:], pz[:], ACT.Copy).then_inc(S["t_copied"], 1)
                for n in range(2):
                    mix_high(0, n)
                for k in range(KD):
                    act.wait_ge(raw_in[k % SLOTS], 16 * (k // SLOTS + 1))
                    nc.scalar.activation(wh[:, k, :], raw[k % SLOTS][:], ACT.Copy).then_inc(S["w_hi"], 1)
                with act.Fori(0, ROUNDS - 1) as i:
                    chain.enter(i, 4)
                    for n in range(2):
                        step(i, n, True)
                chain.leave(ROUNDS - 1)
                for n in range(2):
                    step(ROUNDS - 1, n, False)

            @block.vector
            def _(dve):
                for n in range(2):
                    dve.sem_inc(stored[n], 16)

                def mix_low(i, n):
                    dve.wait_ge(S["m_hi"], i * 2 + (n + 1))
                    nc.vector.tensor_tensor(ml[n % 2][:], mix_tile(i, n), mh[n % 2][:].bitcast(F32),
                                            ALU.subtract).then_inc(S["m_lo"], 1)

                def step(i, n, ahead):
                    dve.wait_ge(S["multiplied"], i * 2 + (n + 3))
                    dve.wait_ge(x_in[n], i * 16 + 16)
                    nc.vector.tensor_tensor(mix_tile(i, n), three(xt[n]), three(ph[n]), ALU.add).then_inc(S["h2_done"], 1)
                    dve.wait_ge(S["squared"], i * 2 + (n + 1))
                    nc.vector.scalar_tensor_tensor(out=three(z2[n]), in0=mix_tile(i, n), scalar=rs[:, n:n + 1],
                                                   in1=three(gain), op0=ALU.mult, op1=ALU.mult).then_inc(S["z2_done"], 1)
                    if ahead:
                        mix_low(i, n + 2)
                    dve.wait_ge(S["logits"], i * 2 + (n + 3))
                    nc.vector.tensor_tensor(c.logits[:, bass.ds(i * 2 + n, 1), :].rearrange("p o n -> p (o n)"),
                                            pl[:, n * P:n * P + NR], br[:], ALU.add).then_inc(S["logits_out"], 1)
                for n in range(2):
                    mix_low(0, n)
                for k in range(KD):
                    dve.wait_ge(S["w_hi"], k + 1)
                    nc.vector.tensor_tensor(wl[:, k, :], raw[k % SLOTS][:], wh[:, k, :].bitcast(F32),
                                            ALU.subtract).then_inc(S["w_lo"], 1)
                dve.wait_ge(small_in, 16 * 5)
                with dve.Fori(0, ROUNDS - 1) as i:
                    for n in range(2):
                        step(i, n, True)
                for n in range(2):
                    step(ROUNDS - 1, n, False)

            @block.tensor
            def _(pe):
                pe.sem_inc(S["multiplied"], 2)
                pe.sem_inc(S["turned"], 2)
                pe.sem_inc(S["logits"], 2)

                def product(u, k, b):
                    n = slice(b * BANK, (b + 1) * BANK)
                    return three_passes(nc, ph[u][:, n], mh[u][:, k, :], ml[u][:, k, :], wh[:, k, n], wl[:, k, n],
                                        k == 0, k == KD - 1)

                def step(i, n, ahead):
                    u = (n + 1) % 2
                    if ahead:
                        pe.wait_ge(S["m_lo"], i * 2 + (n + 2))
                        pe.wait_ge(S["h2_done"], i * 2 + n)
                        for k in range(KD):
                            product(u, k, 0)
                    pe.wait_ge(S["z2_done"], i * 2 + (n + 1))
                    pe.wait_ge(S["t_copied"], i * 2 + (n + 1))
                    for k in range(KD):
                        mm = nc.tensor.transpose(pz[:, k * P:(k + 1) * P], z2[n][:, k * P:(k + 1) * P], c.ident[:])
                    mm.then_inc(S["turned"], 1)
                    if ahead:
                        for k in range(KD):
                            mm = product(u, k, 1)
                        mm.then_inc(S["multiplied"], 1)
                    pe.wait_ge(S["t_copied"], i * 2 + (n + 2))
                    pe.wait_ge(S["logits_out"], i * 2 + (n + 1))
                    for k in range(KD):
                        mm = nc.tensor.matmul(pl[:, n * P:n * P + NR], z2t[n][:, k * P:(k + 1) * P], wr[:, k, :],
                                              start=k == 0, stop=k == KD - 1)
                    mm.then_inc(S["logits"], 1)
                pe.sem_inc(S["t_copied"], 1)
                pe.sem_inc(S["logits_out"], 1)
                pe.wait_ge(S["m_lo"], 1)
                for k in range(KD):
                    pe.wait_ge(S["w_lo"], k + 1)
                    for b in range(2):
                        mm = product(0, k, b)
                mm.then_inc(S["multiplied"], 1)
                with pe.Fori(0, ROUNDS - 1) as i:
                    for n in range(2):
                        step(i, n, True)
                step(ROUNDS - 1, 0, True)
                step(ROUNDS - 1, 1, False)


def route(c, nc, w_gate, w_up, w_down):
    with ExitStack() as ctx:
        f = lambda name, shape, dt=F32: c.sb(ctx, "r_" + name, shape, dt)
        iota_i = f("iota_i", [P, NE], I32)
        iota_e = f("iota_e", [P, NE])
        lane_i, lane = f("lane_i", [P, 1], I32), f("lane", [P, 1])
        row_i, row_f = f("row_i", [P, BLK], I32), f("row_f", [P, BLK])
        block_i, block_f = f("block_i", [P, NBLK + 1], I32), f("block_f", [P, NBLK + 1])
        limits_i, limits = f("limits_i", [P, NB_LESS], I32), f("limits", [P, NB_LESS])
        gmax, gsum, gw, gi = (f(n, [P, NT]) for n in ("gmax", "gsum", "gw", "gi"))
        gd, geq, goh, pen = (f(n, [P, NT, NG]) for n in ("gd", "geq", "goh", "pen"))
        masked = [f(f"masked{j}", [P, NT, NE]) for j in range(2)]
        eq = f("eq", [P, NT, NE])
        hot = [f(f"hot{j}", [P, NT, NE]) for j in range(2)]
        both = f("both", [P, NT, NE], BF16)
        emax = [f(f"emax{j}", [P, NT]) for j in range(2)]
        eidx = f("eidx", [P, 2, NT])
        ediff, eexp, eden = (f(n, [P, NT]) for n in ("ediff", "eexp", "eden"))
        rank = f("rank", [P, NT, NE])
        run = f("run", [P, NT + 1, NE])
        over = f("over", [P, NE, NB_LESS])
        nov, ovend, ovstart, onee = (f(n, [P, NE]) for n in ("nov", "ovend", "ovstart", "onee"))
        pick = f("pick", [P, NT, NE])
        r2, ovs, full, isov, shift, blk, row, slot = (
            f(n, [P, 2, NT]) for n in ("r2", "ovs", "full", "isov", "shift", "blk", "row", "slot"))
        passes = f("passes", [P, 2 * NT, NB_LESS])
        in_row = f("in_row", [P, 2 * NT, BLK], BF16)
        in_block = f("in_block", [P, 2 * NT, NBLK + 1])
        token_lane = f("token_lane", [P, 2 * NT, NBLK + 1], BF16)
        token_tile = f("token_tile", [P, 2 * NT, NBLK + 1], BF16)
        lanes = f("lanes", [BLK, NBLK + 1])
        ovcmp = f("ovcmp", [P, OVB, NE])
        ove_f = f("ove_f", [P, OVB])
        pairs_f = f("pairs_f", [P, 1])
        p_in = c.ps(ctx, "r_in", [P, BANK])
        p_tot = c.ps(ctx, "r_tot", [P, BANK])
        p_lane = c.ps(ctx, "r_p_lane", [P, BANK])
        p_tile = c.ps(ctx, "r_p_tile", [P, BANK])
        S = {n: c.sem("r_" + n) for n in ("made", "g_ready", "g_exp", "e_ready", "e_exp", "marked", "counted", "placed",
                                          "collected", "own")}
        tile4 = lambda ap: ap.rearrange("p t (g e) -> p t g e", e=EPG)
        with nc.Block() as block:
            @block.gpsimd
            def _(pool):
                nc.gpsimd.iota(iota_i[:], pattern=[[1, NE]], base=0, channel_multiplier=0)
                nc.gpsimd.iota(limits_i[:], pattern=[[BLK, NB_LESS]], base=BLK, channel_multiplier=0)
                nc.gpsimd.iota(row_i[:], pattern=[[1, BLK]], base=0, channel_multiplier=0)
                nc.gpsimd.iota(block_i[:], pattern=[[1, NBLK + 1]], base=0, channel_multiplier=0)
                nc.gpsimd.iota(lane_i[:], pattern=[[0, 1]], base=0, channel_multiplier=1).then_inc(S["made"], 1)

            @block.sync
            def _(sp):
                for j in range(UNITS):
                    to, src = unit(c.raw[j], j, 0, w_gate, w_up, w_down)
                    sp.dma_start(to, src).then_inc(c.raw_in[j], 16)

            @block.scalar
            def _(act):
                act.wait_ge(S["g_ready"], 1)
                nc.scalar.activation(gd[:], gd[:], ACT.Exp).then_inc(S["g_exp"], 1)
                act.wait_ge(S["e_ready"], 1)
                nc.scalar.activation(eexp[:], ediff[:], ACT.Exp).then_inc(S["e_exp"], 1)

            @block.tensor
            def _(pe):
                pe.wait_ge(S["marked"], 1)
                nc.tensor.matmul(p_in[:, 0:NT * NE], c.tri[:], both[:].rearrange("p t e -> p (t e)"), start=True, stop=True)
                nc.tensor.matmul(p_tot[:, 0:NT * NE], c.ones_bf[:], both[:].rearrange("p t e -> p (t e)"), start=True,
                                 stop=True).then_inc(S["counted"], 1)
                pe.wait_ge(S["placed"], 1)
                for out, values in ((p_lane, token_lane), (p_tile, token_tile)):
                    for n in range(2 * NT):
                        mm = nc.tensor.matmul(out[0:BLK, 0:NBLK + 1], in_row[:, n, :], values[:, n, :], start=n == 0,
                                              stop=n == 2 * NT - 1)
                mm.then_inc(S["collected"], 1)

            @block.vector
            def _(dve):
                link = Chain(dve, S["own"]).link
                V = nc.vector
                dve.wait_ge(S["made"], 1)
                link(V.tensor_copy(iota_e[:], iota_i[:]))
                for as_float, ints in ((limits, limits_i), (row_f, row_i), (block_f, block_i), (lane, lane_i)):
                    link(V.tensor_copy(as_float[:], ints[:]))
                lg, le = c.logits[:, :, 0:NG], c.logits[:, :, NG:NG + NE]
                wide = lambda ap, n: ap.rearrange("p (t o) -> p t o", o=1).to_broadcast([P, NT, n])
                ids = lambda n: iota_e[:, 0:n].rearrange("p (o e) -> p o e", o=1).to_broadcast([P, NT, n])

                def first_of_max(values, top, eq, index, hot, n):
                    link(V.tensor_reduce(top, values, AX.X, ALU.max))
                    link(V.tensor_tensor(eq, values, wide(top, n), ALU.is_equal))
                    link(V.tensor_scalar(eq, eq, -float(n), float(n), ALU.mult, ALU.add))
                    link(V.tensor_tensor(eq, eq, ids(n), ALU.add))
                    link(V.tensor_reduce(index, eq, AX.X, ALU.min))
                    link(V.tensor_tensor(hot, ids(n), wide(index, n), ALU.is_equal))
                first_of_max(lg, gmax[:], geq[:], gi[:], goh[:], NG)
                V.tensor_tensor(gd[:], lg, wide(gmax[:], NG), ALU.subtract).then_inc(S["g_ready"], 1)
                link(V.tensor_scalar(pen[:], goh[:], -NEG, NEG, ALU.mult, ALU.add))
                link(V.tensor_tensor(tile4(masked[0][:]), tile4(le), pen[:].rearrange("p t (g o) -> p t g o", o=1)
                                     .to_broadcast([P, NT, NG, EPG]), ALU.add))
                first_of_max(masked[0][:], emax[0][:], eq[:], eidx[:, 0, :], hot[0][:], NE)
                link(V.scalar_tensor_tensor(out=masked[1][:], in0=hot[0][:], scalar=2 * NEG, in1=masked[0][:],
                                            op0=ALU.mult, op1=ALU.add))
                first_of_max(masked[1][:], emax[1][:], eq[:], eidx[:, 1, :], hot[1][:], NE)
                V.tensor_tensor(ediff[:], emax[1][:], emax[0][:], ALU.subtract).then_inc(S["e_ready"], 1)
                V.tensor_tensor(both[:], hot[0][:], hot[1][:], ALU.add).then_inc(S["marked"], 1)
                dve.wait_ge(S["g_exp"], 1)
                link(V.tensor_reduce(gsum[:], gd[:], AX.X, ALU.add))
                link(V.reciprocal(gw[:], gsum[:]))
                dve.wait_ge(S["e_exp"], 1)
                link(V.tensor_scalar(eden[:], eexp[:], 1.0, None, ALU.add))
                link(V.reciprocal(eden[:], eden[:]))
                link(V.tensor_tensor(c.weight[:, 0:NT], gw[:], eden[:], ALU.mult))
                link(V.tensor_tensor(c.weight[:, NT:2 * NT], c.weight[:, 0:NT], eexp[:], ALU.mult))
                dve.wait_ge(S["counted"], 1)
                link(V.memset(run[:, 0, :], 0.0))
                for t in range(NT):
                    link(V.tensor_tensor(run[:, t + 1, :], run[:, t, :], p_tot[:, t * NE:(t + 1) * NE], ALU.add))
                link(V.tensor_tensor(rank[:], run[:, 0:NT, :], p_in[:, 0:NT * NE].rearrange("p (t e) -> p t e", e=NE), ALU.add))
                link(V.tensor_tensor(over[:], run[:, NT, :].rearrange("p (e o) -> p e o", o=1).to_broadcast([P, NE, NB_LESS]),
                                     limits[:].rearrange("p (o b) -> p o b", o=1).to_broadcast([P, NE, NB_LESS]), ALU.is_gt))
                link(V.tensor_reduce(nov[:], over[:], AX.X, ALU.add))
                link(V.memset(onee[:], 1.0))
                link(V.tensor_tensor_scan(ovend[:], onee[:], nov[:], 0.0, ALU.mult, ALU.add))
                link(V.tensor_tensor(ovstart[:], ovend[:], nov[:], ALU.subtract))
                for j in range(2):
                    link(V.tensor_tensor(pick[:], hot[j][:], rank[:], ALU.mult))
                    link(V.tensor_reduce(r2[:, j, :], pick[:], AX.X, ALU.add))
                    link(V.tensor_tensor(pick[:], hot[j][:], ovstart[:].rearrange("p (o e) -> p o e", o=1)
                                         .to_broadcast([P, NT, NE]), ALU.mult))
                    link(V.tensor_reduce(ovs[:, j, :], pick[:], AX.X, ALU.add))
                spread = lambda ap, n: ap.rearrange("p (a o) -> p a o", o=1).to_broadcast([P, 2 * NT, n])
                along = lambda ap, n: ap.rearrange("p (o b) -> p o b", o=1).to_broadcast([P, 2 * NT, n])
                flat = lambda ap: ap.rearrange("p j t -> p (j t)")
                link(V.tensor_tensor(passes[:], spread(flat(r2[:]), NB_LESS), along(limits[:], NB_LESS), ALU.is_ge))
                link(V.tensor_reduce(flat(full[:]), passes[:], AX.X, ALU.add))
                link(V.tensor_scalar(isov[:], full[:], 1.0, None, ALU.is_ge))
                link(V.tensor_tensor(shift[:], ovs[:], eidx[:], ALU.subtract))
                link(V.tensor_tensor(shift[:], shift[:], full[:], ALU.add))
                link(V.tensor_scalar(shift[:], shift[:], float(NE - 1), None, ALU.add))
                link(V.tensor_tensor(shift[:], shift[:], isov[:], ALU.mult))
                link(V.tensor_tensor(blk[:], eidx[:], shift[:], ALU.add))
                link(V.scalar_tensor_tensor(out=row[:], in0=full[:], scalar=-float(BLK), in1=r2[:], op0=ALU.mult, op1=ALU.add))
                link(V.tensor_tensor(in_row[:], along(row_f[:], BLK), spread(flat(row[:]), BLK), ALU.is_equal))
                link(V.tensor_tensor(in_block[:], along(block_f[:], NBLK + 1), spread(flat(blk[:]), NBLK + 1), ALU.is_equal))
                link(V.tensor_scalar(token_lane[:], in_block[:], lane[:, 0:1], None, ALU.mult))
                tiles = iota_e[:, 0:NT].rearrange("p (o t z) -> p o t z", o=1, z=1).to_broadcast([P, 2, NT, NBLK + 1])
                V.tensor_tensor(token_tile[:].rearrange("p (j t) b -> p j t b", j=2),
                                in_block[:].rearrange("p (j t) b -> p j t b", j=2), tiles, ALU.mult).then_inc(S["placed"], 1)
                link(V.scalar_tensor_tensor(out=slot[:], in0=blk[:], scalar=float(BLK), in1=row[:], op0=ALU.mult, op1=ALU.add))
                link(V.tensor_copy(c.slot_of[:].rearrange("p (j t) -> p j t", j=2), slot[:]))
                link(V.tensor_tensor(ovcmp[:], ovend[:].rearrange("p (o e) -> p o e", o=1).to_broadcast([P, OVB, NE]),
                                     iota_e[:, 0:OVB].rearrange("p (b o) -> p b o", o=1).to_broadcast([P, OVB, NE]), ALU.is_le))
                link(V.tensor_reduce(ove_f[:], ovcmp[:], AX.X, ALU.add))
                link(V.tensor_scalar(ove_f[:], ove_f[:], float(NE - 1), None, ALU.min))
                link(V.tensor_copy(c.over_expert[:, 0:OVB], ove_f[0:1, :]))
                link(V.tensor_scalar(pairs_f[:], ovend[:, NE - 1:NE], 1.0, 0.5, ALU.add, ALU.mult))
                link(V.tensor_tensor(ovcmp[:, 0, 0:OVB // 2 + 1], pairs_f[:, 0:1].to_broadcast([P, OVB // 2 + 1]),
                                     iota_e[:, 1:OVB // 2 + 2], ALU.is_ge))
                link(V.tensor_reduce(pairs_f[:], ovcmp[:, 0, 0:OVB // 2 + 1], AX.X, ALU.add))
                link(V.tensor_copy(c.over_expert[:, OVB:OVB + 1], pairs_f[0:1, :]))
                dve.wait_ge(S["collected"], 1)
                link(V.tensor_copy(lanes[:], p_lane[0:BLK, 0:NBLK + 1]))
                link(V.scalar_tensor_tensor(out=c.row_tokens[:], in0=p_tile[0:BLK, 0:NBLK + 1], scalar=float(P),
                                            in1=lanes[:], op0=ALU.mult, op1=ALU.add))


def unit(raw, j, e, w_gate, w_up, w_down):
    if j < 4:
        n, part = DE, (w_gate, w_up)[j // 2][0, bass.ds(e, 1), (j % 2) * D // 2:(j % 2 + 1) * D // 2, :]
    else:
        n, part = D, w_down[0, bass.ds(e, 1), (j % 2) * DE // 2:(j % 2 + 1) * DE // 2, :]
    return raw[:].rearrange("p (k n) -> p k n", n=n), part.rearrange("o (k p) n -> p (o k) n", p=P)


def experts(c, nc, tag, pairs, block0, w_gate, w_up, w_down):
    dynamic = pairs is None
    RING = 4
    raw = c.raw
    with ExitStack() as ctx:
        wh = [c.sb(ctx, f"{tag}_wh{s}", [P, UNIT], F32R) for s in range(RING)]
        wl = [c.sb(ctx, f"{tag}_wl{s}", [P, UNIT], F32R) for s in range(RING)]
        xg = [c.sb(ctx, f"{tag}_xg{s}", [BLK, D], F32) for s in range(2)]
        xh = [c.sb(ctx, f"{tag}_xh{s}", [P, KD * BLK], F32R) for s in range(2)]
        xl = [c.sb(ctx, f"{tag}_xl{s}", [P, KD * BLK], F32R) for s in range(2)]
        ids = [c.sb(ctx, f"{tag}_ids{s}", [BLK, 1], I32) for s in range(2)]
        act_g = c.sb(ctx, tag + "_act_g", [BLK, DE], F32)
        hid = c.sb(ctx, tag + "_hid", [BLK, DE], F32)
        hh = c.sb(ctx, tag + "_hh", [P, DE // P * BLK], F32R)
        hl = c.sb(ctx, tag + "_hl", [P, DE // P * BLK], F32R)
        ys = [c.sb(ctx, f"{tag}_ys{s}", [BLK, D], F32) for s in range(2)]
        pg = c.ps(ctx, tag + "_pg", [BLK, BANK])
        pu = c.ps(ctx, tag + "_pu", [BLK, BANK])
        px = c.ps(ctx, tag + "_px", [P, D])
        phid = c.ps(ctx, tag + "_phid", [P, BANK])
        py = c.ps(ctx, tag + "_py", [BLK, D])
        S = {n: c.sem(f"{tag}_{n}") for n in ("w_hi", "w_lo", "unit_used", "x_turned", "x_hi", "x_lo",
                                              "silu_done", "h_done", "h_turned", "h_hi", "h_lo",
                                              "y_copied", "ids_ready", "passed")}
        raw_in = [c.sem(f"{tag}_raw_in{j}") for j in range(UNITS)] if dynamic else c.raw_in
        gathered = [c.lasting_sem(f"{tag}_gathered{s}") for s in range(2)]
        stored = [c.sem(f"{tag}_stored{s}") for s in range(2)]

        def tiles4(ap):
            return ap.rearrange("p (b n) -> p b n", n=4 * BLK)

        def banks4(ap):
            return ap.rearrange("p (b n) -> p b n", n=BANK)[:, :, 0:4 * BLK]

        def rounds(eng, body, last=None):
            if not dynamic:
                body(0, True)
                with eng.Fori(1, pairs) as i:
                    body(i, False)
                if last:
                    last(pairs)
                return
            n = eng.value_load(c.over_expert[0:1, OVB:OVB + 1], min_val=0, max_val=OVB // 2)
            with eng.If(n > 0):
                body(0, True)
                with eng.If(n > 1):
                    with eng.Fori(1, n) as i:
                        body(i, False)
                with eng.Else():
                    eng.nop()
                if last:
                    last(n)
            with eng.Else():
                eng.nop()

        def split(N, j):
            return N * UNITS + (UNITS + j + 1)

        def products(N, j):
            return N * UNITS + (RING + j + 1)
        GATE, UP, DOWN = 1, 3, 5

        with nc.Block() as block:
            @block.sync
            def _(sp):
                def load(i, first):
                    for u in range(2):
                        N = i * 2 + u
                        if dynamic:
                            e = sp.value_load(c.over_expert[0:1, bass.ds(N, 1)], min_val=0, max_val=NE - 1)
                        else:
                            e = N
                        if first and u == 0 and not dynamic:
                            continue
                        for j in range(UNITS):
                            sp.wait_ge(S["w_lo"], split(N - 1, j))
                            to, src = unit(raw[j], j, e, w_gate, w_up, w_down)
                            sp.dma_start(to, src).then_inc(raw_in[j], 16)
                rounds(sp, load)

            @block.gpsimd
            def _(pool):
                def gather(slot, column, n):
                    nc.gpsimd.tensor_copy(ids[slot][:], c.row_tokens[:, column]).then_inc(S["ids_ready"], 1)
                    wait_apart(pool, S["ids_ready"], n, S["passed"])
                    nc.gpsimd.indirect_dma_start(out=xg[slot][:], out_offset=None, in_=c.z2rows[:, :],
                                                 in_offset=bass.IndirectOffsetOnAxis(ap=ids[slot][:, 0:1], axis=0)
                                                 ).then_inc(gathered[slot], 16)

                def body(i, first):
                    for u in range(2):
                        N = i * 2 + u
                        if first and u == 0:
                            gather(0, slice(block0, block0 + 1), 1)
                        pool.wait_ge(S["x_turned"], N + 1)
                        gather(1 - u, bass.ds(N + (block0 + 1), 1), N + 2)

                def last(n):
                    pool.wait_ge(gathered[0], n * 16 + 16)
                rounds(pool, body, last)

            @block.scalar
            def _(act):
                def high(N, u, j):
                    s = (UNITS * u + j) % RING
                    act.wait_ge(raw_in[j], N * 16 + 16)
                    act.wait_ge(S["unit_used"], N * UNITS + (j + 1))
                    nc.scalar.activation(wh[s][:], raw[j][:], ACT.Copy).then_inc(S["w_hi"], 1)

                def x_high(k, slot):
                    act.wait_ge(S["x_turned"], k + 2)
                    if not (isinstance(k, int) and k < 2):
                        act.wait_ge(S["unit_used"], products(k - 2, UP))
                    nc.scalar.activation(tiles4(xh[slot][:]), banks4(px[:]), ACT.Copy).then_inc(S["x_hi"], 1)

                def y_out(i, u, N):
                    act.wait_ge(S["unit_used"], products(N, DOWN))
                    act.wait_ge(stored[u], i * 16 + 16)
                    nc.scalar.activation(ys[u][:], py[:], ACT.Copy).then_inc(S["y_copied"], 1)
                    act.wait_ge(S["y_copied"], N + 2)
                    act.dma_start(c.yrows[bass.ds(N * BLK + block0 * BLK, BLK), :], ys[u][:]).then_inc(stored[u], 16)

                def body(i, first):
                    for u in range(2):
                        N = i * 2 + u
                        high(N, u, 0)
                        high(N, u, 1)
                        high(N, u, 2)
                        if first and u == 0:
                            x_high(0, 0)
                        if not (first and u == 0):
                            y_out(i - (1 - u), 1 - u, N - 1)
                        for j in (3, 4):
                            high(N, u, j)
                        act.wait_ge(S["unit_used"], products(N, GATE))
                        act.wait_ge(S["h_done"], N + 1)
                        nc.scalar.activation(act_g[:], pg[:], ACT.Silu).then_inc(S["silu_done"], 1)
                        high(N, u, 5)
                        x_high(N + 1, 1 - u)
                        act.wait_ge(S["h_turned"], N + 2)
                        act.wait_ge(S["unit_used"], products(N, -1))
                        nc.scalar.activation(hh[:], phid[:, 0:DE // P * BLK], ACT.Copy).then_inc(S["h_hi"], 1)

                def last(n):
                    y_out(n - 1, 1, n * 2 - 1)
                    for u in range(2):
                        wait_apart(act, stored[u], n * 16 + 16, S["passed"])
                rounds(act, body, last)

            @block.vector
            def _(dve):
                dve.sem_inc(S["w_lo"], UNITS)
                dve.sem_inc(S["x_lo"], 1)
                dve.sem_inc(S["h_done"], 1)
                dve.sem_inc(S["h_lo"], 1)
                for u in range(2):
                    dve.sem_inc(stored[u], 16)
                dve.sem_inc(S["y_copied"], 1)

                def low(N, u, j):
                    s = (UNITS * u + j) % RING
                    dve.wait_ge(S["w_hi"], N * UNITS + (j + 1))
                    nc.vector.tensor_tensor(wl[s][:], raw[j][:], wh[s][:].bitcast(F32), ALU.subtract).then_inc(S["w_lo"], 1)

                def x_low(k, slot):
                    dve.wait_ge(S["x_hi"], k + 1)
                    nc.vector.tensor_tensor(tiles4(xl[slot][:]), banks4(px[:]), tiles4(xh[slot][:]).bitcast(F32),
                                            ALU.subtract).then_inc(S["x_lo"], 1)

                def body(i, first):
                    for u in range(2):
                        N = i * 2 + u
                        for j in range(UNITS):
                            low(N, u, j)
                            if first and u == 0 and j == 1:
                                x_low(0, 0)
                        dve.wait_ge(S["silu_done"], N + 1)
                        dve.wait_ge(S["unit_used"], products(N, UP))
                        dve.wait_ge(S["h_turned"], N + 1)
                        nc.vector.tensor_tensor(hid[:], act_g[:], pu[:], ALU.mult).then_inc(S["h_done"], 1)
                        x_low(N + 1, 1 - u)
                        dve.wait_ge(S["h_hi"], N + 1)
                        nc.vector.tensor_tensor(hl[:], phid[:, 0:DE // P * BLK], hh[:].bitcast(F32), ALU.subtract).then_inc(S["h_lo"], 1)
                rounds(dve, body)

            @block.tensor
            def _(pe):
                pe.sem_inc(S["unit_used"], RING)
                pe.sem_inc(S["x_turned"], 1)
                pe.sem_inc(S["h_turned"], 1)

                def turn_x(k, slot, arrived):
                    pe.wait_ge(gathered[slot], arrived)
                    pe.wait_ge(S["x_lo"], k + 1)
                    for t in range(KD):
                        at = t // 4 * BANK + t % 4 * BLK
                        mm = nc.tensor.transpose(px[:, at:at + BLK], xg[slot][:, t * P:(t + 1) * P], c.ident[0:BLK, 0:BLK])
                    mm.then_inc(S["x_turned"], 1)

                def body(i, first):
                    for u in range(2):
                        N = i * 2 + u
                        if first and u == 0:
                            turn_x(0, 0, 16)
                        pe.wait_ge(S["x_lo"], N + 2)
                        pe.wait_ge(S["h_done"], N + 1)
                        for j in range(4):
                            s = (UNITS * u + j) % RING
                            out = (pg, pu)[j // 2]
                            pe.wait_ge(S["w_lo"], split(N, j))
                            for b in range(4):
                                k = (j % 2) * 4 + b
                                n = slice(b * DE, (b + 1) * DE)
                                mm = three_passes(nc, out[:], xh[u][:, k * BLK:(k + 1) * BLK], xl[u][:, k * BLK:(k + 1) * BLK],
                                                  wh[s][:, n], wl[s][:, n], k == 0, k == KD - 1)
                            mm.then_inc(S["unit_used"], 1)
                        turn_x(N + 1, 1 - u, i * 16 + 16 * (u + 1))
                        pe.wait_ge(S["h_done"], N + 2)
                        pe.wait_ge(S["h_lo"], N + 1)
                        for t in range(DE // P):
                            mm = nc.tensor.transpose(phid[:, t * BLK:(t + 1) * BLK], hid[:, t * P:(t + 1) * P],
                                                     c.ident[0:BLK, 0:BLK])
                        mm.then_inc(S["h_turned"], 1)
                        pe.wait_ge(S["h_lo"], N + 2)
                        pe.wait_ge(S["y_copied"], N + 1)
                        for j in (4, 5):
                            s = (UNITS * u + j) % RING
                            pe.wait_ge(S["w_lo"], split(N, j))
                            for b in range(2):
                                k = (j - 4) * 2 + b
                                for half in range(2):
                                    n = slice(b * D + half * BANK, b * D + (half + 1) * BANK)
                                    mm = three_passes(nc, py[:, half * BANK:(half + 1) * BANK], hh[:, k * BLK:(k + 1) * BLK],
                                                      hl[:, k * BLK:(k + 1) * BLK], wh[s][:, n], wl[s][:, n], k == 0, k == 3)
                            mm.then_inc(S["unit_used"], 1)
                rounds(pe, body)


def combine(c, nc, final_norm, out):
    U = 4
    with ExitStack() as ctx:
        ids = [[c.sb(ctx, f"e_ids{u}{j}", [P, 1], I32) for j in range(2)] for u in range(U)]
        y = [[c.sb(ctx, f"e_y{u}{j}", [P, D], F32) for j in range(2)] for u in range(U)]
        acc = [c.sb(ctx, f"e_acc{u}", [P, D], F32) for u in range(U)]
        res = [c.sb(ctx, f"e_res{u}", [P, D], F32) for u in range(U)]
        gain = c.sb(ctx, "e_gain", [P, D], F32)
        ss, ms, rs = (c.sb(ctx, "e_" + n, [P, U], F32) for n in ("ss", "ms", "rs"))
        S = {n: c.sem("e_" + n) for n in ("gain_in", "ids_ready", "summed", "rooted", "done", "own", "own_a", "passed")}
        y_in = [[c.lasting_sem(f"e_y_in{u}{j}") for j in range(2)] for u in range(U)]
        stored = [c.sem(f"e_stored{u}") for u in range(U)]
        flat = lambda ap: ap.rearrange("p (k t) -> p k t", k=KD)
        with nc.Block() as block:
            @block.gpsimd
            def _(pool):
                with pool.Fori(0, NT // U) as i:
                    for u in range(U):
                        pool.wait_ge(S["summed"], i * U + (u + 1))
                        for j in range(2):
                            nc.gpsimd.tensor_copy(ids[u][j][:], c.slot_of[:, bass.ds(i * U + (u + j * NT), 1)]
                                                  ).then_inc(S["ids_ready"], 1)
                            wait_apart(pool, S["ids_ready"], i * (2 * U) + (2 * u + j + 1), S["passed"])
                            nc.gpsimd.indirect_dma_start(out=y[u][j][:], out_offset=None, in_=c.yrows[:, :],
                                                         in_offset=bass.IndirectOffsetOnAxis(ap=ids[u][j][:, 0:1], axis=0)
                                                         ).then_inc(y_in[u][j], 16)

            @block.sync
            def _(sp):
                sp.dma_start(gain[:], final_norm[:].partition_broadcast(P)).then_inc(S["gain_in"], 16)
                with sp.Fori(0, NT // U) as i:
                    for u in range(U):
                        sp.wait_ge(S["done"], i * U + (U + u + 1))
                        sp.dma_start(out[0, bass.ds(i * (U * P) + u * P, P), :], res[u][:]).then_inc(stored[u], 16)
                for u in range(U):
                    sp.wait_ge(stored[u], 16 * (NT // U + 1))

            @block.scalar
            def _(act):
                nc.scalar.preload_act_table_set(LN_AND_EXP)
                chain = Chain(act, S["own_a"])
                with act.Fori(0, NT // U) as i:
                    chain.enter(i, 2 * U)
                    for u in range(U):
                        act.wait_ge(S["summed"], i * U + (U + u + 1))
                        act.wait_ge(stored[u], i * 16 + 16)
                        chain.link(nc.scalar.activation(res[u][:], acc[u][:], ACT.Square, accum_out=ss[:, u:u + 1]))
                        chain.link(nc.scalar.activation(ms[:, u:u + 1], ss[:, u:u + 1], ACT.Ln, scale=1.0 / D,
                                                        bias=c.eps[:, 0:1]))
                        nc.scalar.activation(rs[:, u:u + 1], ms[:, u:u + 1], ACT.Exp, scale=-0.5).then_inc(S["rooted"], 1)
                chain.leave(NT // U)

            @block.vector
            def _(dve):
                chain = Chain(dve, S["own"])
                dve.sem_inc(S["summed"], U)
                dve.sem_inc(S["done"], U)
                for u in range(U):
                    dve.sem_inc(stored[u], 16)
                dve.wait_ge(S["gain_in"], 16)

                def finish(i, u):
                    dve.wait_ge(S["rooted"], i * U + (u + 1))
                    nc.vector.scalar_tensor_tensor(out=res[u][:], in0=acc[u][:], scalar=rs[:, u:u + 1], in1=gain[:],
                                                   op0=ALU.mult, op1=ALU.mult).then_inc(S["done"], 1)
                with dve.Fori(0, NT // U) as i:
                    chain.enter(i, U)
                    for u in range(U):
                        h2 = c.mx[:, :, bass.ds(i * (U * P) + u * P, P)]
                        w = [c.weight[:, bass.ds(i * U + (u + j * NT), 1)] for j in range(2)]
                        for j in range(2):
                            dve.wait_ge(y_in[u][j], i * 16 + 16)
                        dve.wait_ge(S["done"], i * U + (u + 1))
                        chain.link(nc.vector.scalar_tensor_tensor(out=flat(acc[u][:]), in0=flat(y[u][0][:]), scalar=w[0],
                                                                  in1=h2, op0=ALU.mult, op1=ALU.add))
                        nc.vector.scalar_tensor_tensor(out=acc[u][:], in0=y[u][1][:], scalar=w[1], in1=acc[u][:],
                                                       op0=ALU.mult, op1=ALU.add).then_inc(S["summed"], 1)
                        if u >= 1:
                            finish(i, u - 1)
                    finish(i, U - 1)
                chain.leave(NT // U)


def program(nc, x, meta_tokens, attn_norm, w_in, b_forget, conv_w, mix_norm, w_out, ffn_norm, w_router_group,
            b_router_group, w_router_expert, b_router_expert, w_gate, w_up, w_down, final_norm, out):
    with ExitStack() as ctx:
        c = Core(nc, ctx)
        c.ident = c.sb(ctx, "ident", [P, P], F32)
        c.ident_bf = c.sb(ctx, "ident_bf", [P, P], BF16)
        c.maskneg = c.sb(ctx, "maskneg", [P, P], BF16)
        c.blkavg = c.sb(ctx, "blkavg", [P, P], F32)
        c.tri = c.sb(ctx, "tri", [P, P], BF16)
        c.ones_bf = c.sb(ctx, "ones_bf", [P, P], BF16)
        c.mixg = c.sb(ctx, "mixg", [P, KD], F32)
        c.eps = c.sb(ctx, "eps", [P, 1], F32)
        c.mx = c.sb(ctx, "mx", [P, KD, SEQ], F32)
        c.negcum = nc.dram_tensor("negcum", [HEADS, L], F32, kind="Internal").ap()
        c.logits = c.sb(ctx, "logits", [P, NT, NG + NE], F32)
        c.weight = c.sb(ctx, "weight", [P, 2 * NT], F32)
        c.slot_of = c.sb(ctx, "slot_of", [P, 2 * NT], I32)
        c.over_expert = c.sb(ctx, "over_expert", [1, OVB + 1], I32)
        c.row_tokens = c.sb(ctx, "row_tokens", [BLK, NBLK + 1], I32)
        c.z2rows = nc.dram_tensor("z2rows", [SEQ, D], F32, kind="Internal").ap()
        c.yrows = nc.dram_tensor("yrows", [NBLK * BLK, D], F32, kind="Internal").ap()
        with c.semaphores():
            constants(c, nc, mix_norm)
            with ExitStack() as zctx:
                c.zh = c.sb(zctx, "zh", [P, KD, LP], F32R)
                c.zl = c.sb(zctx, "zl", [P, KD, LP], F32R)
                norm_and_transpose(c, nc, x, meta_tokens, attn_norm)
                mixers(c, nc, w_in, b_forget, conv_w)
            output_projection(c, nc, x, w_out, ffn_norm, w_router_group, b_router_group, w_router_expert, b_router_expert)
            c.raw = [c.sb(ctx, f"raw{j}", [P, UNIT], F32) for j in range(UNITS)]
            c.raw_in = [c.lasting_sem(f"first_raw_in{j}") for j in range(UNITS)]
            route(c, nc, w_gate, w_up, w_down)
        with c.semaphores():
            experts(c, nc, "m", NE // 2, 0, w_gate, w_up, w_down)
            experts(c, nc, "x", None, NE, w_gate, w_up, w_down)
            combine(c, nc, final_norm, out)


_INS = ["x", "meta_tokens", "attn_norm", "w_in", "b_forget", "conv_w", "mix_norm", "w_out", "ffn_norm", "w_router_group",
        "b_router_group", "w_router_expert", "b_router_expert", "w_gate", "w_up", "w_down", "final_norm"]


def kernel(**inputs):
    import numpy as _np
    import concourse.bacc as _bacc
    from concourse import mybir as _mybir
    from concourse.bass_utils import run_bass_kernel_spmd as _run

    nc = _bacc.Bacc("TRN2", target_bir_lowering=False, num_devices=1)
    arrays, args = {}, []
    for name in _INS:
        a = _np.ascontiguousarray(inputs[name])
        arrays[f"in_{name}_dram"] = a
        args.append(nc.dram_tensor(f"in_{name}_dram", a.shape, _mybir.dt.from_np(a.dtype), kind="ExternalInput").ap())
    out = nc.dram_tensor("out_0_dram", (1, SEQ, D), F32, kind="ExternalOutput").ap()
    program(nc, *args, out)
    r = _run(nc, [arrays], core_ids=[0])
    return r.results[0]["out_0_dram"]
```
